# Optimizing a Trainium2 kernel written in Bass

```python
import jax, jax.numpy as jnp
from jax import lax
import numpy as np

D_MODEL = 1024
BATCH = 1
SEQ = 1024
DEPTH = 1
DEC_BATCH = 1
DEC_SEQ = 32
PAST_LEN = 256

CHUNK = 64
N_HEADS_A = 16
N_KV_A = 2
HEAD_DIM_A = 64
GROUP_A = N_HEADS_A // N_KV_A
WINDOW = 128
WINDOW_CHUNKS = WINDOW // CHUNK
KV_WIN = min(WINDOW, PAST_LEN)
N_HEADS_B = 4
DQK_B = 128
DV_B = 256
D_FF = 2816
CONV_W = 3
LN_EPS = 1e-5
ALPHA = (2 * DEPTH) ** 0.25
BETA = (8 * DEPTH) ** -0.25
Q_A = N_HEADS_A * HEAD_DIM_A
KV_A_W = N_KV_A * HEAD_DIM_A
QK_B = N_HEADS_B * DQK_B
V_B = N_HEADS_B * DV_B
Z_PARTS = (Q_A, KV_A_W, KV_A_W, QK_B, QK_B, V_B, N_HEADS_B, N_HEADS_B, V_B, D_MODEL, D_MODEL)
Z_WIDTH = int(sum(Z_PARTS))
Z_OFFSETS = tuple(int(v) for v in np.cumsum(Z_PARTS)[:-1])

kernel_name = 'streaming_swa_mlstm_convffn_hybrid_step'

def layer_norm(x, w, b):
    xf = x.astype(jnp.float32)
    mu = jnp.mean(xf, -1, keepdims=True)
    var = jnp.mean(jnp.square(xf - mu), -1, keepdims=True)
    y = (xf - mu) * lax.rsqrt(var + LN_EPS)
    return (y * w.astype(jnp.float32) + b.astype(jnp.float32)).astype(x.dtype)

def head_norm(h, w):
    N, T = h.shape[:2]
    hf = h.astype(jnp.float32)
    mu = jnp.mean(hf, -1, keepdims=True)
    var = jnp.mean(jnp.square(hf - mu), -1, keepdims=True)
    y = ((hf - mu) * lax.rsqrt(var + LN_EPS)).reshape(N, T, V_B)
    return (y * w.astype(jnp.float32)).astype(h.dtype)

def alibi_slopes():
    return 2.0 ** (-8.0 * jnp.arange(1, N_HEADS_A + 1, dtype=jnp.float32) / N_HEADS_A)

def banded_attention(qb, kb, vb, qpos, kpos, sinks):
    s = jnp.einsum('nbqhgd,nbshd->nbhgqs', qb.astype(jnp.float32), kb.astype(jnp.float32)) * (HEAD_DIM_A ** -0.5)
    qc = qpos // CHUNK
    kc = kpos // CHUNK
    visible = ((kpos[:, None, :] >= 0) & (kc[:, None, :] <= qc[:, :, None])
               & (kc[:, None, :] >= qc[:, :, None] - WINDOW_CHUNKS))
    dist = jnp.abs(qpos[:, :, None] - kpos[:, None, :]).astype(jnp.float32)
    slopes = alibi_slopes().reshape(N_KV_A, GROUP_A)
    s = s - slopes[None, None, :, :, None, None] * dist[None, :, None, None]
    s = jnp.where(visible[None, :, None, None], s, -jnp.inf)
    sink = sinks.astype(jnp.float32).reshape(1, 1, N_KV_A, GROUP_A, 1, 1)
    mx = jnp.maximum(jnp.max(s, -1, keepdims=True), sink)
    p = jnp.exp(s - mx)
    p = p / (jnp.sum(p, -1, keepdims=True) + jnp.exp(sink - mx))
    o = jnp.einsum('nbhgqs,nbshd->nbqhgd', p, vb.astype(jnp.float32))
    return o.astype(qb.dtype)

def local_attention(q, k, v, k_cache, v_cache, sinks):
    N, T = q.shape[:2]
    if k_cache is None:
        nb = T // CHUNK
        pad = WINDOW_CHUNKS * CHUNK
        span = (WINDOW_CHUNKS + 1) * CHUNK
        qb = q.reshape(N, nb, CHUNK, N_KV_A, GROUP_A, HEAD_DIM_A)

        def bands(a):
            ap = jnp.pad(a, ((0, 0), (pad, 0), (0, 0), (0, 0)))
            ap = ap.reshape(N, nb + WINDOW_CHUNKS, CHUNK, N_KV_A, HEAD_DIM_A)
            return jnp.concatenate([ap[:, j:j + nb] for j in range(WINDOW_CHUNKS + 1)], axis=2)

        kb, vb = bands(k), bands(v)
        qpos = jnp.arange(T).reshape(nb, CHUNK)
        kpos = jnp.arange(nb)[:, None] * CHUNK - pad + jnp.arange(span)[None, :]
        k_win, v_win = k[:, T - KV_WIN:], v[:, T - KV_WIN:]
    else:
        kk = jnp.concatenate([k_cache.astype(k.dtype), k], axis=1)
        vv = jnp.concatenate([v_cache.astype(v.dtype), v], axis=1)
        qb = q.reshape(N, 1, T, N_KV_A, GROUP_A, HEAD_DIM_A)
        kb, vb = kk[:, None], vv[:, None]
        qpos = (PAST_LEN + jnp.arange(T))[None]
        kpos = (PAST_LEN - KV_WIN + jnp.arange(KV_WIN + T))[None]
        k_win, v_win = kk[:, T:], vv[:, T:]
    o = banded_attention(qb, kb, vb, qpos, kpos, sinks)
    return o.reshape(N, T, Q_A), k_win, v_win

def mlstm_chunkwise(q, k, v, i_pre, logf, C0, n0, m0, chunk):
    N, T = q.shape[:2]
    nc = T // chunk

    def to_chunks(a):
        a = a.astype(jnp.float32).reshape((N, nc, chunk) + a.shape[2:])
        return jnp.swapaxes(jnp.moveaxis(a, 1, 0), 2, 3)

    xs = (to_chunks(q), to_chunks(k), to_chunks(v), to_chunks(i_pre), to_chunks(logf))
    causal = jnp.tril(jnp.ones((chunk, chunk), dtype=bool))

    def step(carry, inp):
        C, n, m = carry
        qc, kc, vc, ic, fc = inp
        b = jnp.cumsum(fc, axis=-1)
        dmat = jnp.where(causal, b[..., :, None] - b[..., None, :] + ic[..., None, :], -jnp.inf)
        inter = b + m[..., None]
        m_t = jnp.maximum(jnp.max(dmat, -1), inter)
        w = jnp.exp(dmat - m_t[..., None])
        g = jnp.exp(inter - m_t)
        s = jnp.einsum('nhld,nhsd->nhls', qc, kc) * w
        num = jnp.einsum('nhls,nhsv->nhlv', s, vc) + g[..., None] * jnp.einsum('nhvd,nhld->nhlv', C, qc)
        den = jnp.sum(s, -1) + g * jnp.einsum('nhd,nhld->nhl', n, qc)
        h = num / jnp.maximum(jnp.abs(den), jnp.exp(-m_t))[..., None]
        m_new = m_t[..., -1]
        wk = jnp.exp(b[..., -1:] - b + ic - m_new[..., None])
        decay = jnp.exp(b[..., -1] + m - m_new)
        C_new = decay[..., None, None] * C + jnp.einsum('nhl,nhlv,nhld->nhvd', wk, vc, kc)
        n_new = decay[..., None] * n + jnp.einsum('nhl,nhld->nhd', wk, kc)
        return (C_new, n_new, m_new), h

    init = (C0.astype(jnp.float32), n0.astype(jnp.float32), m0.astype(jnp.float32))
    (C, n, m), h = lax.scan(step, init, xs)
    h = jnp.moveaxis(jnp.swapaxes(h, 2, 3), 0, 1).reshape(N, T, N_HEADS_B, DV_B)
    return h.astype(q.dtype), C, n, m

def conv_ffn(h, conv_buf, w_up, b_up, conv_w, conv_b, w_down):
    T = h.shape[1]
    u = h @ w_up + b_up
    ctx = jnp.concatenate([conv_buf.astype(u.dtype), u], axis=1)
    uc = conv_b + sum(conv_w[j] * ctx[:, j:j + T] for j in range(CONV_W))
    a, g = jnp.split(uc, 2, axis=-1)
    return (a * jax.nn.gelu(g)) @ w_down, ctx[:, T:]

def trunk_layer(x, c, k_cache, v_cache, C0, n0, m0, conv_buf, mlstm_chunk, prm):
    N, T, _ = x.shape
    mod = jax.nn.silu(c) @ prm['w_ada'] + prm['b_ada']
    sh1, sc1, g1, sh2, sc2, g2 = jnp.split(mod[:, None, :], 6, axis=-1)
    h = x * (1 + sc1) + sh1
    z = h @ prm['w_in']
    qa, ka, va, qm, km, vm, ig, fg, og, ga, gb = jnp.split(z, Z_OFFSETS, axis=-1)
    ya, k_win, v_win = local_attention(qa.reshape(N, T, N_HEADS_A, HEAD_DIM_A),
                                       ka.reshape(N, T, N_KV_A, HEAD_DIM_A),
                                       va.reshape(N, T, N_KV_A, HEAD_DIM_A),
                                       k_cache, v_cache, prm['attn_sinks'])
    i_pre = (ig + prm['b_igate']).astype(jnp.float32)
    logf = jax.nn.log_sigmoid((fg + prm['b_fgate']).astype(jnp.float32))
    hm, C, n, m = mlstm_chunkwise(qm.reshape(N, T, N_HEADS_B, DQK_B),
                                  km.reshape(N, T, N_HEADS_B, DQK_B) * (DQK_B ** -0.5),
                                  vm.reshape(N, T, N_HEADS_B, DV_B),
                                  i_pre, logf, C0, n0, m0, mlstm_chunk)
    yb = jax.nn.sigmoid(og) * head_norm(hm, prm['mlstm_norm_w'])
    merged = jax.nn.sigmoid(ga) * (ya @ prm['w_proj_a']) + jax.nn.sigmoid(gb) * (yb @ prm['w_proj_b'])
    x = layer_norm(ALPHA * x + g1 * (merged @ prm['w_out']), prm['ln1_w'], prm['ln1_b'])
    h = x * (1 + sc2) + sh2
    f, conv_new = conv_ffn(h, conv_buf, prm['w_up'], prm['b_up'], prm['conv_w'], prm['conv_b'], prm['w_down'])
    x = layer_norm(ALPHA * x + g2 * f, prm['ln2_w'], prm['ln2_b'])
    dt = x.dtype
    return x, k_win, v_win, C.astype(dt), n.astype(dt), m.astype(dt), conv_new

def setup_inputs(seed: int = 0) -> dict:
    key = jax.random.key(seed)
    ks = jax.random.split(key, 32)
    L, D = DEPTH, D_MODEL

    def nrm(k, shape, s):
        return jax.random.normal(k, shape, jnp.float32) * s

    return {
        'x_prompt': nrm(ks[0], (BATCH, SEQ, D), 1.0),
        'x_sample': nrm(ks[1], (DEC_BATCH, DEC_SEQ, D), 1.0),
        'cache_attn_k': nrm(ks[2], (L, DEC_BATCH, KV_WIN, N_KV_A, HEAD_DIM_A), 1.0),
        'cache_attn_v': nrm(ks[3], (L, DEC_BATCH, KV_WIN, N_KV_A, HEAD_DIM_A), 1.0),
        'state_mlstm_C': nrm(ks[4], (L, DEC_BATCH, N_HEADS_B, DV_B, DQK_B), 0.1),
        'state_mlstm_n': nrm(ks[5], (L, DEC_BATCH, N_HEADS_B, DQK_B), 0.1),
        'state_mlstm_m': nrm(ks[6], (L, DEC_BATCH, N_HEADS_B), 0.5),
        'state_ffn_conv': nrm(ks[7], (L, DEC_BATCH, CONV_W - 1, 2 * D_FF), 1.0),
        'c_prompt': nrm(ks[8], (BATCH, D), 1.0),
        'c_sample': nrm(ks[9], (DEC_BATCH, D), 1.0),
        'w_ada': nrm(ks[10], (L, D, 6 * D), 0.5 * D ** -0.5),
        'b_ada': nrm(ks[11], (L, 6 * D), 0.01),
        'w_in': nrm(ks[12], (L, D, Z_WIDTH), D ** -0.5),
        'b_igate': nrm(ks[13], (L, N_HEADS_B), 0.1),
        'b_fgate': jnp.linspace(3.0, 6.0, N_HEADS_B, dtype=jnp.float32)[None] + nrm(ks[14], (L, N_HEADS_B), 0.1),
        'attn_sinks': nrm(ks[15], (L, N_HEADS_A), 0.5),
        'mlstm_norm_w': 1.0 + nrm(ks[16], (L, V_B), 0.02),
        'w_proj_a': nrm(ks[17], (L, Q_A, D), Q_A ** -0.5),
        'w_proj_b': nrm(ks[18], (L, V_B, D), V_B ** -0.5),
        'w_out': nrm(ks[19], (L, D, D), BETA * D ** -0.5),
        'ln1_w': 1.0 + nrm(ks[20], (L, D), 0.02),
        'ln1_b': nrm(ks[21], (L, D), 0.02),
        'w_up': nrm(ks[22], (L, D, 2 * D_FF), D ** -0.5),
        'b_up': nrm(ks[23], (L, 2 * D_FF), 0.01),
        'conv_w': nrm(ks[24], (L, CONV_W, 2 * D_FF), CONV_W ** -0.5),
        'conv_b': nrm(ks[25], (L, 2 * D_FF), 0.01),
        'w_down': nrm(ks[26], (L, D_FF, D), BETA * D_FF ** -0.5),
        'ln2_w': 1.0 + nrm(ks[27], (L, D), 0.02),
        'ln2_b': nrm(ks[28], (L, D), 0.02),
    }

def reference(x_prompt, x_sample, cache_attn_k, cache_attn_v, state_mlstm_C, state_mlstm_n, state_mlstm_m,
              state_ffn_conv, c_prompt, c_sample, w_ada, b_ada, w_in, b_igate, b_fgate, attn_sinks, mlstm_norm_w,
              w_proj_a, w_proj_b, w_out, ln1_w, ln1_b, w_up, b_up, conv_w, conv_b, w_down, ln2_w, ln2_b):
    Bp = x_prompt.shape[0]
    dec_t = x_sample.shape[1]
    y_prompt, y_sample = x_prompt, x_sample
    p_out, s_out = [], []
    for l in range(DEPTH):
        prm = dict(w_ada=w_ada[l], b_ada=b_ada[l], w_in=w_in[l], b_igate=b_igate[l], b_fgate=b_fgate[l],
                   attn_sinks=attn_sinks[l], mlstm_norm_w=mlstm_norm_w[l], w_proj_a=w_proj_a[l],
                   w_proj_b=w_proj_b[l], w_out=w_out[l], ln1_w=ln1_w[l], ln1_b=ln1_b[l], w_up=w_up[l],
                   b_up=b_up[l], conv_w=conv_w[l], conv_b=conv_b[l], w_down=w_down[l], ln2_w=ln2_w[l],
                   ln2_b=ln2_b[l])
        C0 = jnp.zeros((Bp, N_HEADS_B, DV_B, DQK_B), jnp.float32)
        n0 = jnp.zeros((Bp, N_HEADS_B, DQK_B), jnp.float32)
        m0 = jnp.zeros((Bp, N_HEADS_B), jnp.float32)
        conv0 = jnp.zeros((Bp, CONV_W - 1, 2 * D_FF), x_prompt.dtype)
        res_p = trunk_layer(y_prompt, c_prompt, None, None, C0, n0, m0, conv0, CHUNK, prm)
        y_prompt = res_p[0]
        p_out.append(res_p[1:])
        res_s = trunk_layer(y_sample, c_sample, cache_attn_k[l], cache_attn_v[l], state_mlstm_C[l],
                            state_mlstm_n[l], state_mlstm_m[l], state_ffn_conv[l], dec_t, prm)
        y_sample = res_s[0]
        s_out.append(res_s[1:])
    p_k, p_v, p_C, p_n, p_m, p_conv = [jnp.stack([o[i] for o in p_out]) for i in range(6)]
    s_k, s_v, s_C, s_n, s_m, s_conv = [jnp.stack([o[i] for o in s_out]) for i in range(6)]
    return (y_prompt, y_sample, p_k, p_v, p_C, p_n, p_m, p_conv, s_k, s_v, s_C, s_n, s_m, s_conv)


_drawn_inputs = setup_inputs


def setup_inputs(seed=0):
    import zlib

    import numpy as np

    out = dict(_drawn_inputs(seed))
    spreads = {}
    factors = {'state_mlstm_m': 3.926,
     'attn_sinks': 200.0,
     'mlstm_norm_w': 64.0,
     'ln1_w': 8.153,
     'ln1_b': 7.634,
     'b_up': 47.555,
     'conv_b': 39.173,
     'ln2_w': 28.97,
     'ln2_b': 26.248,
     'state_ffn_conv': 3.152,
     'w_proj_a': 6.088}
    for name, (base, spread) in spreads.items():
        noise = np.random.default_rng([zlib.crc32(name.encode()), seed]).standard_normal(out[name].shape)
        drawn = base * np.exp(spread * noise) if base else spread * noise
        out[name] = __import__('jax').numpy.asarray(drawn.astype(out[name].dtype))
    for name, factor in factors.items():
        out[name] = (out[name] * factor).astype(out[name].dtype)
    return out
```

```python
from contextlib import ExitStack

import numpy as np
import concourse.bass as bass
from concourse import mybir

F32 = mybir.dt.float32
F32R = mybir.dt.float32r
ALU = mybir.AluOpType
ACT = mybir.ActivationFunctionType
AX = mybir.AxisListType

P = 128
D = 1024
KT = D // P
TP, TS = 1024, 32
T = TP + TS
NT = 3
NW = T // NT
CH = 64
NCH = TP // CH
BAND = 3 * CH
WIN = 128
HB, DV = 4, 256
LC = 128
NLC = TP // LC
UT = 5632 // P
FG = UT // 4
UW = T + 4
CW = UW - 2
ALPHA = 2.0 ** 0.25
EPS = 1e-5
KB_SCALE = 128.0 ** -0.5

P_ATT = 11
P_ML = P_ATT + NCH + 1
N_MLG = 6
P_PA = P_ML + 4 * N_MLG
P_PB = P_PA + KT
P_OUT = P_PB + KT
P_FFN = P_OUT + KT
N_PANEL = P_FFN + 6 * FG
M_LN1 = P_FFN
M_FFN = M_LN1 + 2
M_LN2 = M_FFN + 12 * FG
N_SPILL = P_PA - P_ATT
Q_O, Q_GB, Q_GA = 17, 25, 33

C_BADA, C_L1W, C_L1B, C_L2W, C_L2B, C_NW, C_C, C_SINK, C_BI, C_BF, C_M0 = 0, 48, 56, 64, 72, 80, 88, 104, 112, 113, 114
N_SMALL = 116


def wait(eng, sem, v):
    if isinstance(v, int) and v <= 0:
        return
    eng.wait_ge(sem, v)


def build(nc, io):
    ctx = ExitStack()
    with ctx:
        W0 = 16512
        RAW_B, WHL_B = 2 * 4096, 4 * 4096
        A_B = 2 * KT * T * 4
        C_B = KT * T * 4
        o_raw = W0
        o_whl = o_raw + RAW_B
        o_A = o_whl + WHL_B
        o_B = o_A + A_B
        o_C = o_B + A_B
        o_S = o_C + C_B
        o_M = o_S + 4 * UW * 4
        place = {"end": 0}

        def at(name, shape, off, dt=F32):
            n = int(np.prod(shape[1:])) * 4
            place["end"] = off + n
            return nc.alloc_sbuf_tensor_at(name, shape, dt, offset=off)

        def after(name, shape, dt=F32):
            return at(name, shape, (place["end"] + 31) // 32 * 32, dt)

        raw = at("w_raw", [P, 2, D], o_raw)
        whl = at("w_hilo", [P, 2, 2, D], o_whl, F32R)
        XA = at("x_hilo_a", [P, 2, KT, T], o_A, F32R)
        XB = at("x_hilo_b", [P, 2, KT, T], o_B, F32R)
        XC = at("x_c", [P, KT, T], o_C)
        ST = at("stage", [P, 4, UW], o_S)
        small = at("small", [P, N_SMALL], o_M)
        ident = after("ident", [P, P])
        ones = after("ones", [P, P])
        mod = after("mod", [P, 6, KT, 2])
        der = after("der", [P, 6, KT])
        assert place["end"] <= 229344
        ada = at("ada_ring", [P, KT, D], o_B)
        silu = after("silu", [P, 3, KT, 2])
        kk = at("k_dup", [P, 2, TP + WIN + TS], o_B)
        vv = after("v_feat", [P, TP + WIN + TS])
        alibi = after("alibi", [P, 8, BAND])
        qs = after("q_stage", [P, 2, KT, CH])
        ks = after("k_stage", [P, 2, 2, BAND])
        vs = after("v_stage", [P, 2, BAND])
        vt = after("v_tok", [P, 2, 2, P])
        pb = after("probs", [P, 2, 4, BAND])
        pta = after("probs_ta", [P, 4, P])
        ptb = after("probs_tb", [P, 4, P])
        nmx = after("neg_max", [P, 2, 4])
        esk = after("exp_sink", [P, 2, 4])
        rsum = after("row_sum", [P, 2, 4])
        rden = after("row_den", [P, 4])
        assert place["end"] <= o_C
        zc = at("zc", [P, 2, 16, LC], o_B)
        cst = after("c_state", [P, 2, HB, DV + 1])
        rowC = after("rowC", [HB, T])
        rowD = after("rowD", [HB, T])
        rowE = after("rowE", [HB, T])
        rowM = after("rowM", [HB, T])
        rowR = after("rowR", [HB, T])
        sel = after("sel", [HB, HB, P])
        cmask = after("cmask", [P, P])
        mprow = after("mprow", [HB, NLC + 1])
        at_c = after("a_cols", [P, NLC + 1, HB])
        em_c = after("em_cols", [P, NLC + 1, HB])
        mp_c = after("mp_cols", [P, HB, NLC + 1])
        rs = after("r_bc", [P, LC])
        wd = after("w_dec", [P, LC])
        gb = after("g_bc", [P, LC])
        wks = after("wk_col", [P, 1])
        pt = after("p_t", [P, LC])
        qg = after("q_g", [P, LC])
        kw = after("k_w", [P, LC])
        va = after("v_aug", [P, DV + 1])
        hh = after("h_tok", [P, HB, DV])
        hn = at("hn_tok", [P, HB, DV], place["end"])
        dn = after("den", [P, 2])
        bst = after("bn_st", [P, HB, 6])
        mv = after("mean_var", [P, HB, 2])
        rstd = after("rstd", [P, HB])
        hT = after("hn_feat", [P, KT, LC]) if place["end"] + 4096 <= o_C else None
        assert hT is not None and place["end"] <= o_C, (place["end"], o_C)
        rowI = ST[0:HB, 2, 0:T]
        rowF = ST[0:HB, 3, 0:T]
        fa = at("ffn_act", [P, 2, 2, 2, T], o_B, F32R)
        ub = after("u_rows", [P, 4, UW])
        fc = after("ffn_consts", [P, FG, 4, 8])
        cs = after("conv_out", [P, FG, 4, 4])
        fca = after("consts_act", [P, 4, 8])
        fcd = after("consts_dve", [P, 4, 8])
        assert place["end"] <= o_C

        acc = ctx.enter_context(nc.psum_tensor("acc", [P, NT, 512], F32))
        px = ctx.enter_context(nc.psum_tensor("px", [P, 5, 512], F32))

        def sem(name):
            return ctx.enter_context(nc.semaphore(name))

        raw_in = [sem("raw_in0"), sem("raw_in1")]
        raw_used, split_begun, w_hi, w_ready, w_start = sem("raw_used"), sem("split_begun"), sem("w_hi"), sem("w_ready"), sem("w_start")
        acc_ready = [sem(f"acc_ready{n}") for n in range(NT)]
        acc_free = [sem(f"acc_free{n}") for n in range(NT)]
        c_in, x_in = sem("c_in"), [sem(f"x_in{i}") for i in range(2)]
        ada_in = [sem(f"ada_in{i}") for i in range(KT)]
        ada_used, ada_ev = sem("ada_used"), sem("ada_ev")
        sl_e, sl_d = sem("sl_e"), sem("sl_d")
        h_tmp, h_hi, h_lo = sem("h_tmp"), sem("h_hi"), sem("h_lo")
        qkv_ev, kv_in, kv_out = sem("qkv_ev"), sem("kv_in"), sem("kv_out")
        st_rdy, s_rdy, s_used, mx_rdy, ex_rdy, pn_rdy = (sem(n) for n in ("st_rdy", "s_rdy", "s_used", "mx_rdy", "ex_rdy", "pn_rdy"))
        tr_rdy, pt_rdy, pv_rdy, o_used, v_tok = (sem(n) for n in ("tr_rdy", "pt_rdy", "pv_rdy", "o_used", "v_tok_rdy"))
        sp_cp = sem("sp_cp")
        sp_out = [sem("sp_out0"), sem("sp_out1")]
        ml_in, g_in, row_d, row_a, row_p, row_v = (sem(n) for n in ("ml_in", "g_in", "row_d", "row_a", "row_p", "row_v"))
        zc_in = [sem("zc_in0"), sem("zc_in1")]
        sr_rdy, kvt_rdy, d_rdy, wg_rdy, kv_rdy, p_rdy, nu_rdy, e_done, var_rdy, sd_rdy, hn_rdy, ht_rdy, ht_cp = (
            sem(n) for n in ("sr_rdy", "kvt_rdy", "d_rdy", "wg_rdy", "kv_rdy", "p_rdy", "nu_rdy", "e_done", "var_rdy", "sd_rdy",
                             "hn_rdy", "ht_rdy", "ht_cp"))
        hs_out, st_out = sem("hs_out"), sem("st_out")
        ya_hi, ya_lo = sem("ya_hi"), sem("ya_lo")
        og_in, hn_in, sg_rdy, yb_rdy, yb_hi, yb_lo = (sem(n) for n in ("og_in", "hn_in", "sg_rdy", "yb_rdy", "yb_hi", "yb_lo"))
        gt_in = [sem("gt_in0"), sem("gt_in1")]
        gt_rdy, gt_used, mg_rdy, mg_hi, mg_lo = (sem(n) for n in ("gt_rdy", "gt_used", "mg_rdy", "mg_hi", "mg_lo"))
        xr_in = [sem("xr_in0"), sem("xr_in1")]
        r_rdy, ln_d, ln_sq, ln_squ, ln_v, ln_s, ln_t = (sem(n) for n in ("r_rdy", "ln_d", "ln_sq", "ln_squ", "ln_v", "ln_s", "ln_t"))
        h2_t, h2_hi, h2_lo, fc_in = (sem(n) for n in ("h2_t", "h2_hi", "h2_lo", "fc_in"))
        u_rdy, cv_a, cv_d, gl_rdy, pr_rdy, fa_hi, fa_lo = (sem(n) for n in ("u_rdy", "cv_a", "cv_d", "gl_rdy", "pr_rdy", "fa_hi", "fa_lo"))
        y_rdy, y_out, cs_out = sem("y_rdy"), sem("y_out"), sem("cs_out")
        block = ctx.enter_context(nc.Block())

        XCt = XC[:, :, :].rearrange("p k (n w) -> p k n w", n=NT)
        acc_w = acc[:, :, 0:NW]

        def stage3(i):
            return ST[:, i, 0:T].rearrange("p (n w) -> p n w", n=NT)

        def pieces(n):
            a, b = n * NW, (n + 1) * NW
            return [(a, b, 0)] if b <= TP else [(a, TP, 0), (TP, b, 1)]

        def spill_round(q0):
            return q0 % 2, q0 // 2

        @block.sync
        def _(sp):
            def ada_group(i):
                for m in range(KT):
                    wait(sp, ada_used, (i - 1) * KT + m + 1)
                    src = io["w_ada"][bass.ds(i * KT + m, 1), :, :]
                    sp.dma_start(ada[:, m, :], src.rearrange("o p n -> p (o n)")).then_inc(ada_in[m], 16)

            ada_group(0)
            with sp.Fori(1, 6) as i:
                ada_group(i)

            def panel_pair(i):
                for s in range(2):
                    wait(sp, raw_used, 2 * i + s - 1)
                    sp.dma_start(raw[:, s, :], io["w_panels"][bass.ds(i * 2 + s, 1), :, :].rearrange("o p n -> p (o n)"))\
                      .then_inc(raw_in[s], 16)

            panel_pair(0)
            with sp.Fori(1, N_PANEL // 2) as i:
                panel_pair(i)

        @block.gpsimd
        def _(pool):
            def split_pair(i):
                for s in range(2):
                    pool.wait_ge(raw_in[s], (i + 1) * 16)
                    if not isinstance(i, int):
                        pool.wait_ge(w_start, i * 2 + s)
                    pool.sem_inc(split_begun, 1)
                    nc.gpsimd.tensor_copy(whl[:, s, 0, :], raw[:, s, :]).then_inc(w_hi, 1)
                    pool.wait_ge(w_hi, i * 2 + s + 1)
                    nc.gpsimd.tensor_tensor(whl[:, s, 1, :], raw[:, s, :], whl[:, s, 0, :].bitcast(F32), ALU.subtract)\
                      .then_inc(w_ready, 1)
                    pool.wait_ge(w_ready, i * 2 + s + 1)
                    pool.sem_inc(raw_used, 1)

            split_pair(0)
            with pool.Fori(1, N_PANEL // 2) as i:
                split_pair(i)

        @block.tensor
        def _(pe):
            mm = nc.tensor.matmul

            def gemm(p, slot, n, rhs, last_of_panel=None):
                if n == 0:
                    pe.wait_ge(w_ready, p + 1)
                wait(pe, acc_free[n], p)
                for k in range(KT):
                    for j, (wi, xi) in enumerate(((0, 0), (0, 1), (1, 0))):
                        last = mm(acc[:, n, 0:NW], whl[:, slot, wi, k * P:(k + 1) * P], rhs[:, xi, k, n * NW:(n + 1) * NW],
                                  start=(k == 0 and j == 0), stop=(k == KT - 1 and j == 2))
                        if n == 0 and k == 0 and j == 0:
                            last.then_inc(w_start, 1)
                last.then_inc(acc_ready[n], 1)

            pe.wait_ge(sl_d, 2)

            def ada_mm_group(i):
                if not isinstance(i, int) or i > 0:
                    pe.wait_ge(ada_ev, i)
                for m in range(KT):
                    pe.wait_ge(ada_in[m], (i + 1) * 16)
                    for k in range(KT):
                        last = mm(px[:, 0, 2 * m:2 * m + 2], ada[:, m, k * P:(k + 1) * P], silu[:, 2, k, :],
                                  start=(k == 0), stop=(k == KT - 1))
                    last.then_inc(ada_used, 1)

            ada_mm_group(0)
            with pe.Fori(1, 6) as i:
                ada_mm_group(i)

            pe.wait_ge(h_lo, KT)
            for p in range(2):
                for n in range(NT):
                    gemm(p, p, n, XA)
            with pe.Fori(1, KT // 2) as i:
                for s in range(2):
                    for n in range(NT):
                        gemm(i * 2 + s, s, n, XA)
            for p in range(KT, P_ATT):
                for n in range(NT):
                    gemm(p, p % 2, n, XA)

            def att_scores(c, a, par, g, w, kb):
                if g == 0:
                    pe.wait_ge(st_rdy, c + 1)
                if g == 0:
                    wait(pe, s_used, a)
                if g == 0:
                    if w > kb:
                        nc.tensor.transpose(px[0:w - kb, 0, 384:512], vs[:, par, 0:w - kb], ident[:, :])
                    nc.tensor.transpose(px[0:kb, 1, 384:512], vs[:, par, w - kb:w], ident[:, :])
                for j in range(4):
                    for e in range(2):
                        last = mm(px[64 * e:64 * e + 64, j // 2, (j % 2) * BAND:(j % 2) * BAND + w],
                                  qs[64 * e:64 * e + 64, par, 4 * g + j, :], ks[64 * e:64 * e + 64, par, g, 0:w],
                                  start=True, stop=True, skip_group_check=True)
                last.then_inc(s_rdy, 1)

            def att_transpose(a, g, w, kb):
                pe.wait_ge(pn_rdy, a + 1)
                wait(pe, pt_rdy, a)
                for j in range(4):
                    if w > kb:
                        nc.tensor.transpose(px[0:w - kb, 2, j * P:(j + 1) * P], pb[:, g, j, 0:w - kb], ident[:, :])
                    last = nc.tensor.transpose(px[0:kb, 3, j * P:(j + 1) * P], pb[:, g, j, w - kb:w], ident[:, :])
                last.then_inc(tr_rdy, 1)

            def att_values(a, par, g, w, kb):
                pe.wait_ge(pt_rdy, a + 1)
                wait(pe, o_used, a)
                for e in range(2):
                    out = px[64 * e:64 * e + 64, 4, 0:4 * CH]
                    if w > kb:
                        mm(out, vt[0:w - kb, par, 0, g * 64:g * 64 + 64], pta[0:w - kb, :, 64 * e:64 * e + 64],
                           start=True, stop=False)
                    last = mm(out, vt[0:kb, par, 1, g * 64:g * 64 + 64], ptb[0:kb, :, 64 * e:64 * e + 64],
                              start=(w == kb), stop=True)
                last.then_inc(pv_rdy, 1)

            def att_chunk(c, par, w, kb, wp, kbp):
                slot = (P_ATT + par) % 2
                first = isinstance(c, int) and c == 0
                att_scores(c, c * 2, par, 0, w, kb)
                gemm(c + P_ATT, slot, 0, XA)
                pe.wait_ge(s_used, c * 2 + 1)
                if not first:
                    att_transpose(c * 2 - 1, 1, wp, kbp)
                att_scores(c, c * 2 + 1, par, 1, w, kb)
                gemm(c + P_ATT, slot, 1, XA)
                if not first:
                    att_values(c * 2 - 1, 1 - par, 1, wp, kbp)
                att_transpose(c * 2, 0, w, kb)
                gemm(c + P_ATT, slot, 2, XA)
                att_values(c * 2, par, 0, w, kb)

            att_chunk(0, 0, CH, CH, 0, 0)
            att_chunk(1, 1, 2 * CH, CH, CH, CH)
            att_chunk(2, 0, BAND, CH, 2 * CH, CH)
            att_chunk(3, 1, BAND, CH, BAND, CH)
            with pe.Fori(2, NCH // 2) as i:
                att_chunk(i * 2, 0, BAND, CH, BAND, CH)
                att_chunk(i * 2 + 1, 1, BAND, CH, BAND, CH)
            att_chunk(NCH, 0, WIN + TS, TS, BAND, CH)
            att_transpose(2 * NCH + 1, 1, WIN + TS, TS)
            att_values(2 * NCH + 1, 0, 1, WIN + TS, TS)

            pe.wait_ge(row_d, 2)
            pe.wait_ge(ml_in, 16 * 3)
            for c in range(NLC + 1):
                L = LC if c < NLC else TS
                nc.tensor.transpose(px[0:L, 0, 4 * c:4 * c + 4], rowC[:, c * LC:c * LC + L], ident[0:HB, 0:HB])
                nc.tensor.transpose(px[0:L, 0, 64 + 4 * c:68 + 4 * c], rowM[:, c * LC:c * LC + L], ident[0:HB, 0:HB])
            for h in range(HB):
                last = mm(px[:, 0, 128 + 9 * h:137 + 9 * h], sel[:, h, :], mprow[:, :], start=True, stop=True)
            last.then_inc(row_p, 1)

            def ml_unit(c, r, par, h, L, panel):
                u = c * 4 + h
                z = zc[:, par, :, :]
                if h == 0:
                    pe.wait_ge(zc_in[par], (r + 1) * 16)
                if isinstance(c, int) and c == 0 and h == 0:
                    pe.wait_ge(row_v, 2)
                wait(pe, p_rdy, u)
                mm(px[0:L, 0, 0:L], z[:, h, 0:L], z[:, 4 + h, 0:L], start=True, stop=True)
                tok = slice(c * LC, c * LC + L) if isinstance(c, int) else bass.ds(c * LC, L)
                mm(px[:, 0, P:P + L], sel[:, h, :], rowR[:, tok], start=True, stop=True).then_inc(sr_rdy, 1)
                wait(pe, kv_rdy, u)
                nc.tensor.transpose(px[0:L, 1, 0:P], z[:, h, 0:L], ident[:, :])
                nc.tensor.transpose(px[0:L, 1, P:2 * P], z[:, 8 + 2 * h, 0:L], ident[:, :])
                nc.tensor.transpose(px[0:L, 1, 2 * P:3 * P], z[:, 9 + 2 * h, 0:L], ident[:, :]).then_inc(kvt_rdy, 1)
                if panel:
                    gemm(u + P_ML, (P_ML + h) % 2, 0, XA)
                pe.wait_ge(kv_rdy, u + 1)
                pe.wait_ge(p_rdy, u + 1)
                wait(pe, e_done, u)
                st = cst[:, 0 if not (isinstance(c, int) and c == NLC) else 1, h, :]
                mm(px[0:L, 2, 0:DV + 1], pt[0:L, 0:L], va[0:L, :], start=True, stop=False)
                mm(px[0:L, 2, 0:DV + 1], qg[:, 0:L], st, start=False, stop=True)
                mm(px[:, 3, 0:DV + 1], kw[0:L, :], va[0:L, :], start=True, stop=True).then_inc(nu_rdy, 1)
                if panel:
                    gemm(u + P_ML, (P_ML + h) % 2, 1, XA)
                if not (isinstance(c, int) and c == 0) and h in (1, 2):
                    ml_turn(c - 1, h - 1, LC)
                if panel:
                    gemm(u + P_ML, (P_ML + h) % 2, 2, XA)

            def ml_turn(c, b, L):
                if b == 0:
                    pe.wait_ge(hn_rdy, c + 1)
                wait(pe, ht_cp, c * 2 + b)
                for j in range(4):
                    last = nc.tensor.transpose(px[:, 4, j * P:j * P + L], hn[0:L, 2 * b + j // 2, (j % 2) * P:(j % 2) * P + P],
                                               ident[0:L, 0:L])
                last.then_inc(ht_rdy, 1)

            for c in range(2):
                for h in range(HB):
                    ml_unit(c, 0, c, h, LC, True)
            with pe.Fori(1, N_MLG // 2) as i:
                for par in range(2):
                    for h in range(HB):
                        ml_unit(i * 2 + par, i, par, h, LC, True)
            for c in range(N_MLG, NLC + 1):
                for h in range(HB):
                    ml_unit(c, c // 2, c % 2, h, LC if c < NLC else TS, False)
            for b in range(2):
                ml_turn(NLC, b, TS)

            def panels8(p0, rhs):
                with pe.Fori(0, KT // 2) as i:
                    for s in range(2):
                        for n in range(NT):
                            gemm(i * 2 + (p0 + s), (p0 + s) % 2, n, rhs)

            pe.wait_ge(ya_lo, KT)
            panels8(P_PA, XB)
            pe.wait_ge(yb_lo, KT)
            panels8(P_PB, XA)
            pe.wait_ge(mg_lo, KT)
            panels8(P_OUT, XB)

            def ln_stats(M, ln):
                pe.wait_ge(r_rdy, KT * (ln + 1))
                for n in range(NT):
                    pe.wait_ge(acc_free[n], M)
                    for k in range(KT):
                        last = mm(acc[:, n, 0:NW], ones[:, :], XC[:, k, n * NW:(n + 1) * NW], start=(k == 0), stop=(k == KT - 1))
                    last.then_inc(acc_ready[n], 1)
                for k in range(KT):
                    pe.wait_ge(ln_sq, KT * ln + k + 1)
                    for n in range(NT):
                        if k == 0:
                            pe.wait_ge(acc_free[n], M + 1)
                        last = mm(acc[:, n, 0:NW], ones[:, :], ST[:, k % 4, n * NW:(n + 1) * NW], start=(k == 0), stop=(k == KT - 1))
                        if k == KT - 1:
                            last.then_inc(acc_ready[n], 1)
                    if k < KT - 1:
                        last.then_inc(ln_squ, 1)

            ln_stats(M_LN1, 0)

            def up(pi, M, i):
                pe.wait_ge(w_ready, pi + 1)
                for n in range(NT):
                    pe.wait_ge(acc_free[n], M)
                    for k in range(KT):
                        for j, (wi, xi) in enumerate(((0, 0), (0, 1), (1, 0))):
                            last = mm(acc[:, n, 0:NW], whl[:, i % 2, wi, k * P:(k + 1) * P], XA[:, xi, k, n * NW:(n + 1) * NW],
                                      start=(k == 0 and j == 0), stop=(k == KT - 1 and j == 2))
                            if n == 0 and k == 0 and j == 0:
                                last.then_inc(w_start, 1)
                    last.then_inc(acc_ready[n], 1)

            def down(pi, M, par, j):
                pe.wait_ge(fa_lo, j * 2 + 2)
                for m in range(KT):
                    s = m // 4
                    if m % 4 == 0:
                        pe.wait_ge(w_ready, pi + s + 1)
                    for n in range(NT):
                        pe.wait_ge(acc_free[n], M + m)
                        for k in range(2):
                            col = ((m % 4) * 2 + k) * P
                            for q, (wi, xi) in enumerate(((0, 0), (0, 1), (1, 0))):
                                last = mm(acc[:, n, 0:NW], whl[:, s, wi, col:col + P], fa[:, par, xi, k, n * NW:(n + 1) * NW],
                                          start=(k == 0 and q == 0), stop=(k == 1 and q == 2))
                                if m % 4 == 0 and n == 0 and k == 0 and q == 0:
                                    last.then_inc(w_start, 1)
                        last.then_inc(acc_ready[n], 1)

            pe.wait_ge(h2_lo, KT)
            for i in range(4):
                up(P_FFN + i, M_FFN + i, i)

            def ffn_iter(j, par):
                for i in range(4):
                    up(j * 6 + (P_FFN - 2 + i), j * 12 + (M_FFN - 8 + i), i)
                down(j * 6 + (P_FFN + 2), j * 12 + (M_FFN - 4), 1 - par, j - 1)

            with pe.Fori(0, (FG - 1) // 2) as i:
                ffn_iter(i * 2 + 1, 1)
                ffn_iter(i * 2 + 2, 0)
            down(P_FFN + 6 * FG - 2, M_FFN + 12 * FG - 8, 0, FG - 1)
            ln_stats(M_LN2, 1)

        @block.scalar
        def _(act):
            A = nc.scalar.activation
            act.dma_start(small[:, :], io["small"]).then_inc(c_in, 16)
            act.dma_start(ident[:, :], io["ident"]).then_inc(c_in, 16)
            act.dma_start(ones[:, :], io["ones"]).then_inc(c_in, 16)
            for i in range(2):
                act.dma_start(XC[:, 4 * i:4 * i + 4, :], io["x"][:, 4 * i:4 * i + 4, :]).then_inc(x_in[i], 16)
            act.wait_ge(c_in, 48)
            A(silu[:, 0, :, :], small[:, C_C:C_C + 16].rearrange("p (k s) -> p k s", s=2), ACT.Exp, scale=-1.0).then_inc(sl_e, 1)
            for k in range(KT):
                act.wait_ge(h_tmp, k + 1)
                A(XA[:, 0, k, :], ST[:, k % 4, 0:T], ACT.Copy).then_inc(h_hi, 1)

            act.wait_ge(ada_ev, 6)
            act.dma_start(alibi[:, :, :], io["alibi"]).then_inc(kv_in, 16)
            act.dma_start(kk[:, :, TP:TP + WIN], io["k_cache"]).then_inc(kv_in, 16)
            act.dma_start(vv[:, TP:TP + WIN], io["v_cache"]).then_inc(kv_in, 16)

            def take(M, n, dsts, func=ACT.Copy, **kw):
                act.wait_ge(acc_ready[n], M + 1)
                for dst, a, b in dsts:
                    last = A(dst, acc[:, n, a:b], func, **kw)
                last.then_inc(acc_free[n], 1)
                return last

            def q_evac(m):
                for n in range(NT):
                    dst = XC[:, m, n * NW:(n + 1) * NW] if isinstance(m, int) else \
                        XC[:, bass.ds(m, 1), n * NW:(n + 1) * NW].rearrange("p o w -> p (o w)")
                    take(m, n, [(dst, 0, NW)])

            q_evac(0)
            with act.Fori(1, KT) as m:
                q_evac(m)
            for p in range(KT, P_ATT):
                row = vv[:, :] if p == P_ATT - 1 else kk[:, p - KT, :]
                for n in range(NT):
                    dst = []
                    for a, b, s in pieces(n):
                        o = WIN * s
                        dst.append((row[:, a + o:b + o], a - n * NW, b - n * NW))
                    take(p, n, dst)
            act.drain().then_inc(qkv_ev, 1)
            act.wait_ge(qkv_ev, 1)
            act.wait_ge(kv_in, 48)
            for j in range(2):
                for s, a in ((0, TP - WIN), (1, TP + TS)):
                    act.dma_start(io["k_out"][j, s], kk[0:64, j, a:a + WIN]).then_inc(kv_out, 16)
                    act.dma_start(io["v_out"][j, s], vv[64 * j:64 * j + 64, a:a + WIN]).then_inc(kv_out, 16)

            def att_stage(c, par, w):
                smp = isinstance(c, int) and c == NCH
                qn = TS if smp else CH
                lo = TP if smp else None
                if isinstance(c, int):
                    qsl = slice(c * CH, c * CH + qn)
                    lo = TP if smp else (c + 1) * CH - w
                    bsl = slice(lo, lo + w)
                else:
                    qsl = bass.ds(c * CH, qn)
                    bsl = bass.ds(c * CH + (CH - w), w)
                wait(act, s_rdy, c * 2 - 2)
                A(qs[:, par, :, 0:qn], XC[:, :, qsl], ACT.Copy, scale=0.125)
                A(ks[:, par, :, 0:w], kk[:, :, bsl], ACT.Copy)
                A(vs[:, par, 0:w], vv[:, bsl], ACT.Copy).then_inc(st_rdy, 1)

            def att_exp(a, g, w):
                act.wait_ge(mx_rdy, a + 1)
                for j in range(4):
                    A(pb[:, g, j, 0:w], pb[:, g, j, 0:w], ACT.Exp, bias=nmx[:, g, j:j + 1], accum_out=rsum[:, g, j:j + 1])
                A(esk[:, g, :], esk[:, g, :], ACT.Exp).then_inc(ex_rdy, 1)

            def att_ptake(a, w, kb):
                act.wait_ge(tr_rdy, a + 1)
                wait(act, pv_rdy, a)
                if w > kb:
                    A(pta[0:w - kb, :, :], px[0:w - kb, 2, :].rearrange("p (j q) -> p j q", j=4), ACT.Copy)
                A(ptb[0:kb, :, :], px[0:kb, 3, :].rearrange("p (j q) -> p j q", j=4), ACT.Copy).then_inc(pt_rdy, 1)

            def spill_take(M, n, slot):
                act.wait_ge(acc_ready[n], M + 1)
                A(ST[:, slot, n * NW:(n + 1) * NW], acc[:, n, 0:NW], ACT.Copy).then_inc(acc_free[n], 1)

            def spill_free(slot, rounds):
                wait(act, sp_out[slot], rounds * 16)

            def spill_store(q, slot):
                act.drain().then_inc(sp_cp, 1)
                act.wait_ge(sp_cp, q + 1)
                act.dma_start(io["zs"][bass.ds(q, 1), :, :].rearrange("o p n -> p (o n)"), ST[:, slot, 0:T]).then_inc(sp_out[slot], 16)

            def att_chunk(c, r, par, w, wp, kbp, wn):
                kb = TS if isinstance(c, int) and c == NCH else CH
                att_exp(c * 2, 0, w)
                if wp:
                    att_ptake(c * 2 - 1, wp, kbp)
                spill_free(par, r)
                spill_take(c + P_ATT, 0, par)
                att_exp(c * 2 + 1, 1, w)
                if wn:
                    att_stage(c + 1, 1 - par, wn)
                spill_take(c + P_ATT, 1, par)
                att_ptake(c * 2, w, kb)
                spill_take(c + P_ATT, 2, par)
                spill_store(c, par)

            att_stage(0, 0, CH)
            att_chunk(0, 0, 0, CH, 0, 0, 2 * CH)
            att_chunk(1, 0, 1, 2 * CH, CH, CH, BAND)
            att_chunk(2, 1, 0, BAND, 2 * CH, CH, BAND)
            att_chunk(3, 1, 1, BAND, BAND, CH, BAND)
            with act.Fori(2, NCH // 2 - 1) as i:
                att_chunk(i * 2, i, 0, BAND, BAND, CH, BAND)
                att_chunk(i * 2 + 1, i, 1, BAND, BAND, CH, BAND)
            att_chunk(NCH - 2, NCH // 2 - 1, 0, BAND, BAND, CH, BAND)
            att_chunk(NCH - 1, NCH // 2 - 1, 1, BAND, BAND, CH, WIN + TS)
            att_chunk(NCH, NCH // 2, 0, WIN + TS, BAND, CH, 0)
            att_ptake(2 * NCH + 1, WIN + TS, TS)

            act.wait_ge(o_used, 2 * NCH + 2)
            act.wait_ge(sp_out[0], 16 * 9)
            act.wait_ge(sp_out[1], 16 * 8)
            act.wait_ge(kv_out, 16 * 8)
            act.dma_start(rowI, io["zs"][0, 0:HB, :]).then_inc(g_in, 16)
            act.dma_start(rowF, io["zs"][0, HB:2 * HB, :]).then_inc(g_in, 16)
            act.dma_start(rowE[:, :], io["rmask"]).then_inc(g_in, 16)
            act.dma_start(sel[:, :, :], io["sel"]).then_inc(ml_in, 16)
            act.dma_start(cmask[:, :], io["cmask"]).then_inc(ml_in, 16)
            act.dma_start(cst[:, 1, :, :], io["c_state"]).then_inc(ml_in, 16)

            def load_chunk(c, par, L):
                tok = slice(c * LC, c * LC + L) if isinstance(c, int) else bass.ds(c * LC, L)
                act.dma_start(zc[:, par, :, 0:L], io["zs"][1:17, :, tok].rearrange("q p t -> p q t")).then_inc(zc_in[par], 16)

            load_chunk(0, 0, LC)
            act.wait_ge(g_in, 48)
            A(rowC[:, :], rowF, ACT.Abs, bias=small[0:HB, C_BF:C_BF + 1])
            act.drain()
            A(rowC[:, :], rowC[:, :], ACT.Exp, scale=-1.0).then_inc(row_a, 1)
            act.wait_ge(row_d, 1)
            A(rowD[:, :], rowD[:, :], ACT.Ln).then_inc(row_a, 1)
            act.wait_ge(row_v, 1)
            for c in range(NLC + 1):
                L = LC if c < NLC else TS
                A(em_c[0:L, c, :], em_c[0:L, c, :], ACT.Exp, scale=-1.0)
            act.drain().then_inc(row_v, 1)

            def ml_unit(c, r, par, h, L, panel):
                u = c * 4 + h
                act.wait_ge(d_rdy, u + 1)
                A(wd[0:L, 0:L], wd[0:L, 0:L], ACT.Exp)
                ci = c if isinstance(c, int) else None
                bias = mp_c[:, h, c:c + 1] if ci is not None else mp_c[:, h, bass.ds(c, 1)]
                A(gb[:, 0:L], rs[:, 0:L], ACT.Exp, bias=bias).then_inc(wg_rdy, 1)
                act.wait_ge(wg_rdy, u + 1)
                A(wks[0:L, :], wd[0:L, L - 1:L], ACT.Copy, scale=KB_SCALE)
                act.wait_ge(kvt_rdy, u + 1)
                wait(act, nu_rdy, u)
                A(va[0:L, 0:DV], px[0:L, 1, P:3 * P], ACT.Copy)
                act.drain()
                A(kw[0:L, :], px[0:L, 1, 0:P], ACT.Copy, scale=wks[0:L, :]).then_inc(kv_rdy, 1)
                if panel:
                    slot = (1 + h) % 2
                    spill_free(slot, c * 2 + (17 + h - slot) // 2)
                    spill_take(u + P_ML, 0, slot)
                    spill_take(u + P_ML, 1, slot)
                if h in (1, 2) and not (ci == 0):
                    ml_turn(c - 1, h - 1, LC)
                if panel:
                    spill_take(u + P_ML, 2, slot)
                    spill_store(u + 17, slot)
                if h == 1 and ci != NLC:
                    wait(act, nu_rdy, c * 4)
                    load_chunk(c + 1, 1 - par, LC if ci is None or ci + 1 < NLC else TS)
                if h == 3:
                    act.wait_ge(var_rdy, c + 1)
                    A(rstd[0:L, :], rstd[0:L, :], ACT.Sqrt).then_inc(sd_rdy, 1)

            def ml_turn(c, b, L):
                act.wait_ge(ht_rdy, c * 2 + b + 1)
                if b == 0:
                    wait(act, hs_out, c * 16)
                A(hT[:, 4 * b:4 * b + 4, 0:L], px[:, 4, :].rearrange("p (j q) -> p j q", j=4)[:, :, 0:L], ACT.Copy).then_inc(ht_cp, 1)
                if b == 1:
                    act.wait_ge(ht_cp, c * 2 + 2)
                    tok = slice(c * LC, c * LC + L) if isinstance(c, int) else bass.ds(c * LC, L)
                    act.dma_start(io["hs"][:, :, tok].rearrange("j p t -> p j t"), hT[:, :, 0:L]).then_inc(hs_out, 16)

            act.wait_ge(row_v, 3)
            for c in range(2):
                for h in range(HB):
                    ml_unit(c, 0, c, h, LC, True)
            with act.Fori(1, N_MLG // 2) as i:
                for par in range(2):
                    for h in range(HB):
                        ml_unit(i * 2 + par, i, par, h, LC, True)
            for c in range(N_MLG, NLC + 1):
                for h in range(HB):
                    ml_unit(c, c // 2, c % 2, h, LC if c < NLC else TS, False)
            for b in range(2):
                ml_turn(NLC, b, TS)
            act.wait_ge(e_done, 4 * NLC + 4)
            act.dma_start(io["c_out"].rearrange("s p h v -> p s h v"), cst[:, :, :, :]).then_inc(st_out, 16)
            act.dma_start(io["m_out"][0], rowM[:, TP - 1:TP]).then_inc(st_out, 16)
            act.dma_start(io["m_out"][1], rowM[:, T - 1:T]).then_inc(st_out, 16)

            act.wait_ge(sp_out[0], 16 * ((N_SPILL + 1) // 2))
            act.wait_ge(sp_out[1], 16 * (N_SPILL // 2))
            act.wait_ge(hs_out, 16 * (NLC + 1))
            act.wait_ge(st_out, 48)

            def load_gate(q0, m, s, used):
                wait(act, gt_used, used)
                act.dma_start(ST[:, 2 + s, 0:T], io["zs"][q0 + m]).then_inc(gt_in[s], 16)

            for m in range(2):
                load_gate(Q_GA, m, m, 0)
            for k in range(KT):
                A(XB[:, 0, k, :], XC[:, k, :], ACT.Copy).then_inc(ya_hi, 1)
            for m in range(KT):
                wait(act, yb_lo, m)
                act.dma_start(ST[:, 0, 0:T], io["zs"][Q_O + m]).then_inc(og_in, 16)
                act.dma_start(ST[:, 1, 0:T], io["hs"][m]).then_inc(hn_in, 16)
                act.wait_ge(gt_in[m % 2], 16 * (m // 2 + 1))
                A(ST[:, 2 + m % 2, 0:T], ST[:, 2 + m % 2, 0:T], ACT.Sigmoid).then_inc(gt_rdy, 1)
                act.wait_ge(og_in, 16 * (m + 1))
                A(ST[:, 0, 0:T], ST[:, 0, 0:T], ACT.Sigmoid).then_inc(sg_rdy, 1)
                act.wait_ge(yb_rdy, m + 1)
                A(XA[:, 0, m, :], ST[:, 0, 0:T], ACT.Copy).then_inc(yb_hi, 1)
                if m >= 1 and m + 1 < KT:
                    load_gate(Q_GA, m + 1, (m + 1) % 2, m)
            for m in range(2):
                load_gate(Q_GB, m, m, KT - 1 + m)
            for m in range(KT):
                act.wait_ge(gt_in[m % 2], 16 * (4 + m // 2 + 1))
                A(ST[:, 2 + m % 2, 0:T], ST[:, 2 + m % 2, 0:T], ACT.Sigmoid).then_inc(gt_rdy, 1)
                act.wait_ge(mg_rdy, m + 1)
                A(XB[:, 0, m, :], ST[:, 0, 0:T], ACT.Copy).then_inc(mg_hi, 1)
                if m + 2 < KT:
                    load_gate(Q_GB, m + 2, m % 2, KT + m + 1)
            for m in range(KT):
                wait(act, gt_used, 2 * KT if m < 2 else 0)
                wait(act, r_rdy, m - 1)
                act.dma_start(ST[:, 2 + m % 2, 0:T], io["x"][:, m, :]).then_inc(xr_in[m % 2], 16)

            def ln_act(ln):
                for k in range(KT):
                    act.wait_ge(ln_d, KT * ln + k + 1)
                    if k >= 4:
                        act.wait_ge(ln_squ, (KT - 1) * ln + k - 3)
                    A(ST[:, k % 4, 0:T], XC[:, k, :], ACT.Square).then_inc(ln_sq, 1)
                for n in range(NT):
                    act.wait_ge(ln_v, NT * ln + n + 1)
                    A(ST[:, 0, n * NW:(n + 1) * NW], ST[:, 0, n * NW:(n + 1) * NW], ACT.Sqrt).then_inc(ln_s, 1)

            ln_act(0)
            act.wait_ge(mg_lo, KT)
            act.wait_ge(acc_ready[NT - 1], P_FFN)
            act.dma_start(fc[:, :, :, :], io["ffn_consts"]).then_inc(fc_in, 16)
            for k in range(KT):
                act.wait_ge(ln_t, k + 1)
                if k >= 3:
                    act.wait_ge(h2_lo, k - 2)
                s = 1 + k % 3
                A(ST[:, s, 0:TP], XC[:, k, 0:TP], ACT.Identity, scale=der[:, 0, k:k + 1], bias=der[:, 2, k:k + 1])
                A(ST[:, s, TP:T], XC[:, k, TP:T], ACT.Identity, scale=der[:, 1, k:k + 1], bias=der[:, 3, k:k + 1]).then_inc(h2_t, 1)
                act.wait_ge(h2_t, k + 1)
                A(XA[:, 0, k, :], ST[:, s, 0:T], ACT.Copy).then_inc(h2_hi, 1)

            def fgroup(j):
                return fc[:, j, :, :] if isinstance(j, int) else fc[:, bass.ds(j, 1), :, :].rearrange("p o a b -> p (o a) b")

            def ffn_up(j, M, par, i):
                wait(act, cv_d, j * 4 + i - 3)
                A(ub[:, i, TP + 2:TP + 4], fca[:, i, 5:7], ACT.Copy)
                for n in range(NT):
                    act.wait_ge(acc_ready[n], M + 1)
                    for a, b, s in pieces(n):
                        last = A(ub[:, i, 2 + a + 2 * s:2 + b + 2 * s], acc[:, n, a - n * NW:b - n * NW], ACT.Identity,
                                 bias=fca[:, i, 0:1])
                    last.then_inc(acc_free[n], 1)
                act.drain().then_inc(u_rdy, 1)
                wait(act, fa_lo, j * 2)
                A(ST[:, i, 0:CW], ub[:, i, 2:UW], ACT.Identity, scale=fca[:, i, 3:4], bias=fca[:, i, 4:5]).then_inc(cv_a, 1)

            def ffn_gelu(j, i):
                act.wait_ge(cv_d, j * 4 + i + 1)
                A(ST[:, i, 0:CW], ST[:, i, 0:CW], ACT.Gelu_apprx_tanh).then_inc(gl_rdy, 1)

            def ffn_round(j, par):
                for t in range(2):
                    act.wait_ge(pr_rdy, j * 2 + t + 1)
                    A(fa[:, par, 0, t, 0:TP], ST[:, t, 0:TP], ACT.Copy)
                    A(fa[:, par, 0, t, TP:T], ST[:, t, TP + 2:CW], ACT.Copy).then_inc(fa_hi, 1)

            def ffn_group(j, M, par):
                A(fca[:, :, :], fgroup(j), ACT.Copy)
                act.drain()
                for i in range(4):
                    ffn_up(j, M + i, par, i)
                    if i == 3:
                        ffn_gelu(j, 2)
                ffn_gelu(j, 3)
                ffn_round(j, par)

            act.wait_ge(fc_in, 16)
            act.wait_ge(h2_lo, KT)
            ffn_group(0, M_FFN, 0)
            with act.Fori(0, (FG - 1) // 2) as i:
                ffn_group(i * 2 + 1, i * 24 + (M_FFN + 4), 1)
                ffn_group(i * 2 + 2, i * 24 + (M_FFN + 16), 0)
            act.wait_ge(cs_out, 1)
            act.dma_start(io["cs_out"], cs[:, :, :, :]).then_inc(cs_out, 16)
            ln_act(1)
            for k in range(KT):
                act.wait_ge(ln_t, KT + k + 1)
                A(XC[:, k, :], XC[:, k, :], ACT.Identity, scale=small[:, C_L2W + k:C_L2W + k + 1],
                  bias=small[:, C_L2B + k:C_L2B + k + 1]).then_inc(y_rdy, 1)
                act.wait_ge(y_rdy, k + 1)
                act.dma_start(io["y"][:, k, :], XC[:, k, :]).then_inc(y_out, 16)
            act.wait_ge(y_out, 16 * KT)
            act.wait_ge(cs_out, 17)

        @block.vector
        def _(dve):
            V = nc.vector
            dve.wait_ge(c_in, 48)
            dve.wait_ge(sl_e, 1)
            V.tensor_scalar(silu[:, 1, :, :], silu[:, 0, :, :], 1.0, None, ALU.add)
            dve.drain()
            V.reciprocal(silu[:, 0, :, :], silu[:, 1, :, :]).then_inc(sl_d, 1)
            dve.drain()
            V.tensor_tensor(silu[:, 2, :, :], silu[:, 0, :, :], small[:, C_C:C_C + 16].rearrange("p (k s) -> p k s", s=2),
                            ALU.mult).then_inc(sl_d, 1)
            bada = small[:, C_BADA:C_BADA + 48].rearrange("p (i m) -> p i m", i=6)
            for i in range(6):
                dve.wait_ge(ada_used, KT * (i + 1))
                V.tensor_tensor(mod[:, i, :, :], px[:, 0, 0:16].rearrange("p (m s) -> p m s", s=2),
                                bada[:, i, :].unsqueeze(2).to_broadcast([P, KT, 2]), ALU.add).then_inc(ada_ev, 1)
                if i in (1, 4):
                    dve.drain()
                    V.tensor_scalar(mod[:, i, :, :], mod[:, i, :, :], 1.0, None, ALU.add)
                if i == 1:
                    dve.drain()
                    for k in range(KT):
                        dve.wait_ge(x_in[k // 4], 16)
                        for a, b, s in ((0, TP, 0), (TP, T, 1)):
                            last = V.tensor_scalar(ST[:, k % 4, a:b], XC[:, k, a:b], mod[:, 1, k, s:s + 1], mod[:, 0, k, s:s + 1],
                                                   ALU.mult, ALU.add)
                        last.then_inc(h_tmp, 1)
                        dve.wait_ge(h_hi, k + 1)
                        V.tensor_tensor(XA[:, 1, k, :], ST[:, k % 4, 0:T], XA[:, 0, k, :].bitcast(F32), ALU.subtract).then_inc(h_lo, 1)
            dve.drain()
            for k in range(KT):
                w, b = small[:, C_L1W + k:C_L1W + k + 1], small[:, C_L1B + k:C_L1B + k + 1]
                for s in range(2):
                    V.tensor_scalar(der[:, s, k:k + 1], w, mod[:, 4, k, s:s + 1], None, ALU.mult)
                    V.tensor_scalar(der[:, 2 + s, k:k + 1], b, mod[:, 4, k, s:s + 1], mod[:, 3, k, s:s + 1], ALU.mult, ALU.add)
            V.tensor_scalar(der[:, 4, :], small[:, C_L1W:C_L1W + KT], ALPHA, None, ALU.mult)
            V.tensor_scalar(der[:, 5, :], small[:, C_L1B:C_L1B + KT], ALPHA, None, ALU.mult)
            dve.drain()

            def att_max(c, a, par, g, w, kb):
                dve.wait_ge(s_rdy, a + 1)
                wait(dve, tr_rdy, a - 1)
                for b in range(2):
                    V.tensor_tensor(pb[:, g, 2 * b:2 * b + 2, 0:w],
                                    px[:, b, 0:2 * BAND].rearrange("p (j w) -> p j w", j=2)[:, :, 0:w],
                                    alibi[:, 4 * g + 2 * b:4 * g + 2 * b + 2, alo(c, w):alo(c, w) + w], ALU.add)
                if g == 0:
                    wait(dve, pv_rdy, a - 2)
                    if w > kb:
                        V.tensor_copy(vt[0:w - kb, par, 0, :], px[0:w - kb, 0, 384:512])
                    V.tensor_copy(vt[0:kb, par, 1, :], px[0:kb, 1, 384:512])
                dve.drain().then_inc(s_used, 1)
                V.tensor_reduce(nmx[:, g, :], pb[:, g, :, 0:w], AX.X, ALU.max)
                dve.drain()
                V.tensor_tensor(nmx[:, g, :], nmx[:, g, :], small[:, C_SINK + 4 * g:C_SINK + 4 * g + 4], ALU.max)
                dve.drain()
                V.tensor_scalar(nmx[:, g, :], nmx[:, g, :], -1.0, None, ALU.mult)
                dve.drain()
                V.tensor_tensor(esk[:, g, :], nmx[:, g, :], small[:, C_SINK + 4 * g:C_SINK + 4 * g + 4], ALU.add).then_inc(mx_rdy, 1)

            def alo(c, w):
                return 0 if isinstance(c, int) and c == NCH else BAND - w

            def att_norm(a, g, w):
                dve.wait_ge(ex_rdy, a + 1)
                V.tensor_tensor(rden[:, :], rsum[:, g, :], esk[:, g, :], ALU.add)
                dve.drain()
                V.reciprocal(rden[:, :], rden[:, :])
                dve.drain()
                V.tensor_tensor(pb[:, g, :, 0:w], pb[:, g, :, 0:w], rden[:, :].unsqueeze(2).to_broadcast([P, 4, w]), ALU.mult)\
                 .then_inc(pn_rdy, 1)

            def att_take(c, a, g):
                dve.wait_ge(pv_rdy, a + 1)
                n = TS if isinstance(c, int) and c == NCH else CH
                tok = slice(c * CH, c * CH + n) if isinstance(c, int) else bass.ds(c * CH, n)
                V.tensor_copy(XC[:, 4 * g:4 * g + 4, tok], px[:, 4, 0:4 * CH].rearrange("p (j q) -> p j q", j=4)[:, :, 0:n])\
                 .then_inc(o_used, 1)

            def att_chunk(c, par, w, wp):
                kb = TS if isinstance(c, int) and c == NCH else CH
                att_max(c, c * 2, par, 0, w, kb)
                if wp:
                    att_norm(c * 2 - 1, 1, wp)
                att_max(c, c * 2 + 1, par, 1, w, kb)
                if wp:
                    att_take(c - 1, c * 2 - 1, 1)
                att_norm(c * 2, 0, w)
                att_take(c, c * 2, 0)

            dve.wait_ge(kv_in, 48)
            att_chunk(0, 0, CH, 0)
            att_chunk(1, 1, 2 * CH, CH)
            att_chunk(2, 0, BAND, 2 * CH)
            att_chunk(3, 1, BAND, BAND)
            with dve.Fori(2, NCH // 2) as i:
                att_chunk(i * 2, 0, BAND, BAND)
                att_chunk(i * 2 + 1, 1, BAND, BAND)
            att_chunk(NCH, 0, WIN + TS, BAND)
            att_norm(2 * NCH + 1, 1, WIN + TS)
            att_take(NCH, 2 * NCH + 1, 1)

            dve.wait_ge(row_a, 1)
            V.tensor_scalar(rowD[:, :], rowC[:, :], 1.0, None, ALU.add)
            V.tensor_scalar(rowF, rowF, small[0:HB, C_BF:C_BF + 1], 0.0, ALU.add, ALU.min)
            V.tensor_scalar(rowI, rowI, small[0:HB, C_BI:C_BI + 1], None, ALU.add)
            dve.drain()
            V.tensor_scalar(rowR[:, :], rowD[:, :], -1.0, None, ALU.add).then_inc(row_d, 1)
            dve.drain()
            V.tensor_tensor(rowC[:, :], rowC[:, :], rowR[:, :], ALU.subtract)
            dve.wait_ge(row_a, 2)
            dve.drain()
            V.tensor_tensor(rowC[:, :], rowC[:, :], rowD[:, :], ALU.add)
            dve.drain()
            V.tensor_tensor(rowF, rowF, rowC[:, :], ALU.subtract)
            dve.drain()
            V.tensor_tensor_scan(rowD[:, :], rowE[:, :], rowF, 0.0, ALU.mult, ALU.add)
            V.tensor_tensor_scan(rowM[:, 0:TP], rowF[:, 0:TP], rowI[:, 0:TP], 0.0, ALU.add, ALU.max)
            V.tensor_tensor_scan(rowM[:, TP:T], rowF[:, TP:T], rowI[:, TP:T], small[0:HB, C_M0:C_M0 + 1], ALU.add, ALU.max)
            V.memset(mprow[:, 0:1], 0.0)
            V.tensor_copy(mprow[:, NLC:NLC + 1], small[0:HB, C_M0:C_M0 + 1])
            V.memset(va[:, DV:DV + 1], 1.0)
            V.memset(cst[:, 0, :, :], 0.0)
            dve.drain()
            V.tensor_copy(mprow[:, 1:NLC], rowM[:, 0:TP].rearrange("p (c l) -> p c l", l=LC)[:, 0:NLC - 1, LC - 1])
            V.tensor_tensor(rowC[:, :], rowI, rowD[:, :], ALU.subtract)
            V.tensor_tensor(rowR[:, :], rowD[:, :], rowM[:, :], ALU.subtract)
            dve.drain().then_inc(row_d, 1)
            dve.wait_ge(row_p, 1)
            dve.wait_ge(ml_in, 48)
            for c0, c1, L in ((0, NLC, LC), (NLC, NLC + 1, TS)):
                V.tensor_copy(at_c[0:L, c0:c1, :], px[0:L, 0, 4 * c0:4 * c1].rearrange("p (c h) -> p c h", h=HB))
                V.tensor_copy(em_c[0:L, c0:c1, :], px[0:L, 0, 64 + 4 * c0:64 + 4 * c1].rearrange("p (c h) -> p c h", h=HB))
            V.tensor_copy(mp_c[:, :, :], px[:, 0, 128:164].rearrange("p (h c) -> p h c", h=HB))
            dve.drain().then_inc(row_v, 1)
            dve.wait_ge(row_v, 2)
            dve.drain().then_inc(row_v, 1)

            def ml_unit(c, par, h, L):
                u = c * 4 + h
                ci = c if isinstance(c, int) else None

                def col(t, n=L):
                    return t[0:n, c, h:h + 1] if ci is not None else \
                        t[0:n, bass.ds(c, 1), h:h + 1].rearrange("p a b -> p (a b)")

                dve.wait_ge(sr_rdy, u + 1)
                V.tensor_copy(rs[:, 0:L], px[:, 0, P:P + L])
                dve.drain()
                V.scalar_tensor_tensor(wd[0:L, 0:L], rs[0:L, 0:L], col(at_c), cmask[0:L, 0:L], ALU.add, ALU.add).then_inc(d_rdy, 1)
                dve.wait_ge(wg_rdy, u + 1)
                V.scalar_tensor_tensor(pt[0:L, 0:L], px[0:L, 0, 0:L], KB_SCALE, wd[0:L, 0:L], ALU.mult, ALU.mult)
                V.tensor_tensor(qg[:, 0:L], zc[:, par, 4 + h, 0:L], gb[:, 0:L], ALU.mult)
                dve.drain().then_inc(p_rdy, 1)
                if h == 0 and ci != 0:
                    ml_norm(c - 1, LC)
                dve.wait_ge(nu_rdy, u + 1)
                s = 1 if ci == NLC else 0
                V.scalar_tensor_tensor(cst[:, s, h, :], cst[:, s, h, :], gb[:, L - 1:L], px[:, 3, 0:DV + 1], ALU.mult, ALU.add)
                V.tensor_scalar(dn[0:L, 0:1], px[0:L, 2, DV:DV + 1], -1.0, col(em_c), ALU.mult, ALU.max)
                dve.drain()
                V.tensor_tensor(dn[0:L, 0:1], dn[0:L, 0:1], px[0:L, 2, DV:DV + 1], ALU.max)
                dve.drain()
                V.reciprocal(dn[0:L, 1:2], dn[0:L, 0:1])
                dve.drain()
                V.tensor_scalar(hh[0:L, h, :], px[0:L, 2, 0:DV], dn[0:L, 1:2], None, ALU.mult)
                dve.drain().then_inc(e_done, 1)
                V.bn_stats(bst[0:L, h, :], hh[0:L, h, :])
                dve.drain()
                V.bn_aggr(mv[0:L, h, :], bst[0:L, h, :])
                if h == HB - 1:
                    dve.drain()
                    V.tensor_scalar(rstd[0:L, :], mv[0:L, :, 1], EPS, None, ALU.add).then_inc(var_rdy, 1)

            def ml_norm(c, L):
                dve.wait_ge(sd_rdy, c + 1)
                wait(dve, ht_rdy, c * 2)
                V.reciprocal(rstd[0:L, :], rstd[0:L, :])
                dve.drain()
                for h in range(HB):
                    last = V.tensor_scalar(hn[0:L, h, :], hh[0:L, h, :], mv[0:L, h, 0:1], rstd[0:L, h:h + 1],
                                           ALU.subtract, ALU.mult)
                dve.drain().then_inc(hn_rdy, 1)

            for c in range(2):
                for h in range(HB):
                    ml_unit(c, c, h, LC)
            with dve.Fori(1, N_MLG // 2) as i:
                for par in range(2):
                    for h in range(HB):
                        ml_unit(i * 2 + par, par, h, LC)
            for c in range(N_MLG, NLC + 1):
                for h in range(HB):
                    ml_unit(c, c % 2, h, LC if c < NLC else TS)
            ml_norm(NLC, TS)

            for k in range(KT):
                dve.wait_ge(ya_hi, k + 1)
                V.tensor_tensor(XB[:, 1, k, :], XC[:, k, :], XB[:, 0, k, :].bitcast(F32), ALU.subtract).then_inc(ya_lo, 1)
            dve.drain()
            for m in range(KT):
                dve.wait_ge(hn_in, 16 * (m + 1))
                dve.wait_ge(sg_rdy, m + 1)
                V.scalar_tensor_tensor(ST[:, 0, 0:T], ST[:, 0, 0:T], small[:, C_NW + m:C_NW + m + 1], ST[:, 1, 0:T],
                                       ALU.mult, ALU.mult).then_inc(yb_rdy, 1)
                dve.wait_ge(yb_hi, m + 1)
                V.tensor_tensor(XA[:, 1, m, :], ST[:, 0, 0:T], XA[:, 0, m, :].bitcast(F32), ALU.subtract).then_inc(yb_lo, 1)
                dve.wait_ge(gt_rdy, m + 1)
                for n in range(NT):
                    dve.wait_ge(acc_ready[n], P_PA + m + 1)
                    V.tensor_tensor(XC[:, m, n * NW:(n + 1) * NW], acc[:, n, 0:NW], ST[:, 2 + m % 2, n * NW:(n + 1) * NW], ALU.mult)\
                     .then_inc(acc_free[n], 1)
                dve.drain().then_inc(gt_used, 1)
            for m in range(KT):
                dve.wait_ge(gt_rdy, KT + m + 1)
                for n in range(NT):
                    dve.wait_ge(acc_ready[n], P_PB + m + 1)
                    V.tensor_tensor(ST[:, 0, n * NW:(n + 1) * NW], acc[:, n, 0:NW], ST[:, 2 + m % 2, n * NW:(n + 1) * NW], ALU.mult)\
                     .then_inc(acc_free[n], 1)
                dve.drain().then_inc(gt_used, 1)
                V.tensor_tensor(ST[:, 0, 0:T], ST[:, 0, 0:T], XC[:, m, :], ALU.add).then_inc(mg_rdy, 1)
                dve.wait_ge(mg_hi, m + 1)
                V.tensor_tensor(XB[:, 1, m, :], ST[:, 0, 0:T], XB[:, 0, m, :].bitcast(F32), ALU.subtract).then_inc(mg_lo, 1)
                dve.drain()
            for m in range(KT):
                dve.wait_ge(xr_in[m % 2], 16 * (m // 2 + 1))
                V.tensor_scalar(ST[:, 2 + m % 2, 0:T], ST[:, 2 + m % 2, 0:T], ALPHA, None, ALU.mult)
                dve.drain()
                for n in range(NT):
                    dve.wait_ge(acc_ready[n], P_OUT + m + 1)
                    for a, b, s in pieces(n):
                        last = V.scalar_tensor_tensor(XC[:, m, a:b], acc[:, n, a - n * NW:b - n * NW], mod[:, 2, m, s:s + 1],
                                                      ST[:, 2 + m % 2, a:b], ALU.mult, ALU.add)
                    last.then_inc(acc_free[n], 1)
                dve.drain().then_inc(r_rdy, 1)

            def ln_dve(M, ln):
                for n in range(NT):
                    dve.wait_ge(acc_ready[n], M + 1)
                for k in range(KT):
                    V.tensor_tensor(XCt[:, k, :, :], XCt[:, k, :, :], acc_w, ALU.subtract).then_inc(ln_d, 1)
                dve.drain()
                for n in range(NT):
                    dve.sem_inc(acc_free[n], 1)
                for n in range(NT):
                    dve.wait_ge(acc_ready[n], M + 2)
                    V.tensor_scalar(ST[:, 0, n * NW:(n + 1) * NW], acc[:, n, 0:NW], EPS, None, ALU.add).then_inc(acc_free[n], 1)
                for n in range(NT):
                    dve.drain()
                    V.reciprocal(ST[:, 0, n * NW:(n + 1) * NW], ST[:, 0, n * NW:(n + 1) * NW]).then_inc(ln_v, 1)
                dve.wait_ge(ln_s, NT * (ln + 1))
                for k in range(KT):
                    V.tensor_tensor(XC[:, k, :], XC[:, k, :], ST[:, 0, 0:T], ALU.mult).then_inc(ln_t, 1)
                    if ln == 0 and k >= 1:
                        ln1_rest(k - 1)
                if ln == 0:
                    ln1_rest(KT - 1)

            def ln1_rest(k):
                dve.wait_ge(h2_hi, k + 1)
                V.tensor_tensor(XA[:, 1, k, :], ST[:, 1 + k % 3, 0:T], XA[:, 0, k, :].bitcast(F32), ALU.subtract).then_inc(h2_lo, 1)
                V.tensor_scalar(XC[:, k, :], XC[:, k, :], der[:, 4, k:k + 1], der[:, 5, k:k + 1], ALU.mult, ALU.add)

            ln_dve(M_LN1, 0)

            def fgroup(j):
                return fc[:, j, :, :] if isinstance(j, int) else fc[:, bass.ds(j, 1), :, :].rearrange("p o a b -> p (o a) b")

            def cout(j, i, a):
                return cs[:, j, i, a:a + 2] if isinstance(j, int) else \
                    cs[:, bass.ds(j, 1), i, a:a + 2].rearrange("p a b -> p (a b)")

            def ffn_conv(j, i):
                dve.wait_ge(u_rdy, j * 4 + i + 1)
                V.tensor_copy(cout(j, i, 0), ub[:, i, TP:TP + 2])
                V.tensor_copy(cout(j, i, 2), ub[:, i, UW - 2:UW])
                dve.wait_ge(cv_a, j * 4 + i + 1)
                V.scalar_tensor_tensor(ST[:, i, 0:CW], ub[:, i, 0:CW], fcd[:, i, 1:2], ST[:, i, 0:CW], ALU.mult, ALU.add)
                dve.drain()
                V.scalar_tensor_tensor(ST[:, i, 0:CW], ub[:, i, 1:CW + 1], fcd[:, i, 2:3], ST[:, i, 0:CW], ALU.mult, ALU.add)\
                 .then_inc(cv_d, 1)

            def ffn_prod(j, t):
                dve.wait_ge(gl_rdy, j * 2 + t + 1)
                V.tensor_tensor(ST[:, t, 0:CW], ST[:, t, 0:CW], ST[:, 2 + t, 0:CW], ALU.mult).then_inc(pr_rdy, 1)

            def ffn_low(j, par, t):
                dve.wait_ge(fa_hi, j * 2 + t + 1)
                V.tensor_tensor(fa[:, par, 1, t, 0:TP], ST[:, t, 0:TP], fa[:, par, 0, t, 0:TP].bitcast(F32), ALU.subtract)
                V.tensor_tensor(fa[:, par, 1, t, TP:T], ST[:, t, TP + 2:CW], fa[:, par, 0, t, TP:T].bitcast(F32), ALU.subtract)
                dve.drain().then_inc(fa_lo, 1)

            def ffn_take(M, m):
                for n in range(NT):
                    dve.wait_ge(acc_ready[n], M + m + 1)
                    for a, b, s in pieces(n):
                        last = V.scalar_tensor_tensor(XC[:, m, a:b], acc[:, n, a - n * NW:b - n * NW], mod[:, 5, m, s:s + 1],
                                                      XC[:, m, a:b], ALU.mult, ALU.add)
                    last.then_inc(acc_free[n], 1)

            def ffn_iter(j, par, M):
                V.tensor_copy(fcd[:, :, :], fgroup(j))
                dve.drain()
                for i in range(3):
                    ffn_conv(j, i)
                ffn_take(M, 0)
                ffn_conv(j, 3)
                ffn_take(M, 1)
                ffn_prod(j, 0)
                ffn_take(M, 2)
                ffn_prod(j, 1)
                ffn_take(M, 3)
                ffn_low(j, par, 0)
                ffn_take(M, 4)
                ffn_low(j, par, 1)
                for m in range(5, KT):
                    ffn_take(M, m)

            dve.wait_ge(fc_in, 16)
            V.memset(ub[:, :, 0:2], 0.0)
            V.tensor_copy(fcd[:, :, :], fgroup(0))
            dve.drain()
            for i in range(4):
                ffn_conv(0, i)
            for t in range(2):
                ffn_prod(0, t)
            for t in range(2):
                ffn_low(0, 0, t)
            with dve.Fori(0, (FG - 1) // 2) as i:
                ffn_iter(i * 2 + 1, 1, i * 24 + (M_FFN + 8))
                ffn_iter(i * 2 + 2, 0, i * 24 + (M_FFN + 20))
            dve.drain().then_inc(cs_out, 1)
            for m in range(KT):
                ffn_take(M_FFN + 12 * FG - 8, m)
                dve.drain().then_inc(r_rdy, 1)
            ln_dve(M_LN2, 1)


IN_SHAPES = {
    "w_panels": (N_PANEL, P, D), "w_ada": (48, P, D), "x": (P, KT, T), "small": (P, N_SMALL), "ident": (P, P), "ones": (P, P),
    "alibi": (P, 8, BAND), "k_cache": (P, 2, WIN), "v_cache": (P, WIN), "rmask": (HB, T), "sel": (HB, HB, P), "cmask": (P, P),
    "c_state": (P, HB, DV + 1), "ffn_consts": (P, FG, 4, 8),
}
OUT_SHAPES = {
    "y": (P, KT, T), "k_out": (2, 2, 64, WIN), "v_out": (2, 2, 64, WIN), "c_out": (2, P, HB, DV + 1), "m_out": (2, HB, 1),
    "cs_out": (P, FG, 4, 4),
}


def tiles(w):
    n = w.shape[1] // P
    return w.reshape(KT, P, n, P).transpose(2, 1, 0, 3).reshape(n, P, D)


def kernel(**inputs):
    import concourse.bacc as bacc
    from concourse.bass_utils import run_bass_kernel_spmd

    a = {k: np.asarray(v) for k, v in inputs.items()}
    f = np.float32
    w_in = a["w_in"][0]
    cut = np.cumsum([1024, 128, 128, 512, 512, 1024, 4, 4, 1024, 1024])
    qa, ka, va, qb, kb, vb, ig, fg, og, ga, gb = np.split(w_in, cut, axis=1)
    kdup = np.concatenate([ka[:, 0:64], ka[:, 0:64], ka[:, 64:128], ka[:, 64:128]], axis=1)
    gates = np.concatenate([ig, fg, np.zeros((D, P - 8), f)], axis=1)
    up = tiles(a["w_up"][0])
    dn = a["w_down"][0].reshape(FG, 2, P, 2, 4, P).transpose(0, 3, 2, 4, 1, 5).reshape(FG, 2, P, D)

    def up4(j):
        return [up[2 * j], up[2 * j + 1], up[UT // 2 + 2 * j], up[UT // 2 + 2 * j + 1]]

    panels = [tiles(np.concatenate([qa, kdup, va, gates, kb, qb, vb, og, gb, ga], axis=1)),
              tiles(a["w_proj_a"][0]), tiles(a["w_proj_b"][0]), tiles(a["w_out"][0])]
    ffn = up4(0)
    for j in range(1, FG):
        ffn += up4(j) + [dn[j - 1, 0], dn[j - 1, 1]]
    ffn += [dn[FG - 1, 0], dn[FG - 1, 1]]
    w_panels = np.concatenate(panels + [np.stack(ffn)], axis=0)

    def cols(v):
        return v.reshape(-1, P).T

    x = np.concatenate([a["x_prompt"][0], a["x_sample"][0]], axis=0)
    small = np.zeros((P, N_SMALL), f)
    small[:, C_BADA:C_BADA + 48] = cols(a["b_ada"][0])
    for c, nme in ((C_L1W, "ln1_w"), (C_L1B, "ln1_b"), (C_L2W, "ln2_w"), (C_L2B, "ln2_b"), (C_NW, "mlstm_norm_w")):
        small[:, c:c + 8] = cols(a[nme][0])
    small[:, C_C:C_C + 16:2] = cols(a["c_prompt"][0])
    small[:, C_C + 1:C_C + 16:2] = cols(a["c_sample"][0])
    small[:, C_SINK:C_SINK + 8] = np.repeat(a["attn_sinks"][0].reshape(8, 2).T, 64, axis=0)
    small[0:HB, C_BI] = a["b_igate"][0]
    small[0:HB, C_BF] = a["b_fgate"][0]
    small[0:HB, C_M0] = a["state_mlstm_m"][0, 0]
    kc = a["cache_attn_k"][0, 0].transpose(1, 2, 0)
    vc = a["cache_attn_v"][0, 0].transpose(1, 2, 0)
    k_cache = np.concatenate([kc, kc], axis=1).transpose(1, 0, 2)
    c_state = np.concatenate([a["state_mlstm_C"][0, 0], a["state_mlstm_n"][0, 0][:, None, :]], axis=1).transpose(2, 0, 1)
    fcn = np.zeros((UT, P, 8), f)
    fcn[:, :, 0] = a["b_up"][0].reshape(UT, P)
    for j in range(3):
        fcn[:, :, 1 + j] = a["conv_w"][0, j].reshape(UT, P)
    fcn[:, :, 4] = a["conv_b"][0].reshape(UT, P)
    for j in range(2):
        fcn[:, :, 5 + j] = a["state_ffn_conv"][0, 0, j].reshape(UT, P)
    ffn_consts = fcn.reshape(2, FG, 2, P, 8).transpose(3, 1, 0, 2, 4).reshape(P, FG, 4, 8)

    slopes = (f(2.0) ** (f(-8.0) * np.arange(1, 17, dtype=f) / f(16))).astype(f)
    dist = np.abs(WIN + np.arange(CH)[:, None] - np.arange(BAND)[None, :]).astype(f)
    alibi = (-slopes.reshape(8, 2).transpose(1, 0)[:, None, :, None] * dist[None, :, None, :]).reshape(P, 8, BAND)
    rmask = np.ones((HB, T), f)
    rmask[:, 0:T:LC] = 0.0
    sel = np.zeros((HB, HB, P), f)
    for h in range(HB):
        sel[h, h, :] = 1.0
    cmask = np.where(np.arange(P)[:, None] <= np.arange(P)[None, :], f(0), f(-1e30)).astype(f)

    arrays = {
        "w_panels": w_panels, "w_ada": tiles(a["w_ada"][0]), "x": x.T.reshape(KT, P, T).transpose(1, 0, 2), "small": small,
        "ident": np.eye(P, dtype=f), "ones": np.full((P, P), 1.0 / D, f), "alibi": alibi, "k_cache": k_cache,
        "v_cache": vc.reshape(P, WIN), "rmask": rmask, "sel": sel, "cmask": cmask, "c_state": c_state, "ffn_consts": ffn_consts,
    }
    nc = bacc.Bacc("TRN2", target_bir_lowering=False, num_devices=1)
    io, feed = {}, {}
    for name, shape in IN_SHAPES.items():
        feed[f"in_{name}"] = np.ascontiguousarray(arrays[name].reshape(shape), dtype=f)
        io[name] = nc.dram_tensor(f"in_{name}", shape, F32, kind="ExternalInput").ap()
    for name, shape in OUT_SHAPES.items():
        io[name] = nc.dram_tensor(f"out_{name}", shape, F32, kind="ExternalOutput").ap()
    io["zs"] = nc.dram_tensor("z_spill", (N_SPILL, P, T), F32, kind="Internal").ap()
    io["hs"] = nc.dram_tensor("h_spill", (KT, P, T), F32, kind="Internal").ap()
    build(nc, io)
    r = run_bass_kernel_spmd(nc, [feed], core_ids=[0]).results[0]
    o = {name: np.asarray(r[f"out_{name}"]) for name in OUT_SHAPES}
    y = o["y"].transpose(1, 0, 2).reshape(D, T).T
    ko = o["k_out"].transpose(1, 3, 0, 2)
    vo = o["v_out"].transpose(1, 3, 0, 2)
    co = o["c_out"].transpose(0, 2, 3, 1)
    cso = o["cs_out"].reshape(P, FG, 2, 2, 4).transpose(4, 2, 1, 3, 0).reshape(4, UT * P)
    outs = []
    for s in range(2):
        outs.append((ko[s][None, None], vo[s][None, None], co[s, :, 0:DV][None, None], co[s, :, DV][None, None],
                     o["m_out"][s, :, 0][None, None], cso[2 * s:2 * s + 2][None, None]))
    c = np.ascontiguousarray
    return (c(y[0:TP][None]), c(y[TP:][None])) + tuple(c(t) for t in outs[0]) + tuple(c(t) for t in outs[1])
```

```python
from contextlib import ExitStack

import numpy as np
import concourse.bass as bass
from concourse import mybir

F32 = mybir.dt.float32
F32R = mybir.dt.float32r
ALU = mybir.AluOpType
ACT = mybir.ActivationFunctionType
AX = mybir.AxisListType

P = 128
D = 1024
KT = D // P
TP, TS = 1024, 32
T = TP + TS
NT = 3
NW = T // NT
CH = 64
NCH = TP // CH
BAND = 3 * CH
WIN = 128
HB, DV = 4, 256
LC = 128
NLC = TP // LC
UT = 5632 // P
FG = UT // 4
UW = T + 4
CW = UW - 2
ALPHA = 2.0 ** 0.25
EPS = 1e-5
KB_SCALE = 128.0 ** -0.5

P_ATT = 11
P_ML = P_ATT + NCH + 1
PPC = 3
P_PA = P_ML + 3 * KT
P_PB = P_PA + KT
P_OUT = P_PB + KT
P_FFN = P_OUT + KT
N_PANEL = P_FFN + 6 * FG
M_LN1 = P_FFN
M_FFN = M_LN1 + 1
M_LN2 = M_FFN + 12 * FG
N_SPILL = P_PA - P_ATT
Q_O, Q_GB, Q_GA = 17, 25, 33

C_BADA, C_L1W, C_L1B, C_L2W, C_L2B, C_NW, C_C, C_SINK, C_BI, C_BF, C_M0 = 0, 48, 56, 64, 72, 80, 88, 104, 112, 113, 114
N_SMALL = 116

LN2_DVE, LN2_POOL = (0, 1, 3, 4, 5, 7), (2, 6)
LN2_ORDER = (0, 1, 3, 2, 4, 5, 7, 6)


def ml_part(c):
    if isinstance(c, int) and c >= NLC - 2:
        return PPC * (NLC - 2) + 2 * (c - NLC + 2), (0, 3, 6, 9, 12)
    return c * PPC, ((6, 9, 12, 15, 18) if isinstance(c, int) and c == 0 else (0, 5, 9, 14, 18))


def wait(eng, sem, v):
    if isinstance(v, int) and v <= 0:
        return
    eng.wait_ge(sem, v)


def build(nc, io):
    ctx = ExitStack()
    with ctx:
        W0 = 16512
        RAW_B, WHL_B = 2 * 4096, 4 * 4096
        A_B = 2 * KT * T * 4
        C_B = KT * T * 4
        o_raw = W0
        o_whl = o_raw + RAW_B
        o_A = o_whl + WHL_B
        o_B = o_A + A_B
        o_C = o_B + A_B
        o_S = o_C + C_B
        o_M = o_S + 4 * UW * 4
        place = {"end": 0}

        def at(name, shape, off, dt=F32):
            n = int(np.prod(shape[1:])) * 4
            place["end"] = off + n
            return nc.alloc_sbuf_tensor_at(name, shape, dt, offset=off)

        def after(name, shape, dt=F32):
            return at(name, shape, (place["end"] + 31) // 32 * 32, dt)

        raw = at("w_raw", [P, 2, D], o_raw)
        whl = at("w_hilo", [P, 2, 2, D], o_whl, F32R)
        XA = at("x_hilo_a", [P, 2, KT, T], o_A, F32R)
        XB = at("x_hilo_b", [P, 2, KT, T], o_B, F32R)
        XC = at("x_c", [P, KT, T], o_C)
        ST = at("stage", [P, 4, UW], o_S)
        small = at("small", [P, N_SMALL], o_M)
        ident = after("ident", [P, P])
        ones = after("ones", [P, P])
        mod = after("mod", [P, 6, KT, 2])
        der = after("der", [P, 6, KT])
        lst = after("ln_stats", [P, 5, NLC + 1])
        assert place["end"] <= 229344
        ada = at("ada_ring", [P, KT, D], o_B)
        silu = after("silu", [P, 2, KT, 2])
        mrow = after("mod_row", [2, 2, D])
        kk = at("k_dup", [P, 2, TP + WIN + TS], o_B)
        vv = after("v_feat", [P, TP + WIN + TS])
        alibi = after("alibi", [P, 8, BAND])
        qs = after("q_stage", [P, 2, KT, P])
        ks = after("k_stage", [P, 2, 2, BAND])
        vs = after("v_stage", [P, 2, BAND])
        vt = after("v_tok", [P, 2, 2, P])
        pb = after("probs", [P, 2, 4, BAND])
        pta = after("probs_ta", [P, 4, P])
        ptb = after("probs_tb", [P, 4, P])
        nmx = after("neg_max", [P, 2, 4])
        esk = after("exp_sink", [P, 2, 4])
        rsum = after("row_sum", [P, 2, 4])
        rden = after("row_den", [P, 4])
        o_rows = o_C - 5 * T * 4
        assert place["end"] <= o_rows
        adaT = at("adaT_ring", [P, 4, D], o_B + 48128)
        assert place["end"] <= o_C
        sbc = at("silu_bc", [P, 2, D], o_S)
        ast = at("ada_sums", [P, 4, 2], o_B + 48128 + 4 * 4096)
        assert place["end"] <= o_C
        rowC, rowD, rowE, rowM, rowR = (at(n, [HB, T], o_rows + i * T * 4)
                                        for i, n in enumerate(("rowC", "rowD", "rowE", "rowM", "rowR")))
        zc = at("zc", [P, 2, 16, LC], o_B)
        cst = after("c_state", [P, 2, HB, DV + 1])
        sel = after("sel", [HB, HB, P])
        cmask = after("cmask", [P, P])
        mprow = after("mprow", [HB, NLC + 1])
        at_c = after("a_cols", [P, NLC + 1, HB])
        em_c = after("em_cols", [P, NLC + 1, HB])
        mp_c = after("mp_cols", [P, HB, NLC + 1])
        rs = after("r_bc", [P, LC])
        wd = after("w_dec", [P, LC])
        gb = after("g_bc", [P, LC])
        wks = after("wk_col", [P, 1])
        pt = after("p_t", [P, LC])
        qg = after("q_g", [P, LC])
        kw = after("k_w", [P, LC])
        va = after("v_aug", [P, DV + 1])
        hh = after("h_tok", [P, HB, DV])
        hn = at("hn_tok", [P, HB, DV], place["end"])
        dn = after("den", [P, 2])
        bst = after("bn_st", [P, HB, 6])
        mv = after("mean_var", [P, HB, 2])
        rstd = after("rstd", [P, HB])
        hT = after("hn_feat", [P, KT, LC])
        assert place["end"] <= o_rows, (place["end"], o_rows)
        rowI = ST[0:HB, 2, 0:T]
        rowF = ST[0:HB, 3, 0:T]
        fa = at("ffn_act", [P, 2, 2, 2, T], o_B, F32R)
        ub = after("u_rows", [P, 4, UW])
        fc = after("ffn_consts", [P, FG, 4, 8])
        cs = after("conv_out", [P, FG, 4, 4])
        fca = after("consts_act", [P, 4, 8])
        fcd = after("consts_dve", [P, 4, 8])
        lsum = after("ln_sums", [P, 2, T])
        assert place["end"] <= o_C

        acc = ctx.enter_context(nc.psum_tensor("acc", [P, NT, 512], F32))
        px = ctx.enter_context(nc.psum_tensor("px", [P, 5, 512], F32))

        def sem(name):
            return ctx.enter_context(nc.semaphore(name))

        raw_in = [sem("raw_in0"), sem("raw_in1")]
        raw_used, split_begun, w_hi, w_ready, w_start = sem("raw_used"), sem("split_begun"), sem("w_hi"), sem("w_ready"), sem("w_start")
        acc_ready = [sem(f"acc_ready{n}") for n in range(NT)]
        acc_free = [sem(f"acc_free{n}") for n in range(NT)]
        c_in, x_in = sem("c_in"), [sem(f"x_in{i}") for i in range(2)]
        ada_in = [sem(f"ada_in{i}") for i in range(KT)]
        adaT_in = [sem(f"adaT_in{i}") for i in range(4)]
        cb_in, ada_used, ada_ev, ada_row, ada_col, adaT_used = (sem(n) for n in ("cb_in", "ada_used", "ada_ev", "ada_row", "ada_col", "adaT_used"))
        sl_e, sl_d = sem("sl_e"), sem("sl_d")
        h_tmp, h_hi, h_lo = sem("h_tmp"), sem("h_hi"), sem("h_lo")
        qkv_ev, kv_in, kv_out = sem("qkv_ev"), sem("kv_in"), sem("kv_out")
        st_rdy, s_rdy, s_used, mx_rdy, ex_rdy, pn_rdy = (sem(n) for n in ("st_rdy", "s_rdy", "s_used", "mx_rdy", "ex_rdy", "pn_rdy"))
        tr_rdy, pt_rdy, pv_rdy, o_used, v_tok = (sem(n) for n in ("tr_rdy", "pt_rdy", "pv_rdy", "o_used", "v_tok_rdy"))
        sp_cp = sem("sp_cp")
        sp_out = [sem("sp_out0"), sem("sp_out1")]
        ml_in, g_in, row_d, row_a, row_p, row_v = (sem(n) for n in ("ml_in", "g_in", "row_d", "row_a", "row_p", "row_v"))
        zc_in = [sem("zc_in0"), sem("zc_in1")]
        sr_rdy, kvt_rdy, d_rdy, wg_rdy, kv_rdy, p_rdy, nu_rdy, e_done, var_rdy, sd_rdy, hn_rdy, ht_rdy, ht_cp = (
            sem(n) for n in ("sr_rdy", "kvt_rdy", "d_rdy", "wg_rdy", "kv_rdy", "p_rdy", "nu_rdy", "e_done", "var_rdy", "sd_rdy",
                             "hn_rdy", "ht_rdy", "ht_cp"))
        hs_out, st_out = sem("hs_out"), sem("st_out")
        ya_hi, ya_lo = sem("ya_hi"), sem("ya_lo")
        og_in, hn_in, sg_rdy, yb_rdy, yb_hi, yb_lo = (sem(n) for n in ("og_in", "hn_in", "sg_rdy", "yb_rdy", "yb_hi", "yb_lo"))
        gt_in = [sem("gt_in0"), sem("gt_in1")]
        gt_rdy, gt_used, mg_rdy, mg_hi, mg_lo = (sem(n) for n in ("gt_rdy", "gt_used", "mg_rdy", "mg_hi", "mg_lo"))
        xr_in = [sem("xr_in0"), sem("xr_in1")]
        ln_s1, s1_add, sq_used, r_rdy, ln_sq, ln_squ, ln_v, ln_s, ln_dg, ln_r, ln_t, ln_bc, ln_p, ln_m = (sem(n) for n in ("ln_s1", "s1_add", "sq_used", "r_rdy", "ln_sq", "ln_squ", "ln_v", "ln_s", "ln_dg", "ln_r", "ln_t", "ln_bc", "ln_p", "ln_m"))
        h2_hi, h2_lo, fc_in = (sem(n) for n in ("h2_hi", "h2_lo", "fc_in"))
        u_rdy, cv_a, cv_d, gl_rdy, pr_rdy, fa_hi, fa_lo = (sem(n) for n in ("u_rdy", "cv_a", "cv_d", "gl_rdy", "pr_rdy", "fa_hi", "fa_lo"))
        y_rdy, y_out, cs_out = sem("y_rdy"), sem("y_out"), sem("cs_out")
        block = ctx.enter_context(nc.Block())

        def hslot(q):
            return ST[:, (q % 12) // 3, (q % 3) * NW:(q % 3 + 1) * NW]

        adaT_tmp = at("adaT_tmp", [P, 2, D], o_S + 8192)[:, :, :]

        def pieces(n):
            a, b = n * NW, (n + 1) * NW
            return [(a, b, 0)] if b <= TP else [(a, TP, 0), (TP, b, 1)]

        @block.sync
        def _(sp):
            for i in range(2):
                for m in range(KT):
                    wait(sp, ada_used, (i - 1) * KT + m + 1)
                    sp.dma_start(ada[:, m, :], io["w_ada"][i * KT + m]).then_inc(ada_in[m], 16)

            def panel_pair(i):
                for s in range(2):
                    wait(sp, raw_used, 2 * i + s - 1)
                    sp.dma_start(raw[:, s, :], io["w_panels"][bass.ds(i * 2 + s, 1), :, :].rearrange("o p n -> p (o n)"))\
                      .then_inc(raw_in[s], 16)

            panel_pair(0)
            with sp.Fori(1, N_PANEL // 2) as i:
                panel_pair(i)

        @block.gpsimd
        def _(pool):
            def split_pair(i, both=False):
                for s in range(2):
                    pool.wait_ge(raw_in[s], (i + 1) * 16)
                    if both:
                        pool.wait_ge(ln_squ, 1)
                    elif not isinstance(i, int):
                        pool.wait_ge(w_start, i * 2 + s)
                    pool.sem_inc(split_begun, 1)
                    nc.gpsimd.tensor_copy(whl[:, s, 0, :], raw[:, s, :]).then_inc(w_hi, 1)
                    pool.wait_ge(w_hi, i * 2 + s + 1)
                    nc.gpsimd.tensor_tensor(whl[:, s, 1, :], raw[:, s, :], whl[:, s, 0, :].bitcast(F32), ALU.subtract)\
                      .then_inc(w_ready, 1)
                    pool.wait_ge(w_ready, i * 2 + s + 1)
                    pool.sem_inc(raw_used, 1)

            split_pair(0)
            with pool.Fori(1, P_FFN // 2) as i:
                split_pair(i)
            split_pair(P_FFN // 2, both=True)
            for q in range(NT * KT):
                n, k = divmod(q, KT)
                cols = slice(n * NW, (n + 1) * NW)
                pool.wait_ge(h2_hi, q + 1)
                nc.gpsimd.tensor_tensor(XA[:, 1, k, cols], hslot(q), XA[:, 0, k, cols].bitcast(F32), ALU.subtract).then_inc(h2_lo, 1)
            with pool.Fori(P_FFN // 2 + 1, N_PANEL // 2) as i:
                split_pair(i)
            for k in range(1, KT - 1):
                pool.wait_ge(r_rdy, KT + k + 1)
                wait(pool, s1_add, k - 1)
                nc.gpsimd.tensor_tensor(lsum[:, 0, :], XC[:, 0, :] if k == 1 else lsum[:, 0, :], XC[:, k, :], ALU.add)\
                  .then_inc(s1_add if k < KT - 2 else ln_s1, 1)
            pool.wait_ge(ln_bc, 2)
            for i, k in enumerate(LN2_POOL):
                nc.gpsimd.tensor_tensor(XC[:, k, :], XC[:, k, :], lsum[:, 0, :], ALU.mult).then_inc(ln_m, 1)
                pool.wait_ge(ln_m, i + 1)
                nc.gpsimd.tensor_tensor(XC[:, k, :], XC[:, k, :], lsum[:, 1, :], ALU.add).then_inc(ln_p, 1)

        @block.tensor
        def _(pe):
            mm = nc.tensor.matmul

            def gemm_half(p, slot, n, half, rhs):
                if n == 0 and half == 0:
                    pe.wait_ge(w_ready, p + 1)
                if half == 0:
                    wait(pe, acc_free[n], p)
                for k in range(half * KT // 2, (half + 1) * KT // 2):
                    for j, (wi, xi) in enumerate(((0, 0), (0, 1), (1, 0))):
                        last = mm(acc[:, n, 0:NW], whl[:, slot, wi, k * P:(k + 1) * P], rhs[:, xi, k, n * NW:(n + 1) * NW],
                                  start=(k == 0 and j == 0), stop=(k == KT - 1 and j == 2))
                        if n == 0 and k == 0 and j == 0:
                            last.then_inc(w_start, 1)
                if half == 1:
                    last.then_inc(acc_ready[n], 1)

            def gemm(p, slot, n, rhs):
                for half in range(2):
                    gemm_half(p, slot, n, half, rhs)

            pe.wait_ge(sl_d, 1)
            for i in range(2):
                for m in range(KT):
                    pe.wait_ge(ada_in[m], (i + 1) * 16)
                    for k in range(KT):
                        last = mm(px[0:2, 2 * i + m // 4, (m % 4) * P:(m % 4 + 1) * P], silu[:, 1, k, :], ada[:, m, k * P:(k + 1) * P],
                                  start=(k == 0), stop=(k == KT - 1))
                    last.then_inc(ada_used, 1)
            for i in range(2):
                pe.wait_ge(ada_row, i + 1)
                for m in range(KT):
                    last = nc.tensor.transpose(px[:, 4, 16 * i + 2 * m:16 * i + 2 * m + 2], mrow[:, i, m * P:(m + 1) * P], ident[0:2, 0:2])
            last.then_inc(ada_col, 1)

            for p in range(2):
                for n in range(NT):
                    if p == 0:
                        pe.wait_ge(h_lo, KT * (n + 1))
                    gemm(p, p, n, XA)
            with pe.Fori(1, KT // 2) as i:
                for s in range(2):
                    for n in range(NT):
                        gemm(i * 2 + s, s, n, XA)
            for p in range(KT, P_ATT):
                for n in range(NT):
                    gemm(p, p % 2, n, XA)

            def att_scores(c, a, par, g, w, kb):
                if g == 0:
                    pe.wait_ge(st_rdy, c + 1)
                wait(pe, s_used, a)
                if g == 0:
                    if w > kb:
                        nc.tensor.transpose(px[0:w - kb, 0, 384:512], vs[:, par, 0:w - kb], ident[:, :])
                    nc.tensor.transpose(px[0:kb, 1, 384:512], vs[:, par, w - kb:w], ident[:, :])
                for j in range(4):
                    last = mm(px[:, j // 2, (j % 2) * BAND:(j % 2) * BAND + w], qs[:, par, 4 * g + j, :], ks[:, par, g, 0:w],
                              start=True, stop=True, skip_group_check=True)
                last.then_inc(s_rdy, 1)

            def att_transpose(a, g, w, kb):
                pe.wait_ge(pn_rdy, a + 1)
                wait(pe, pt_rdy, a)
                for j in range(4):
                    if w > kb:
                        nc.tensor.transpose(px[0:w - kb, 2, j * P:(j + 1) * P], pb[:, g, j, 0:w - kb], ident[:, :])
                    last = nc.tensor.transpose(px[0:kb, 3, j * P:(j + 1) * P], pb[:, g, j, w - kb:w], ident[:, :])
                last.then_inc(tr_rdy, 1)

            def att_values(a, par, g, w, kb):
                pe.wait_ge(pt_rdy, a + 1)
                wait(pe, o_used, a)
                for e in range(2):
                    out = px[64 * e:64 * e + 64, 4, 0:4 * CH]
                    if w > kb:
                        mm(out, vt[0:w - kb, par, 0, g * 64:g * 64 + 64], pta[0:w - kb, :, 64 * e:64 * e + 64],
                           start=True, stop=False)
                    last = mm(out, vt[0:kb, par, 1, g * 64:g * 64 + 64], ptb[0:kb, :, 64 * e:64 * e + 64],
                              start=(w == kb), stop=True)
                last.then_inc(pv_rdy, 1)

            def att_chunk(c, par, w, kb, wp, kbp):
                slot = (P_ATT + par) % 2
                first = isinstance(c, int) and c == 0
                for g in range(2):
                    if first and g == 0:
                        for half in range(2):
                            gemm_half(P_ATT, slot, 0, half, XA)
                        att_scores(0, 0, 0, 0, w, kb)
                        gemm_half(P_ATT, slot, 1, 0, XA)
                        continue
                    before = (c * 2 - 1, 1 - par, 1, wp, kbp) if g == 0 else (c * 2, par, 0, w, kb)
                    att_scores(c, c * 2 + g, par, g, w, kb)
                    gemm_half(c + P_ATT, slot, *divmod(3 * g, 2), XA)
                    att_transpose(before[0], before[2], before[3], before[4])
                    gemm_half(c + P_ATT, slot, *divmod(3 * g + 1, 2), XA)
                    att_values(*before)
                    gemm_half(c + P_ATT, slot, *divmod(3 * g + 2, 2), XA)

            att_chunk(0, 0, CH, CH, 0, 0)
            att_chunk(1, 1, 2 * CH, CH, CH, CH)
            att_chunk(2, 0, BAND, CH, 2 * CH, CH)
            att_chunk(3, 1, BAND, CH, BAND, CH)
            with pe.Fori(2, NCH // 2) as i:
                att_chunk(i * 2, 0, BAND, CH, BAND, CH)
                att_chunk(i * 2 + 1, 1, BAND, CH, BAND, CH)
            att_chunk(NCH, 0, WIN + TS, TS, BAND, CH)
            att_transpose(2 * NCH + 1, 1, WIN + TS, TS)
            att_values(2 * NCH + 1, 0, 1, WIN + TS, TS)

            for n in range(NT):
                gemm(P_ML, P_ML % 2, n, XA)
            pe.wait_ge(row_d, 2)
            pe.wait_ge(ml_in, 16 * 3)
            for c in range(NLC + 1):
                L = LC if c < NLC else TS
                nc.tensor.transpose(px[0:L, 0, 4 * c:4 * c + 4], rowC[:, c * LC:c * LC + L], ident[0:HB, 0:HB])
                nc.tensor.transpose(px[0:L, 0, 64 + 4 * c:68 + 4 * c], rowM[:, c * LC:c * LC + L], ident[0:HB, 0:HB])
            for h in range(HB):
                last = mm(px[:, 0, 128 + 9 * h:137 + 9 * h], sel[:, h, :], mprow[:, :], start=True, stop=True)
            last.then_inc(row_p, 1)

            def ml_unit(c, r, par, h, L):
                u = c * 4 + h
                z = zc[:, par, :, :]
                smp = isinstance(c, int) and c == NLC
                q0, cuts = ml_part(c)
                part = list(range(cuts[h], cuts[h + 1]))

                def share(n):
                    for i in part[:n]:
                        b = i // 6
                        slot = (P_ML + b + (q0 if isinstance(c, int) else par)) % 2
                        gemm_half(q0 + (P_ML + b), slot, *divmod(i % 6, 2), XA)
                    del part[:n]

                if h == 0:
                    pe.wait_ge(zc_in[par], (r + 1) * 16)
                if isinstance(c, int) and c == 0 and h == 0:
                    pe.wait_ge(row_v, 2)
                wait(pe, p_rdy, u)
                mm(px[0:L, 0, 0:L], z[:, h, 0:L], z[:, 4 + h, 0:L], start=True, stop=True)
                tok = slice(c * LC, c * LC + L) if isinstance(c, int) else bass.ds(c * LC, L)
                mm(px[:, 0, P:P + L], sel[:, h, :], rowR[:, tok], start=True, stop=True).then_inc(sr_rdy, 1)
                wait(pe, kv_rdy, u)
                nc.tensor.transpose(px[0:L, 1, 0:P], z[:, h, 0:L], ident[:, :])
                nc.tensor.transpose(px[0:L, 1, P:2 * P], z[:, 8 + 2 * h, 0:L], ident[:, :])
                nc.tensor.transpose(px[0:L, 1, 2 * P:3 * P], z[:, 9 + 2 * h, 0:L], ident[:, :]).then_inc(kvt_rdy, 1)
                share(2)
                pe.wait_ge(kv_rdy, u + 1)
                pe.wait_ge(p_rdy, u + 1)
                wait(pe, e_done, u)
                st = cst[:, 1 if smp else 0, h, :]
                mm(px[0:L, 2, 0:DV + 1], pt[0:L, 0:L], va[0:L, :], start=True, stop=False)
                mm(px[0:L, 2, 0:DV + 1], qg[:, 0:L], st, start=False, stop=True)
                mm(px[:, 3, 0:DV + 1], kw[0:L, :], va[0:L, :], start=True, stop=True).then_inc(nu_rdy, 1)
                share(1)
                if not (isinstance(c, int) and c == 0) and h in (1, 2):
                    ml_turn(c - 1, h - 1, LC)
                share(2)

            def ml_turn(c, b, L):
                if b == 0:
                    pe.wait_ge(hn_rdy, c + 1)
                wait(pe, ht_cp, c * 2 + b)
                for j in range(4):
                    last = nc.tensor.transpose(px[:, 4, j * P:j * P + L], hn[0:L, 2 * b + j // 2, (j % 2) * P:(j % 2) * P + P],
                                               ident[0:L, 0:L])
                last.then_inc(ht_rdy, 1)

            for c in range(2):
                for h in range(HB):
                    ml_unit(c, 0, c, h, LC)
            with pe.Fori(1, NLC // 2 - 1) as i:
                for par in range(2):
                    for h in range(HB):
                        ml_unit(i * 2 + par, i, par, h, LC)
            for c in range(NLC - 2, NLC):
                for h in range(HB):
                    ml_unit(c, NLC // 2 - 1, c % 2, h, LC)
            for h in range(HB):
                ml_unit(NLC, NLC // 2, 0, h, TS)

            def panels8(p0, rhs, first=0):
                with pe.Fori(first, KT // 2) as i:
                    for s in range(2):
                        for n in range(NT):
                            gemm(i * 2 + (p0 + s), (p0 + s) % 2, n, rhs)

            for n in range(NT):
                pe.wait_ge(ya_lo, KT * (n + 1))
                gemm(P_PA, P_PA % 2, n, XA)
            for b in range(2):
                ml_turn(NLC, b, TS)
            for n in range(NT):
                gemm(P_PA + 1, (P_PA + 1) % 2, n, XA)
            panels8(P_PA, XA, 1)
            pe.wait_ge(yb_lo, KT)
            panels8(P_PB, XB)

            def ln_sum(ln):
                k = KT - 1
                for tail, src, ready, counts in ((0, (lsum[:, 0, :], lsum[:, 1, :]), (ln_s1, sq_used), (ln + 1, (KT - 2) * (ln + 1))),
                                                (1, (XC[:, k, :], ST[:, k % 2, 0:T]), (r_rdy, ln_sq), (KT * (ln + 1), KT * (ln + 1)))):
                    for q in range(2):
                        pe.wait_ge(ready[q], counts[q])
                        for c in range(NLC + 1):
                            L = LC if c < NLC else TS
                            last = mm(px[0:L, 3 + q, c:c + 1], src[q][:, c * LC:c * LC + L], ones[:, 0:1],
                                      start=(tail == 0 and c == 0), stop=(tail == 1), skip_group_check=True)
                last.then_inc(ln_squ, 1)

            def ln_spread(M, ln):
                pe.wait_ge(ln_dg, ln + 1)
                for n in range(NT):
                    mm(px[:, n, 0:NW], ones[:, :], ST[:, 0, n * NW:(n + 1) * NW], start=True, stop=True).then_inc(ln_r, 1)
                    pe.wait_ge(acc_free[n], M)
                    mm(acc[:, n, 0:NW], ones[:, :], ST[:, 1, n * NW:(n + 1) * NW], start=True, stop=True).then_inc(acc_ready[n], 1)

            pe.wait_ge(mg_lo, KT)
            for m in range(KT):
                for n in range(NT):
                    gemm(P_OUT + m, (P_OUT + m) % 2, n, XA)
            ln_sum(0)
            ln_spread(M_LN1, 0)

            def up(pi, M, i, first=False):
                pe.wait_ge(w_ready, pi + 1)
                for n in range(NT):
                    if first:
                        pe.wait_ge(h2_lo, KT * (n + 1))
                    pe.wait_ge(acc_free[n], M)
                    for k in range(KT):
                        for j, (wi, xi) in enumerate(((0, 0), (0, 1), (1, 0))):
                            last = mm(acc[:, n, 0:NW], whl[:, i % 2, wi, k * P:(k + 1) * P], XA[:, xi, k, n * NW:(n + 1) * NW],
                                      start=(k == 0 and j == 0), stop=(k == KT - 1 and j == 2))
                            if n == 0 and k == 0 and j == 0:
                                last.then_inc(w_start, 1)
                    last.then_inc(acc_ready[n], 1)

            def down(pi, M, par, j):
                pe.wait_ge(fa_lo, j * 2 + 2)
                for m in range(KT):
                    s = m // 4
                    if m % 4 == 0:
                        pe.wait_ge(w_ready, pi + s + 1)
                    for n in range(NT):
                        pe.wait_ge(acc_free[n], M + m)
                        for k in range(2):
                            col = ((m % 4) * 2 + k) * P
                            for q, (wi, xi) in enumerate(((0, 0), (0, 1), (1, 0))):
                                last = mm(acc[:, n, 0:NW], whl[:, s, wi, col:col + P], fa[:, par, xi, k, n * NW:(n + 1) * NW],
                                          start=(k == 0 and q == 0), stop=(k == 1 and q == 2))
                                if m % 4 == 0 and n == 0 and k == 0 and q == 0:
                                    last.then_inc(w_start, 1)
                        last.then_inc(acc_ready[n], 1)

            for i in range(4):
                up(P_FFN + i, M_FFN + i, i, first=(i == 0))

            def ffn_iter(j, par):
                for i in range(4):
                    up(j * 6 + (P_FFN - 2 + i), j * 12 + (M_FFN - 8 + i), i)
                down(j * 6 + (P_FFN + 2), j * 12 + (M_FFN - 4), 1 - par, j - 1)

            with pe.Fori(0, (FG - 1) // 2) as i:
                ffn_iter(i * 2 + 1, 1)
                ffn_iter(i * 2 + 2, 0)
            down(P_FFN + 6 * FG - 2, M_FFN + 12 * FG - 8, 0, FG - 1)
            ln_sum(1)
            ln_spread(M_LN2, 1)

        @block.scalar
        def _(act):
            A = nc.scalar.activation
            act.dma_start(small[:, :], io["small"]).then_inc(c_in, 16)
            act.dma_start(ident[:, :], io["ident"]).then_inc(c_in, 16)
            act.dma_start(ones[:, :], io["ones"]).then_inc(c_in, 16)
            for i in range(2):
                act.dma_start(XC[:, 4 * i:4 * i + 4, :], io["x"][:, 4 * i:4 * i + 4, :]).then_inc(x_in[i], 16)
            act.wait_ge(c_in, 48)
            A(silu[:, 0, :, :], small[:, C_C:C_C + 16].rearrange("p (k s) -> p k s", s=2), ACT.Sigmoid).then_inc(sl_e, 1)
            for i in range(2):
                act.wait_ge(ada_used, KT * (i + 1))
                A(mrow[:, i, :], px[0:2, 2 * i:2 * i + 2, :].rearrange("p b c -> p (b c)"), ACT.Copy).then_inc(ada_row, 1)
            for n in range(NT):
                for k in range(KT):
                    act.wait_ge(h_tmp, n * KT + k + 1)
                    A(XA[:, 0, k, n * NW:(n + 1) * NW], hslot(n * KT + k), ACT.Copy).then_inc(h_hi, 1)
            act.wait_ge(h_lo, NT * KT)
            act.dma_start(sbc[:, :, :], io["c_bc"]).then_inc(cb_in, 16)

            act.wait_ge(ada_ev, 1)
            act.dma_start(alibi[:, :, :], io["alibi"]).then_inc(kv_in, 16)
            act.dma_start(kk[:, :, TP:TP + WIN], io["k_cache"]).then_inc(kv_in, 16)
            act.dma_start(vv[:, TP:TP + WIN], io["v_cache"]).then_inc(kv_in, 16)

            def take(M, n, dsts, func=ACT.Copy, **kw):
                act.wait_ge(acc_ready[n], M + 1)
                for dst, a, b in dsts:
                    last = A(dst, acc[:, n, a:b], func, **kw)
                last.then_inc(acc_free[n], 1)
                return last

            def q_evac(m):
                for n in range(NT):
                    dst = XC[:, m, n * NW:(n + 1) * NW] if isinstance(m, int) else \
                        XC[:, bass.ds(m, 1), n * NW:(n + 1) * NW].rearrange("p o w -> p (o w)")
                    take(m, n, [(dst, 0, NW)])

            def adaT_load(m, i):
                wait(act, adaT_used, m * 4 + i - 3)
                act.dma_start(adaT[:, i, :], io["w_adaT"][bass.ds(m * 4 + i, 1), :, :].rearrange("o p n -> p (o n)"))\
                   .then_inc(adaT_in[i], 16)

            for i in range(4):
                adaT_load(0, i)
            act.wait_ge(cb_in, 16)
            A(adaT_tmp, sbc[:, :, :], ACT.Sigmoid).then_inc(sl_e, 1)
            q_evac(0)
            with act.Fori(1, KT) as m:
                for i in range(4):
                    adaT_load(m, i)
                q_evac(m)
            for p in range(KT, P_ATT):
                row = vv[:, :] if p == P_ATT - 1 else kk[:, p - KT, :]
                for n in range(NT):
                    dst = []
                    for a, b, s in pieces(n):
                        o = WIN * s
                        dst.append((row[:, a + o:b + o], a - n * NW, b - n * NW))
                    take(p, n, dst)
            act.drain().then_inc(qkv_ev, 1)

            def att_stage(c, par, w):
                smp = isinstance(c, int) and c == NCH
                qn = TS if smp else CH
                lo = TP if smp else None
                if isinstance(c, int):
                    qsl = slice(c * CH, c * CH + qn)
                    lo = TP if smp else (c + 1) * CH - w
                    bsl = slice(lo, lo + w)
                else:
                    qsl = bass.ds(c * CH, qn)
                    bsl = bass.ds(c * CH + (CH - w), w)
                wait(act, s_rdy, c * 2 - 2)
                for e in range(2):
                    A(qs[64 * e:64 * e + 64, par, :, 64 * e:64 * e + qn], XC[64 * e:64 * e + 64, :, qsl], ACT.Copy, scale=0.125)
                A(ks[:, par, :, 0:w], kk[:, :, bsl], ACT.Copy)
                A(vs[:, par, 0:w], vv[:, bsl], ACT.Copy).then_inc(st_rdy, 1)

            def att_exp(a, g, w):
                act.wait_ge(mx_rdy, a + 1)
                for j in range(4):
                    A(pb[:, g, j, 0:w], pb[:, g, j, 0:w], ACT.Exp, bias=nmx[:, g, j:j + 1], accum_out=rsum[:, g, j:j + 1])
                A(esk[:, g, :], esk[:, g, :], ACT.Exp).then_inc(ex_rdy, 1)

            def att_ptake(a, w, kb):
                act.wait_ge(tr_rdy, a + 1)
                wait(act, pv_rdy, a)
                if w > kb:
                    A(pta[0:w - kb, :, :], px[0:w - kb, 2, :].rearrange("p (j q) -> p j q", j=4), ACT.Copy)
                A(ptb[0:kb, :, :], px[0:kb, 3, :].rearrange("p (j q) -> p j q", j=4), ACT.Copy).then_inc(pt_rdy, 1)

            def spill_take(M, n, slot):
                act.wait_ge(acc_ready[n], M + 1)
                A(ST[:, slot, n * NW:(n + 1) * NW], acc[:, n, 0:NW], ACT.Copy).then_inc(acc_free[n], 1)

            def spill_free(slot, rounds):
                wait(act, sp_out[slot], rounds * 16)

            def spill_store(q, slot):
                act.drain().then_inc(sp_cp, 1)
                act.wait_ge(sp_cp, q + 1)
                act.dma_start(io["zs"][bass.ds(q, 1), :, :].rearrange("o p n -> p (o n)"), ST[:, slot, 0:T]).then_inc(sp_out[slot], 16)

            def att_chunk(c, r, par, w, wp, kbp, wn):
                kb = TS if isinstance(c, int) and c == NCH else CH
                if wp:
                    att_ptake(c * 2 - 1, wp, kbp)
                att_exp(c * 2, 0, w)
                spill_free(par, r)
                spill_take(c + P_ATT, 0, par)
                if wn:
                    att_stage(c + 1, 1 - par, wn)
                att_ptake(c * 2, w, kb)
                att_exp(c * 2 + 1, 1, w)
                spill_take(c + P_ATT, 1, par)
                spill_take(c + P_ATT, 2, par)
                spill_store(c, par)

            act.wait_ge(ada_ev, 2)
            att_stage(0, 0, CH)
            act.wait_ge(qkv_ev, 1)
            act.wait_ge(kv_in, 48)
            for j in range(2):
                for s, a in ((0, TP - WIN), (1, TP + TS)):
                    act.dma_start(io["k_out"][j, s], kk[0:64, j, a:a + WIN]).then_inc(kv_out, 16)
                    act.dma_start(io["v_out"][j, s], vv[64 * j:64 * j + 64, a:a + WIN]).then_inc(kv_out, 16)
            att_chunk(0, 0, 0, CH, 0, 0, 2 * CH)
            att_chunk(1, 0, 1, 2 * CH, CH, CH, BAND)
            act.wait_ge(sp_out[0], 16)
            act.dma_start(rowI, io["zs"][0, 0:HB, :]).then_inc(g_in, 16)
            act.dma_start(rowF, io["zs"][0, HB:2 * HB, :]).then_inc(g_in, 16)
            act.dma_start(rowE[:, :], io["rmask"]).then_inc(g_in, 16)
            att_chunk(2, 1, 0, BAND, 2 * CH, CH, BAND)
            act.wait_ge(g_in, 48)
            A(rowC[:, :], rowF, ACT.Abs, bias=small[0:HB, C_BF:C_BF + 1])
            act.drain()
            A(rowC[:, :], rowC[:, :], ACT.Exp, scale=-1.0).then_inc(row_a, 1)
            att_chunk(3, 1, 1, BAND, BAND, CH, BAND)
            act.wait_ge(row_d, 1)
            A(rowD[:, :], rowD[:, :], ACT.Ln).then_inc(row_a, 1)
            with act.Fori(2, NCH // 2 - 1) as i:
                att_chunk(i * 2, i, 0, BAND, BAND, CH, BAND)
                att_chunk(i * 2 + 1, i, 1, BAND, BAND, CH, BAND)
            att_chunk(NCH - 2, NCH // 2 - 1, 0, BAND, BAND, CH, BAND)
            att_chunk(NCH - 1, NCH // 2 - 1, 1, BAND, BAND, CH, WIN + TS)
            att_chunk(NCH, NCH // 2, 0, WIN + TS, BAND, CH, 0)
            att_ptake(2 * NCH + 1, WIN + TS, TS)

            act.wait_ge(o_used, 2 * NCH + 2)
            act.wait_ge(sp_out[0], 16 * 9)
            act.wait_ge(sp_out[1], 16 * 8)
            act.wait_ge(kv_out, 16 * 8)
            act.dma_start(sel[:, :, :], io["sel"]).then_inc(ml_in, 16)
            act.dma_start(cmask[:, :], io["cmask"]).then_inc(ml_in, 16)
            act.dma_start(cst[:, 1, :, :], io["c_state"]).then_inc(ml_in, 16)

            def load_chunk(c, par, L):
                tok = slice(c * LC, c * LC + L) if isinstance(c, int) else bass.ds(c * LC, L)
                act.dma_start(zc[:, par, :, 0:L], io["zs"][1:17, :, tok].rearrange("q p t -> p q t")).then_inc(zc_in[par], 16)

            def ml_spill(c, r, par, b, n):
                q0 = ml_part(c)[0]
                if isinstance(c, int):
                    slot = (Q_O + q0 + b) % 2
                    earlier = (Q_O + q0 + b) // 2
                else:
                    slot = (Q_O + par + b) % 2
                    earlier = r * PPC + (Q_O + PPC * par + b) // 2
                if n == 0:
                    spill_free(slot, earlier)
                spill_take(q0 + (P_ML + b), n, slot)
                if n == NT - 1:
                    spill_store(q0 + (Q_O + b), slot)

            load_chunk(0, 0, LC)
            for n in range(NT):
                ml_spill(0, 0, 0, 0, n)
            act.wait_ge(row_v, 1)
            for c in range(NLC + 1):
                L = LC if c < NLC else TS
                A(em_c[0:L, c, :], em_c[0:L, c, :], ACT.Exp, scale=-1.0)
            act.drain().then_inc(row_v, 1)

            def ml_unit(c, r, par, h, L):
                u = c * 4 + h
                smp = isinstance(c, int) and c == NLC
                first = isinstance(c, int) and c == 0
                act.wait_ge(d_rdy, u + 1)
                A(wd[0:L, 0:L], wd[0:L, 0:L], ACT.Exp)
                bias = mp_c[:, h, c:c + 1] if isinstance(c, int) else mp_c[:, h, bass.ds(c, 1)]
                A(gb[:, 0:L], rs[:, 0:L], ACT.Exp, bias=bias).then_inc(wg_rdy, 1)
                act.wait_ge(wg_rdy, u + 1)
                A(wks[0:L, :], wd[0:L, L - 1:L], ACT.Copy, scale=KB_SCALE)
                act.wait_ge(kvt_rdy, u + 1)
                wait(act, nu_rdy, u)
                A(va[0:L, 0:DV], px[0:L, 1, P:3 * P], ACT.Copy)
                act.drain()
                A(kw[0:L, :], px[0:L, 1, 0:P], ACT.Copy, scale=wks[0:L, :]).then_inc(kv_rdy, 1)
                if h in (1, 2) and not first:
                    ml_turn(c - 1, h - 1, LC)
                if h == 1 and not smp:
                    wait(act, nu_rdy, c * 4)
                    load_chunk(c + 1, 1 - par, TS if isinstance(c, int) and c == NLC - 1 else LC)
                if h == 3:
                    act.wait_ge(var_rdy, c + 1)
                    A(rstd[0:L, :], rstd[0:L, :], ACT.Sqrt).then_inc(sd_rdy, 1)
                q0, cuts = ml_part(c)
                for i in range(cuts[h], cuts[h + 1]):
                    if i % 2:
                        ml_spill(c, r, par, i // 6, (i % 6) // 2)

            def ml_turn(c, b, L):
                act.wait_ge(ht_rdy, c * 2 + b + 1)
                if b == 0:
                    wait(act, hs_out, c * 16)
                A(hT[:, 4 * b:4 * b + 4, 0:L], px[:, 4, :].rearrange("p (j q) -> p j q", j=4)[:, :, 0:L], ACT.Copy).then_inc(ht_cp, 1)
                if b == 1:
                    act.wait_ge(ht_cp, c * 2 + 2)
                    tok = slice(c * LC, c * LC + L) if isinstance(c, int) else bass.ds(c * LC, L)
                    act.dma_start(io["hs"][:, :, tok].rearrange("j p t -> p j t"), hT[:, :, 0:L]).then_inc(hs_out, 16)

            act.wait_ge(row_v, 3)
            for c in range(2):
                for h in range(HB):
                    ml_unit(c, 0, c, h, LC)
            with act.Fori(1, NLC // 2 - 1) as i:
                for par in range(2):
                    for h in range(HB):
                        ml_unit(i * 2 + par, i, par, h, LC)
            for c in range(NLC - 2, NLC):
                for h in range(HB):
                    ml_unit(c, NLC // 2 - 1, c % 2, h, LC)
            for h in range(HB):
                ml_unit(NLC, NLC // 2, 0, h, TS)
            for n in range(NT):
                act.wait_ge(acc_ready[n], P_PA)
                for k in range(KT):
                    A(XA[:, 0, k, n * NW:(n + 1) * NW], XC[:, k, n * NW:(n + 1) * NW], ACT.Copy).then_inc(ya_hi, 1)
            for b in range(2):
                ml_turn(NLC, b, TS)
            act.wait_ge(e_done, 4 * NLC + 4)
            act.dma_start(io["c_out"].rearrange("s p h v -> p s h v"), cst[:, :, :, :]).then_inc(st_out, 16)
            act.dma_start(io["m_out"][0], rowM[:, TP - 1:TP]).then_inc(st_out, 16)
            act.dma_start(io["m_out"][1], rowM[:, T - 1:T]).then_inc(st_out, 16)

            act.wait_ge(sp_out[0], 16 * ((N_SPILL + 1) // 2))
            act.wait_ge(sp_out[1], 16 * (N_SPILL // 2))
            act.wait_ge(hs_out, 16 * (NLC + 1))
            act.wait_ge(st_out, 48)

            def load_gate(q0, m, s, used):
                wait(act, gt_used, used)
                act.dma_start(ST[:, 2 + s, 0:T], io["zs"][q0 + m]).then_inc(gt_in[s], 16)

            for m in range(2):
                load_gate(Q_GA, m, m, 0)
            for m in range(KT):
                wait(act, yb_lo, m)
                act.dma_start(ST[:, 0, 0:T], io["zs"][Q_O + m]).then_inc(og_in, 16)
                act.dma_start(ST[:, 1, 0:T], io["hs"][m]).then_inc(hn_in, 16)
                act.wait_ge(gt_in[m % 2], 16 * (m // 2 + 1))
                A(ST[:, 2 + m % 2, 0:T], ST[:, 2 + m % 2, 0:T], ACT.Sigmoid).then_inc(gt_rdy, 1)
                act.wait_ge(og_in, 16 * (m + 1))
                A(ST[:, 0, 0:T], ST[:, 0, 0:T], ACT.Sigmoid).then_inc(sg_rdy, 1)
                act.wait_ge(yb_rdy, m + 1)
                A(XB[:, 0, m, :], ST[:, 0, 0:T], ACT.Copy).then_inc(yb_hi, 1)
                if m >= 1 and m + 1 < KT:
                    load_gate(Q_GA, m + 1, (m + 1) % 2, m)
            for m in range(2):
                load_gate(Q_GB, m, m, KT - 1 + m)
            for m in range(KT):
                act.wait_ge(gt_in[m % 2], 16 * (4 + m // 2 + 1))
                A(ST[:, 2 + m % 2, 0:T], ST[:, 2 + m % 2, 0:T], ACT.Sigmoid).then_inc(gt_rdy, 1)
                act.wait_ge(mg_rdy, m + 1)
                A(XA[:, 0, m, :], ST[:, 0, 0:T], ACT.Copy).then_inc(mg_hi, 1)
                if m + 2 < KT:
                    load_gate(Q_GB, m + 2, m % 2, KT + m + 1)
            def squares(ln, k):
                act.wait_ge(r_rdy, KT * ln + k + 1)
                if k >= 2:
                    act.wait_ge(sq_used, (KT - 2) * ln + max(1, k - 2))
                A(ST[:, k % 2, 0:T], XC[:, k, :], ACT.Square).then_inc(ln_sq, 1)

            act.wait_ge(mg_lo, KT)
            for m in range(KT):
                wait(act, gt_used, 2 * KT if m < 2 else 0)
                if m >= 2:
                    squares(0, m - 2)
                act.dma_start(ST[:, 2 + m % 2, 0:T], io["x"][:, m, :]).then_inc(xr_in[m % 2], 16)
            squares(0, KT - 2)
            squares(0, KT - 1)

            def ln_sqrt(ln):
                act.wait_ge(ln_v, ln + 1)
                A(lst[:, 2, :], lst[:, 2, :], ACT.Sqrt).then_inc(ln_s, 1)

            ln_sqrt(0)
            act.dma_start(fc[:, :, :, :], io["ffn_consts"]).then_inc(fc_in, 16)
            for n in range(NT):
                for k in range(KT):
                    q = n * KT + k
                    act.wait_ge(ln_t, q + 1)
                    if q >= 12:
                        act.wait_ge(h2_lo, q - 11)
                    for a, b, s in pieces(n):
                        last = A(hslot(q)[:, a - n * NW:b - n * NW], XC[:, k, a:b], ACT.Identity, scale=der[:, s, k:k + 1],
                                 bias=der[:, 2 + s, k:k + 1])
                    for a, b, s in pieces(n):
                        last = A(XA[:, 0, k, a:b], XC[:, k, a:b], ACT.Identity, scale=der[:, s, k:k + 1],
                                 bias=der[:, 2 + s, k:k + 1])
                    last.then_inc(h2_hi, 1)

            def fgroup(j):
                return fc[:, j, :, :] if isinstance(j, int) else fc[:, bass.ds(j, 1), :, :].rearrange("p o a b -> p (o a) b")

            def ffn_up(j, M, par, i):
                wait(act, cv_d, j * 4 + i - 3)
                A(ub[:, i, TP + 2:TP + 4], fca[:, i, 5:7], ACT.Copy)
                for n in range(NT):
                    act.wait_ge(acc_ready[n], M + 1)
                    for a, b, s in pieces(n):
                        last = A(ub[:, i, 2 + a + 2 * s:2 + b + 2 * s], acc[:, n, a - n * NW:b - n * NW], ACT.Identity,
                                 bias=fca[:, i, 0:1])
                    last.then_inc(acc_free[n], 1)
                act.drain().then_inc(u_rdy, 1)
                wait(act, fa_lo, j * 2)
                A(ST[:, i, 0:CW], ub[:, i, 2:UW], ACT.Identity, scale=fca[:, i, 3:4], bias=fca[:, i, 4:5]).then_inc(cv_a, 1)

            def ffn_gelu(j, i):
                act.wait_ge(cv_d, j * 4 + i + 1)
                A(ST[:, i, 0:CW], ST[:, i, 0:CW], ACT.Gelu_apprx_tanh).then_inc(gl_rdy, 1)

            def ffn_round(j, par):
                for t in range(2):
                    act.wait_ge(pr_rdy, j * 2 + t + 1)
                    A(fa[:, par, 0, t, 0:TP], ST[:, t, 0:TP], ACT.Copy)
                    A(fa[:, par, 0, t, TP:T], ST[:, t, TP + 2:CW], ACT.Copy).then_inc(fa_hi, 1)

            def ffn_group(j, M, par):
                A(fca[:, :, :], fgroup(j), ACT.Copy)
                act.drain()
                for i in range(4):
                    ffn_up(j, M + i, par, i)
                    if i == 3:
                        ffn_gelu(j, 2)
                ffn_gelu(j, 3)
                ffn_round(j, par)

            act.wait_ge(fc_in, 16)
            act.wait_ge(h2_lo, NT * KT)
            ffn_group(0, M_FFN, 0)
            with act.Fori(0, (FG - 1) // 2) as i:
                ffn_group(i * 2 + 1, i * 24 + (M_FFN + 4), 1)
                ffn_group(i * 2 + 2, i * 24 + (M_FFN + 16), 0)
            act.wait_ge(cs_out, 1)
            act.dma_start(io["cs_out"], cs[:, :, :, :]).then_inc(cs_out, 16)
            for k in range(KT):
                squares(1, k)
            ln_sqrt(1)
            for n in range(NT):
                act.wait_ge(acc_ready[n], M_LN2 + 1)
            last = A(lsum[:, 1, :].rearrange("p (n w) -> p n w", n=NT), acc[:, :, 0:NW], ACT.Copy)
            last.then_inc(ln_bc, 1)
            for k in LN2_ORDER:
                if k in LN2_POOL:
                    act.wait_ge(ln_p, LN2_POOL.index(k) + 1)
                else:
                    act.wait_ge(ln_t, NT * KT + LN2_DVE.index(k) + 1)
                A(XC[:, k, :], XC[:, k, :], ACT.Identity, scale=small[:, C_L2W + k:C_L2W + k + 1],
                  bias=small[:, C_L2B + k:C_L2B + k + 1]).then_inc(y_rdy, 1)
                act.wait_ge(y_rdy, LN2_ORDER.index(k) + 1)
                act.dma_start(io["y"][:, k, :], XC[:, k, :]).then_inc(y_out, 16)
            act.wait_ge(y_out, 16 * KT)
            act.wait_ge(cs_out, 17)

        @block.vector
        def _(dve):
            V = nc.vector
            V.memset(lst[:, :, :], 1.0)
            dve.wait_ge(c_in, 48)
            dve.wait_ge(sl_e, 1)
            V.tensor_tensor(silu[:, 1, :, :], silu[:, 0, :, :], small[:, C_C:C_C + 16].rearrange("p (k s) -> p k s", s=2),
                            ALU.mult).then_inc(sl_d, 1)
            bada = small[:, C_BADA:C_BADA + 48].rearrange("p (i m) -> p i m", i=6)
            dve.wait_ge(ada_col, 1)
            V.tensor_tensor(mod[:, 0:2, :, :], px[:, 4, 0:32].rearrange("p (i m s) -> p i m s", i=2, s=2),
                            bada[:, 0:2, :].unsqueeze(3).to_broadcast([P, 2, KT, 2]), ALU.add).then_inc(ada_ev, 1)
            dve.drain()
            V.tensor_scalar(mod[:, 1, :, :], mod[:, 1, :, :], 1.0, None, ALU.add)
            dve.drain()

            def h_low(q):
                n, k = divmod(q, KT)
                dve.wait_ge(h_hi, q + 1)
                cols = slice(n * NW, (n + 1) * NW)
                V.tensor_tensor(XA[:, 1, k, cols], hslot(q), XA[:, 0, k, cols].bitcast(F32), ALU.subtract).then_inc(h_lo, 1)

            for q in range(NT * KT):
                n, k = divmod(q, KT)
                if n == 0:
                    dve.wait_ge(x_in[k // 4], 16)
                for a, b, s in pieces(n):
                    last = V.tensor_scalar(hslot(q)[:, a - n * NW:b - n * NW], XC[:, k, a:b], mod[:, 1, k, s:s + 1],
                                           mod[:, 0, k, s:s + 1], ALU.mult, ALU.add)
                last.then_inc(h_tmp, 1)
                if q >= 2:
                    h_low(q - 2)
            h_low(NT * KT - 2)
            h_low(NT * KT - 1)
            dve.wait_ge(sl_e, 2)
            V.tensor_tensor(sbc[:, :, :], sbc[:, :, :], adaT_tmp, ALU.mult)
            dve.drain()
            modf = mod[:, :, :, :].rearrange("p i m s -> p (i m) s")

            def ada_four(m):
                for i in range(4):
                    dve.wait_ge(adaT_in[i], (m + 1) * 16)
                    for s in range(2):
                        V.tensor_tensor_reduce(adaT_tmp[:, s, :], adaT[:, i, :], sbc[:, s, :], 1.0, 0.0, ALU.mult, ALU.add,
                                                      ast[:, i, s:s + 1])
                    dve.drain().then_inc(adaT_used, 1)
                at4 = slice(16 + 4 * m, 20 + 4 * m) if isinstance(m, int) else bass.ds(m * 4 + 16, 4)
                bt4 = slice(C_BADA + 16 + 4 * m, C_BADA + 20 + 4 * m) if isinstance(m, int) else bass.ds(m * 4 + (C_BADA + 16), 4)
                V.tensor_tensor(modf[:, at4, :], ast[:, :, :], small[:, bt4].unsqueeze(2).to_broadcast([P, 4, 2]), ALU.add)
                dve.drain()

            ada_four(0)
            with dve.Fori(1, KT) as m:
                ada_four(m)
            V.tensor_scalar(mod[:, 4, :, :], mod[:, 4, :, :], 1.0, None, ALU.add)
            V.memset(qs[:, :, :, :], 0.0)
            dve.drain().then_inc(ada_ev, 1)
            for k in range(KT):
                w, b = small[:, C_L1W + k:C_L1W + k + 1], small[:, C_L1B + k:C_L1B + k + 1]
                for s in range(2):
                    V.tensor_scalar(der[:, s, k:k + 1], w, mod[:, 4, k, s:s + 1], None, ALU.mult)
                    V.tensor_scalar(der[:, 2 + s, k:k + 1], b, mod[:, 4, k, s:s + 1], mod[:, 3, k, s:s + 1], ALU.mult, ALU.add)
            V.tensor_scalar(der[:, 4, :], small[:, C_L1W:C_L1W + KT], ALPHA, None, ALU.mult)
            V.tensor_scalar(der[:, 5, :], small[:, C_L1B:C_L1B + KT], ALPHA, None, ALU.mult)
            dve.drain()

            def att_max(c, a, par, g, w, kb):
                dve.wait_ge(s_rdy, a + 1)
                wait(dve, tr_rdy, a - 1)
                for b in range(2):
                    V.tensor_tensor(pb[:, g, 2 * b:2 * b + 2, 0:w],
                                    px[:, b, 0:2 * BAND].rearrange("p (j w) -> p j w", j=2)[:, :, 0:w],
                                    alibi[:, 4 * g + 2 * b:4 * g + 2 * b + 2, alo(c, w):alo(c, w) + w], ALU.add)
                if g == 0:
                    wait(dve, pv_rdy, a - 2)
                    if w > kb:
                        V.tensor_copy(vt[0:w - kb, par, 0, :], px[0:w - kb, 0, 384:512])
                    V.tensor_copy(vt[0:kb, par, 1, :], px[0:kb, 1, 384:512])
                dve.drain().then_inc(s_used, 1)
                V.tensor_reduce(nmx[:, g, :], pb[:, g, :, 0:w], AX.X, ALU.max)
                dve.drain()
                V.tensor_tensor(nmx[:, g, :], nmx[:, g, :], small[:, C_SINK + 4 * g:C_SINK + 4 * g + 4], ALU.max)
                dve.drain()
                V.tensor_scalar(nmx[:, g, :], nmx[:, g, :], -1.0, None, ALU.mult)
                dve.drain()
                V.tensor_tensor(esk[:, g, :], nmx[:, g, :], small[:, C_SINK + 4 * g:C_SINK + 4 * g + 4], ALU.add).then_inc(mx_rdy, 1)

            def alo(c, w):
                return 0 if isinstance(c, int) and c == NCH else BAND - w

            def att_norm(a, g, w):
                dve.wait_ge(ex_rdy, a + 1)
                V.tensor_tensor(rden[:, :], rsum[:, g, :], esk[:, g, :], ALU.add)
                dve.drain()
                V.reciprocal(rden[:, :], rden[:, :])
                dve.drain()
                V.tensor_tensor(pb[:, g, :, 0:w], pb[:, g, :, 0:w], rden[:, :].unsqueeze(2).to_broadcast([P, 4, w]), ALU.mult)\
                 .then_inc(pn_rdy, 1)

            def att_take(c, a, g):
                dve.wait_ge(pv_rdy, a + 1)
                n = TS if isinstance(c, int) and c == NCH else CH
                tok = slice(c * CH, c * CH + n) if isinstance(c, int) else bass.ds(c * CH, n)
                V.tensor_copy(XC[:, 4 * g:4 * g + 4, tok], px[:, 4, 0:4 * CH].rearrange("p (j q) -> p j q", j=4)[:, :, 0:n])\
                 .then_inc(o_used, 1)

            def att_chunk(c, par, w, wp):
                kb = TS if isinstance(c, int) and c == NCH else CH
                att_max(c, c * 2, par, 0, w, kb)
                if wp:
                    att_take(c - 1, c * 2 - 1, 1)
                att_norm(c * 2, 0, w)
                att_max(c, c * 2 + 1, par, 1, w, kb)
                att_take(c, c * 2, 0)
                att_norm(c * 2 + 1, 1, w)

            dve.wait_ge(kv_in, 48)
            att_chunk(0, 0, CH, 0)
            att_chunk(1, 1, 2 * CH, CH)
            att_chunk(2, 0, BAND, 2 * CH)
            dve.wait_ge(row_a, 1)
            V.tensor_scalar(rowD[:, :], rowC[:, :], 1.0, None, ALU.add)
            V.tensor_scalar(rowF, rowF, small[0:HB, C_BF:C_BF + 1], 0.0, ALU.add, ALU.min)
            V.tensor_scalar(rowI, rowI, small[0:HB, C_BI:C_BI + 1], None, ALU.add)
            dve.drain()
            V.tensor_scalar(rowR[:, :], rowD[:, :], -1.0, None, ALU.add).then_inc(row_d, 1)
            dve.drain()
            V.tensor_tensor(rowC[:, :], rowC[:, :], rowR[:, :], ALU.subtract)
            att_chunk(3, 1, BAND, BAND)
            with dve.Fori(2, NCH // 2) as i:
                att_chunk(i * 2, 0, BAND, BAND)
                att_chunk(i * 2 + 1, 1, BAND, BAND)
            dve.wait_ge(row_a, 2)
            dve.drain()
            V.tensor_tensor(rowC[:, :], rowC[:, :], rowD[:, :], ALU.add)
            dve.drain()
            V.tensor_tensor(rowF, rowF, rowC[:, :], ALU.subtract)
            dve.drain()
            V.tensor_tensor_scan(rowD[:, :], rowE[:, :], rowF, 0.0, ALU.mult, ALU.add)
            V.tensor_tensor_scan(rowM[:, 0:TP], rowF[:, 0:TP], rowI[:, 0:TP], 0.0, ALU.add, ALU.max)
            V.tensor_tensor_scan(rowM[:, TP:T], rowF[:, TP:T], rowI[:, TP:T], small[0:HB, C_M0:C_M0 + 1], ALU.add, ALU.max)
            att_chunk(NCH, 0, WIN + TS, BAND)
            V.tensor_tensor(rowC[:, :], rowI, rowD[:, :], ALU.subtract)
            V.tensor_tensor(rowR[:, :], rowD[:, :], rowM[:, :], ALU.subtract)
            att_take(NCH, 2 * NCH + 1, 1)
            V.memset(mprow[:, 0:1], 0.0)
            V.tensor_copy(mprow[:, NLC:NLC + 1], small[0:HB, C_M0:C_M0 + 1])
            V.memset(va[:, DV:DV + 1], 1.0)
            V.memset(cst[:, 0, :, :], 0.0)
            dve.drain()
            V.tensor_copy(mprow[:, 1:NLC], rowM[:, 0:TP].rearrange("p (c l) -> p c l", l=LC)[:, 0:NLC - 1, LC - 1])
            dve.drain().then_inc(row_d, 1)
            dve.wait_ge(row_p, 1)
            dve.wait_ge(ml_in, 48)
            for c0, c1, L in ((0, NLC, LC), (NLC, NLC + 1, TS)):
                V.tensor_copy(at_c[0:L, c0:c1, :], px[0:L, 0, 4 * c0:4 * c1].rearrange("p (c h) -> p c h", h=HB))
                V.tensor_copy(em_c[0:L, c0:c1, :], px[0:L, 0, 64 + 4 * c0:64 + 4 * c1].rearrange("p (c h) -> p c h", h=HB))
            V.tensor_copy(mp_c[:, :, :], px[:, 0, 128:164].rearrange("p (h c) -> p h c", h=HB))
            dve.drain().then_inc(row_v, 1)
            dve.wait_ge(row_v, 2)
            dve.drain().then_inc(row_v, 1)

            def ml_unit(c, par, h, L):
                u = c * 4 + h
                ci = c if isinstance(c, int) else None

                def col(t, n=L):
                    return t[0:n, c, h:h + 1] if ci is not None else \
                        t[0:n, bass.ds(c, 1), h:h + 1].rearrange("p a b -> p (a b)")

                dve.wait_ge(sr_rdy, u + 1)
                V.tensor_copy(rs[:, 0:L], px[:, 0, P:P + L])
                dve.drain()
                V.scalar_tensor_tensor(wd[0:L, 0:L], rs[0:L, 0:L], col(at_c), cmask[0:L, 0:L], ALU.add, ALU.add).then_inc(d_rdy, 1)
                dve.wait_ge(wg_rdy, u + 1)
                V.scalar_tensor_tensor(pt[0:L, 0:L], px[0:L, 0, 0:L], KB_SCALE, wd[0:L, 0:L], ALU.mult, ALU.mult)
                V.tensor_tensor(qg[:, 0:L], zc[:, par, 4 + h, 0:L], gb[:, 0:L], ALU.mult)
                dve.drain().then_inc(p_rdy, 1)
                if h == 0 and ci != 0:
                    ml_norm(c - 1, LC)
                dve.wait_ge(nu_rdy, u + 1)
                s = 1 if ci == NLC else 0
                V.scalar_tensor_tensor(cst[:, s, h, :], cst[:, s, h, :], gb[:, L - 1:L], px[:, 3, 0:DV + 1], ALU.mult, ALU.add)
                V.tensor_scalar(dn[0:L, 0:1], px[0:L, 2, DV:DV + 1], -1.0, col(em_c), ALU.mult, ALU.max)
                dve.drain()
                V.tensor_tensor(dn[0:L, 0:1], dn[0:L, 0:1], px[0:L, 2, DV:DV + 1], ALU.max)
                dve.drain()
                V.reciprocal(dn[0:L, 1:2], dn[0:L, 0:1])
                dve.drain()
                V.tensor_scalar(hh[0:L, h, :], px[0:L, 2, 0:DV], dn[0:L, 1:2], None, ALU.mult)
                dve.drain().then_inc(e_done, 1)
                V.bn_stats(bst[0:L, h, :], hh[0:L, h, :])
                dve.drain()
                V.bn_aggr(mv[0:L, h, :], bst[0:L, h, :])
                if h == HB - 1:
                    dve.drain()
                    V.tensor_scalar(rstd[0:L, :], mv[0:L, :, 1], EPS, None, ALU.add).then_inc(var_rdy, 1)

            def ml_norm(c, L):
                dve.wait_ge(sd_rdy, c + 1)
                wait(dve, ht_rdy, c * 2)
                V.reciprocal(rstd[0:L, :], rstd[0:L, :])
                dve.drain()
                for h in range(HB):
                    last = V.tensor_scalar(hn[0:L, h, :], hh[0:L, h, :], mv[0:L, h, 0:1], rstd[0:L, h:h + 1],
                                           ALU.subtract, ALU.mult)
                dve.drain().then_inc(hn_rdy, 1)

            for c in range(2):
                for h in range(HB):
                    ml_unit(c, c, h, LC)
            with dve.Fori(1, NLC // 2) as i:
                for par in range(2):
                    for h in range(HB):
                        ml_unit(i * 2 + par, par, h, LC)
            for h in range(HB):
                ml_unit(NLC, 0, h, TS)
            for n in range(NT):
                cols = slice(n * NW, (n + 1) * NW)
                for k in range(KT):
                    dve.wait_ge(ya_hi, n * KT + k + 1)
                    V.tensor_tensor(XA[:, 1, k, cols], XC[:, k, cols], XA[:, 0, k, cols].bitcast(F32), ALU.subtract)\
                     .then_inc(ya_lo, 1)
            ml_norm(NLC, TS)

            dve.drain()
            for m in range(KT):
                dve.wait_ge(hn_in, 16 * (m + 1))
                dve.wait_ge(sg_rdy, m + 1)
                V.scalar_tensor_tensor(ST[:, 0, 0:T], ST[:, 0, 0:T], small[:, C_NW + m:C_NW + m + 1], ST[:, 1, 0:T],
                                       ALU.mult, ALU.mult).then_inc(yb_rdy, 1)
                dve.wait_ge(yb_hi, m + 1)
                V.tensor_tensor(XB[:, 1, m, :], ST[:, 0, 0:T], XB[:, 0, m, :].bitcast(F32), ALU.subtract).then_inc(yb_lo, 1)
                dve.wait_ge(gt_rdy, m + 1)
                for n in range(NT):
                    dve.wait_ge(acc_ready[n], P_PA + m + 1)
                    V.tensor_tensor(XC[:, m, n * NW:(n + 1) * NW], acc[:, n, 0:NW], ST[:, 2 + m % 2, n * NW:(n + 1) * NW], ALU.mult)\
                     .then_inc(acc_free[n], 1)
                dve.drain().then_inc(gt_used, 1)
            for m in range(KT):
                dve.wait_ge(gt_rdy, KT + m + 1)
                for n in range(NT):
                    dve.wait_ge(acc_ready[n], P_PB + m + 1)
                    V.tensor_tensor(ST[:, 0, n * NW:(n + 1) * NW], acc[:, n, 0:NW], ST[:, 2 + m % 2, n * NW:(n + 1) * NW], ALU.mult)\
                     .then_inc(acc_free[n], 1)
                dve.drain().then_inc(gt_used, 1)
                V.tensor_tensor(ST[:, 0, 0:T], ST[:, 0, 0:T], XC[:, m, :], ALU.add).then_inc(mg_rdy, 1)
                dve.wait_ge(mg_hi, m + 1)
                V.tensor_tensor(XA[:, 1, m, :], ST[:, 0, 0:T], XA[:, 0, m, :].bitcast(F32), ALU.subtract).then_inc(mg_lo, 1)
                dve.drain()
            def ln_add(k):
                last = V.tensor_tensor(lsum[:, 0, :], XC[:, 0, :] if k == 1 else lsum[:, 0, :], XC[:, k, :], ALU.add)
                if k == KT - 2:
                    last.then_inc(ln_s1, 1)

            def ln_add_square(ln, k):
                dve.wait_ge(ln_sq, KT * ln + k + 1)
                V.tensor_tensor(lsum[:, 1, :], ST[:, 0, 0:T] if k == 1 else lsum[:, 1, :], ST[:, k % 2, 0:T], ALU.add)\
                 .then_inc(sq_used, 1)

            for m in range(KT):
                if m >= 2:
                    ln_add(m - 1)
                    ln_add_square(0, m - 1)
                dve.wait_ge(xr_in[m % 2], 16 * (m // 2 + 1))
                V.tensor_scalar(ST[:, 2 + m % 2, 0:T], ST[:, 2 + m % 2, 0:T], ALPHA, None, ALU.mult)
                dve.drain()
                for n in range(NT):
                    dve.wait_ge(acc_ready[n], P_OUT + m + 1)
                    for a, b, s in pieces(n):
                        last = V.scalar_tensor_tensor(XC[:, m, a:b], acc[:, n, a - n * NW:b - n * NW], mod[:, 2, m, s:s + 1],
                                                      ST[:, 2 + m % 2, a:b], ALU.mult, ALU.add)
                    last.then_inc(acc_free[n], 1)
                dve.drain().then_inc(r_rdy, 1)

            def ln_scales(ln):
                dve.wait_ge(ln_squ, ln + 1)
                for q in range(2):
                    V.tensor_copy(lst[:, q, 0:NLC], px[:, 3 + q, 0:NLC])
                    V.tensor_copy(lst[0:TS, q, NLC:NLC + 1], px[0:TS, 3 + q, NLC:NLC + 1])
                dve.drain()
                V.tensor_tensor(lst[:, 2, :], lst[:, 0, :], lst[:, 0, :], ALU.mult)
                dve.drain()
                V.tensor_tensor(lst[:, 2, :], lst[:, 1, :], lst[:, 2, :], ALU.subtract)
                dve.drain()
                V.tensor_scalar(lst[:, 2, :], lst[:, 2, :], 0.0, EPS, ALU.max, ALU.add)
                dve.drain()
                V.reciprocal(lst[:, 2, :], lst[:, 2, :]).then_inc(ln_v, 1)
                dve.wait_ge(ln_s, ln + 1)
                V.tensor_scalar(lst[:, 3, :], lst[:, 2, :], float(D), None, ALU.mult)
                dve.drain()
                V.scalar_tensor_tensor(lst[:, 4, :], lst[:, 0, :], -1.0, lst[:, 3, :], ALU.mult, ALU.mult)
                dve.drain()
                for q in range(2):
                    V.tensor_tensor(ST[:, q, 0:TP].rearrange("p (c l) -> p c l", c=NLC),
                                    ident[:, :].unsqueeze(1).to_broadcast([P, NLC, LC]),
                                    lst[:, 3 + q, 0:NLC].unsqueeze(2).to_broadcast([P, NLC, LC]), ALU.mult)
                    V.tensor_scalar(ST[:, q, TP:T], ident[:, 0:TS], lst[:, 3 + q, NLC:NLC + 1], None, ALU.mult)
                dve.drain().then_inc(ln_dg, 1)

            ln_scales(0)

            for q in range(NT * KT):
                n, k = divmod(q, KT)
                cols = slice(n * NW, (n + 1) * NW)
                if k == 0:
                    dve.wait_ge(ln_r, NT)
                    for b in range(NT):
                        dve.wait_ge(acc_ready[b], M_LN1 + 1)
                V.tensor_tensor(XC[:, k, cols], XC[:, k, cols], px[:, n, 0:NW], ALU.mult)
                dve.drain()
                last = V.tensor_tensor(XC[:, k, cols], XC[:, k, cols], acc[:, n, 0:NW], ALU.add)
                last.then_inc(ln_t, 1)
                if k == KT - 1:
                    dve.drain().then_inc(acc_free[n], 1)
            dve.wait_ge(h2_hi, NT * KT)
            for k in range(KT):
                V.tensor_scalar(XC[:, k, :], XC[:, k, :], der[:, 4, k:k + 1], der[:, 5, k:k + 1], ALU.mult, ALU.add)

            def fgroup(j):
                return fc[:, j, :, :] if isinstance(j, int) else fc[:, bass.ds(j, 1), :, :].rearrange("p o a b -> p (o a) b")

            def cout(j, i, a):
                return cs[:, j, i, a:a + 2] if isinstance(j, int) else \
                    cs[:, bass.ds(j, 1), i, a:a + 2].rearrange("p a b -> p (a b)")

            def ffn_conv(j, i):
                dve.wait_ge(u_rdy, j * 4 + i + 1)
                V.tensor_copy(cout(j, i, 0), ub[:, i, TP:TP + 2])
                V.tensor_copy(cout(j, i, 2), ub[:, i, UW - 2:UW])
                dve.wait_ge(cv_a, j * 4 + i + 1)
                V.scalar_tensor_tensor(ST[:, i, 0:CW], ub[:, i, 0:CW], fcd[:, i, 1:2], ST[:, i, 0:CW], ALU.mult, ALU.add)
                dve.drain()
                V.scalar_tensor_tensor(ST[:, i, 0:CW], ub[:, i, 1:CW + 1], fcd[:, i, 2:3], ST[:, i, 0:CW], ALU.mult, ALU.add)\
                 .then_inc(cv_d, 1)

            def ffn_prod(j, t):
                dve.wait_ge(gl_rdy, j * 2 + t + 1)
                V.tensor_tensor(ST[:, t, 0:CW], ST[:, t, 0:CW], ST[:, 2 + t, 0:CW], ALU.mult).then_inc(pr_rdy, 1)

            def ffn_low(j, par, t):
                dve.wait_ge(fa_hi, j * 2 + t + 1)
                V.tensor_tensor(fa[:, par, 1, t, 0:TP], ST[:, t, 0:TP], fa[:, par, 0, t, 0:TP].bitcast(F32), ALU.subtract)
                V.tensor_tensor(fa[:, par, 1, t, TP:T], ST[:, t, TP + 2:CW], fa[:, par, 0, t, TP:T].bitcast(F32), ALU.subtract)
                dve.drain().then_inc(fa_lo, 1)

            def ffn_take(M, m):
                for n in range(NT):
                    dve.wait_ge(acc_ready[n], M + m + 1)
                    for a, b, s in pieces(n):
                        last = V.scalar_tensor_tensor(XC[:, m, a:b], acc[:, n, a - n * NW:b - n * NW], mod[:, 5, m, s:s + 1],
                                                      XC[:, m, a:b], ALU.mult, ALU.add)
                    last.then_inc(acc_free[n], 1)

            def ffn_iter(j, par, M):
                V.tensor_copy(fcd[:, :, :], fgroup(j))
                dve.drain()
                for i in range(3):
                    ffn_conv(j, i)
                ffn_take(M, 0)
                ffn_conv(j, 3)
                ffn_take(M, 1)
                ffn_prod(j, 0)
                ffn_take(M, 2)
                ffn_prod(j, 1)
                ffn_take(M, 3)
                ffn_low(j, par, 0)
                ffn_take(M, 4)
                ffn_low(j, par, 1)
                for m in range(5, KT):
                    ffn_take(M, m)

            dve.wait_ge(fc_in, 16)
            V.memset(ub[:, :, 0:2], 0.0)
            V.tensor_copy(fcd[:, :, :], fgroup(0))
            dve.drain()
            for i in range(4):
                ffn_conv(0, i)
            for t in range(2):
                ffn_prod(0, t)
            for t in range(2):
                ffn_low(0, 0, t)
            with dve.Fori(0, (FG - 1) // 2) as i:
                ffn_iter(i * 2 + 1, 1, i * 24 + (M_FFN + 8))
                ffn_iter(i * 2 + 2, 0, i * 24 + (M_FFN + 20))
            dve.drain().then_inc(cs_out, 1)
            for m in range(KT):
                ffn_take(M_FFN + 12 * FG - 8, m)
                dve.drain().then_inc(r_rdy, 1)
                if m >= 2:
                    ln_add_square(1, m - 1)
            ln_scales(1)
            dve.wait_ge(ln_r, 2 * NT)
            V.tensor_copy(lsum[:, 0, :].rearrange("p (n w) -> p n w", n=NT), px[:, 0:NT, 0:NW])
            dve.drain().then_inc(ln_bc, 1)
            dve.wait_ge(ln_bc, 2)
            for k in LN2_DVE:
                V.tensor_tensor(XC[:, k, :], XC[:, k, :], lsum[:, 0, :], ALU.mult)
                dve.drain()
                V.tensor_tensor(XC[:, k, :], XC[:, k, :], lsum[:, 1, :], ALU.add).then_inc(ln_t, 1)


IN_SHAPES = {
    "w_panels": (N_PANEL, P, D), "w_ada": (16, P, D), "w_adaT": (32, P, D), "c_bc": (P, 2, D), "x": (P, KT, T), "small": (P, N_SMALL), "ident": (P, P), "ones": (P, P),
    "alibi": (P, 8, BAND), "k_cache": (P, 2, WIN), "v_cache": (P, WIN), "rmask": (HB, T), "sel": (HB, HB, P), "cmask": (P, P),
    "c_state": (P, HB, DV + 1), "ffn_consts": (P, FG, 4, 8),
}
OUT_SHAPES = {
    "y": (P, KT, T), "k_out": (2, 2, 64, WIN), "v_out": (2, 2, 64, WIN), "c_out": (2, P, HB, DV + 1), "m_out": (2, HB, 1),
    "cs_out": (P, FG, 4, 4),
}


def tiles(w):
    n = w.shape[1] // P
    return w.reshape(KT, P, n, P).transpose(2, 1, 0, 3).reshape(n, P, D)


def kernel(**inputs):
    import concourse.bacc as bacc
    from concourse.bass_utils import run_bass_kernel_spmd

    a = {k: np.asarray(v) for k, v in inputs.items()}
    f = np.float32
    w_in = a["w_in"][0]
    cut = np.cumsum([1024, 128, 128, 512, 512, 1024, 4, 4, 1024, 1024])
    qa, ka, va, qb, kb, vb, ig, fg, og, ga, gb = np.split(w_in, cut, axis=1)
    kdup = np.concatenate([ka[:, 0:64], ka[:, 0:64], ka[:, 64:128], ka[:, 64:128]], axis=1)
    gates = np.concatenate([ig, fg, np.zeros((D, P - 8), f)], axis=1)
    up = tiles(a["w_up"][0])
    dn = a["w_down"][0].reshape(FG, 2, P, 2, 4, P).transpose(0, 3, 2, 4, 1, 5).reshape(FG, 2, P, D)

    def up4(j):
        return [up[2 * j], up[2 * j + 1], up[UT // 2 + 2 * j], up[UT // 2 + 2 * j + 1]]

    panels = [tiles(np.concatenate([qa, kdup, va, gates, kb, qb, vb, og, gb, ga], axis=1)),
              tiles(a["w_proj_a"][0]), tiles(a["w_proj_b"][0]), tiles(a["w_out"][0])]
    ffn = up4(0)
    for j in range(1, FG):
        ffn += up4(j) + [dn[j - 1, 0], dn[j - 1, 1]]
    ffn += [dn[FG - 1, 0], dn[FG - 1, 1]]
    w_panels = np.concatenate(panels + [np.stack(ffn)], axis=0)

    def cols(v):
        return v.reshape(-1, P).T

    x = np.concatenate([a["x_prompt"][0], a["x_sample"][0]], axis=0)
    small = np.zeros((P, N_SMALL), f)
    small[:, C_BADA:C_BADA + 48] = cols(a["b_ada"][0])
    for c, nme in ((C_L1W, "ln1_w"), (C_L1B, "ln1_b"), (C_L2W, "ln2_w"), (C_L2B, "ln2_b"), (C_NW, "mlstm_norm_w")):
        small[:, c:c + 8] = cols(a[nme][0])
    small[:, C_C:C_C + 16:2] = cols(a["c_prompt"][0])
    small[:, C_C + 1:C_C + 16:2] = cols(a["c_sample"][0])
    small[:, C_SINK:C_SINK + 8] = np.repeat(a["attn_sinks"][0].reshape(8, 2).T, 64, axis=0)
    small[0:HB, C_BI] = a["b_igate"][0]
    small[0:HB, C_BF] = a["b_fgate"][0]
    small[0:HB, C_M0] = a["state_mlstm_m"][0, 0]
    kc = a["cache_attn_k"][0, 0].transpose(1, 2, 0)
    vc = a["cache_attn_v"][0, 0].transpose(1, 2, 0)
    k_cache = np.concatenate([kc, kc], axis=1).transpose(1, 0, 2)
    c_state = np.concatenate([a["state_mlstm_C"][0, 0], a["state_mlstm_n"][0, 0][:, None, :]], axis=1).transpose(2, 0, 1)
    fcn = np.zeros((UT, P, 8), f)
    fcn[:, :, 0] = a["b_up"][0].reshape(UT, P)
    for j in range(3):
        fcn[:, :, 1 + j] = a["conv_w"][0, j].reshape(UT, P)
    fcn[:, :, 4] = a["conv_b"][0].reshape(UT, P)
    for j in range(2):
        fcn[:, :, 5 + j] = a["state_ffn_conv"][0, 0, j].reshape(UT, P)
    ffn_consts = fcn.reshape(2, FG, 2, P, 8).transpose(3, 1, 0, 2, 4).reshape(P, FG, 4, 8)

    slopes = (f(2.0) ** (f(-8.0) * np.arange(1, 17, dtype=f) / f(16))).astype(f)
    dist = np.abs(WIN + np.arange(CH)[:, None] - np.arange(BAND)[None, :]).astype(f)
    alibi = (-slopes.reshape(8, 2).transpose(1, 0)[:, None, :, None] * dist[None, :, None, :]).reshape(P, 8, BAND)
    rmask = np.ones((HB, T), f)
    rmask[:, 0:T:LC] = 0.0
    sel = np.zeros((HB, HB, P), f)
    for h in range(HB):
        sel[h, h, :] = 1.0
    cmask = np.where(np.arange(P)[:, None] <= np.arange(P)[None, :], f(0), f(-1e30)).astype(f)

    arrays = {
        "w_panels": w_panels, "w_ada": tiles(a["w_ada"][0][:, 0:2048]), "w_adaT": a["w_ada"][0][:, 2048:].T,
        "c_bc": np.broadcast_to(np.stack([a["c_prompt"][0], a["c_sample"][0]]), (P, 2, D)), "x": x.T.reshape(KT, P, T).transpose(1, 0, 2), "small": small,
        "ident": np.eye(P, dtype=f), "ones": np.full((P, P), 1.0 / D, f), "alibi": alibi, "k_cache": k_cache,
        "v_cache": vc.reshape(P, WIN), "rmask": rmask, "sel": sel, "cmask": cmask, "c_state": c_state, "ffn_consts": ffn_consts,
    }
    nc = bacc.Bacc("TRN2", target_bir_lowering=False, num_devices=1)
    io, feed = {}, {}
    for name, shape in IN_SHAPES.items():
        feed[f"in_{name}"] = np.ascontiguousarray(arrays[name].reshape(shape), dtype=f)
        io[name] = nc.dram_tensor(f"in_{name}", shape, F32, kind="ExternalInput").ap()
    for name, shape in OUT_SHAPES.items():
        io[name] = nc.dram_tensor(f"out_{name}", shape, F32, kind="ExternalOutput").ap()
    io["zs"] = nc.dram_tensor("z_spill", (N_SPILL, P, T), F32, kind="Internal").ap()
    io["hs"] = nc.dram_tensor("h_spill", (KT, P, T), F32, kind="Internal").ap()
    build(nc, io)
    r = run_bass_kernel_spmd(nc, [feed], core_ids=[0]).results[0]
    o = {name: np.asarray(r[f"out_{name}"]) for name in OUT_SHAPES}
    y = o["y"].transpose(1, 0, 2).reshape(D, T).T
    ko = o["k_out"].transpose(1, 3, 0, 2)
    vo = o["v_out"].transpose(1, 3, 0, 2)
    co = o["c_out"].transpose(0, 2, 3, 1)
    cso = o["cs_out"].reshape(P, FG, 2, 2, 4).transpose(4, 2, 1, 3, 0).reshape(4, UT * P)
    outs = []
    for s in range(2):
        outs.append((ko[s][None, None], vo[s][None, None], co[s, :, 0:DV][None, None], co[s, :, DV][None, None],
                     o["m_out"][s, :, 0][None, None], cso[2 * s:2 * s + 2][None, None]))
    c = np.ascontiguousarray
    return (c(y[0:TP][None]), c(y[TP:][None])) + tuple(c(t) for t in outs[0]) + tuple(c(t) for t in outs[1])
```

```python
from contextlib import ExitStack

import numpy as np
import concourse.bass as bass
from concourse import mybir

F32 = mybir.dt.float32
F32R = mybir.dt.float32r
ALU = mybir.AluOpType
ACT = mybir.ActivationFunctionType
AX = mybir.AxisListType

P = 128
D = 1024
KT = D // P
TP, TS = 1024, 32
T = TP + TS
NT = 3
NW = T // NT
CH = 64
NCH = TP // CH
BAND = 3 * CH
WIN = 128
HB, DV = 4, 256
LC = 128
NLC = TP // LC
UT = 5632 // P
FG = UT // 4
UW = T + 4
CW = UW - 2
ALPHA = 2.0 ** 0.25
EPS = 1e-5
KB_SCALE = 128.0 ** -0.5

P_ATT = 11
P_ML = P_ATT + NCH + 1
PPC = 3
P_PA = P_ML + 3 * KT
P_PB = P_PA + KT
P_OUT = P_PB + KT
P_FFN = P_OUT + KT
LN1_STEPS = NT * KT // 2
N_PANEL = P_FFN + 6 * FG
M_LN1 = P_FFN
M_FFN = M_LN1 + 1
M_LN2 = M_FFN + 12 * FG
N_SPILL = P_PA - P_ATT
Q_O, Q_GB, Q_GA = 17, 25, 33

C_BADA, C_L1W, C_L1B, C_L2W, C_L2B, C_NW, C_C, C_SINK, C_BI, C_BF, C_M0 = 0, 48, 56, 64, 72, 80, 88, 104, 112, 113, 114
N_SMALL = 116

LN2_CUTS = (0, 3, 6, KT)

BRANCH_ORDER = tuple((s[0], int(s[1])) for s in "a0 a1 g2 y0 g3 a2 g4 y1 a3 g5 y2 y3 a4 g6 y4 y5 a5 g7 y6 y7 a6 a7".split())


def ml_part(c):
    if isinstance(c, int) and c >= NLC - 2:
        return PPC * (NLC - 2) + 2 * (c - NLC + 2), (0, 3, 6, 9, 12)
    return c * PPC, ((6, 9, 12, 15, 18) if isinstance(c, int) and c == 0 else (0, 5, 9, 14, 18))


def wait(eng, sem, v):
    if isinstance(v, int) and v <= 0:
        return
    eng.wait_ge(sem, v)


def build(nc, io):
    ctx = ExitStack()
    with ctx:
        W0 = 16512
        RAW_B, WHL_B = 2 * D * 4, 2 * 2 * D * 4
        A_B = 2 * KT * T * 4
        C_B = KT * T * 4
        o_raw = W0
        o_whl = o_raw + RAW_B
        o_A = o_whl + WHL_B
        o_B = o_A + A_B
        o_C = o_B + A_B
        o_S = o_C + C_B
        o_M = o_S + 4 * UW * 4
        place = {"end": 0}

        def at(name, shape, off, dt=F32):
            n = int(np.prod(shape[1:])) * 4
            place["end"] = off + n
            return nc.alloc_sbuf_tensor_at(name, shape, dt, offset=off)

        def after(name, shape, dt=F32):
            return at(name, shape, (place["end"] + 31) // 32 * 32, dt)

        raw = at("w_raw", [P, 2, D], o_raw)
        whl = at("w_hilo", [P, 2, 2, D], o_whl, F32R)
        XA = at("x_hilo_a", [P, 2, KT, T], o_A, F32R)
        XB = at("x_hilo_b", [P, 2, KT, T], o_B, F32R)
        XC = at("x_c", [P, KT, T], o_C)
        ST = at("stage", [P, 4, UW], o_S)
        small = at("small", [P, N_SMALL], o_M)
        ident = after("ident", [P, P])
        ones = after("ones", [P, P])
        mod = after("mod", [P, 6, KT, 2])
        der = after("der", [P, 6, KT])
        lst = after("ln_stats", [P, 5, NLC + 1])
        assert place["end"] <= 229344
        ada = at("ada_ring", [P, KT, D], o_B)
        silu = after("silu", [P, 2, KT, 2])
        mrow = after("mod_row", [2, 2, 2 * P])
        kk = at("k_dup", [P, 2, TP + WIN + TS], o_B)
        vv = after("v_feat", [P, TP + WIN + TS])
        alibi = after("alibi", [P, 8, BAND])
        qs = after("q_stage", [P, 2, KT, P])
        ks = after("k_stage", [P, 2, 2, BAND])
        vs = after("v_stage", [P, 2, BAND])
        vt = after("v_tok", [P, 2, 2, P])
        pb = after("probs", [P, 2, 4, BAND])
        pta = after("probs_ta", [P, 4, P])
        ptb = after("probs_tb", [P, 4, P])
        nmx = after("neg_max", [P, 2, 4])
        esk = after("exp_sink", [P, 2, 4])
        rsum = after("row_sum", [P, 2, 4])
        rden = after("row_den", [P, 4])
        o_rows = o_C - 5 * T * 4
        assert place["end"] <= o_rows
        adaT = at("adaT_ring", [P, 4, D], o_B + 48128)
        assert place["end"] <= o_C
        sbc = at("silu_bc", [P, 2, D], o_B + 48128 - 8192)
        ast = at("ada_sums", [P, 4, 2], o_B + 48128 + 4 * 4096)
        assert place["end"] <= o_C
        rowC, rowD, rowE, rowM, rowR = (at(n, [HB, T], o_rows + i * T * 4)
                                        for i, n in enumerate(("rowC", "rowD", "rowE", "rowM", "rowR")))
        zc = at("zc", [P, 2, 16, LC], o_B)
        cst = after("c_state", [P, 2, HB, DV + 1])
        sel = after("sel", [HB, HB, P])
        cmask = after("cmask", [P, P])
        mprow = after("mprow", [HB, NLC + 1])
        at_c = after("a_cols", [P, NLC + 1, HB])
        em_c = after("em_cols", [P, NLC + 1, HB])
        mp_c = after("mp_cols", [P, HB, NLC + 1])
        rs = after("r_bc", [P, LC])
        wd = after("w_dec", [P, LC])
        gb = after("g_bc", [P, LC])
        wks = after("wk_col", [P, 1])
        pt = after("p_t", [P, LC])
        qg = after("q_g", [P, LC])
        kw = after("k_w", [P, LC])
        va = after("v_aug", [P, DV + 1])
        hh = after("h_tok", [P, HB, DV])
        hn = at("hn_tok", [P, HB, DV], place["end"])
        dn = after("den", [P, 2])
        bst = after("bn_st", [P, HB, 6])
        mv = after("mean_var", [P, HB, 2])
        rstd = after("rstd", [P, HB])
        hT = after("hn_feat", [P, KT, LC])
        assert place["end"] <= o_rows, (place["end"], o_rows)
        rowI = ST[0:HB, 2, 0:T]
        rowF = ST[0:HB, 3, 0:T]
        fa = at("ffn_act", [P, 2, 2, 2, T], o_B, F32R)
        ub = after("u_rows", [P, 4, UW])
        fc = after("ffn_consts", [P, FG, 4, 8])
        cs = after("conv_out", [P, FG, 4, 4])
        fca = after("consts_act", [P, 4, 8])
        fcd = after("consts_dve", [P, 4, 8])
        lsum = after("ln_sums", [P, 2, T])
        assert place["end"] <= o_C

        acc = ctx.enter_context(nc.psum_tensor("acc", [P, NT, 512], F32))
        px = ctx.enter_context(nc.psum_tensor("px", [P, 5, 512], F32))

        def sem(name):
            return ctx.enter_context(nc.semaphore(name))

        raw_in = [sem("raw_in0"), sem("raw_in1")]
        raw_used, split_begun, w_hi, w_ready, w_start = sem("raw_used"), sem("split_begun"), sem("w_hi"), sem("w_ready"), sem("w_start")
        acc_ready = [sem(f"acc_ready{n}") for n in range(NT)]
        acc_free = [sem(f"acc_free{n}") for n in range(NT)]
        c_in, x_in = sem("c_in"), [sem(f"x_in{i}") for i in range(KT)]
        ada_in = [sem(f"ada_in{i}") for i in range(KT)]
        adaT_in = [sem(f"adaT_in{i}") for i in range(4)]
        cb_in, ada_used, ada_ev, ada_row, ada_col, ada_mod, adaT_used = (
            sem(n) for n in ("cb_in", "ada_used", "ada_ev", "ada_row", "ada_col", "ada_mod", "adaT_used"))
        sl_e, sl_d = sem("sl_e"), sem("sl_d")
        h_tmp, h_hi, h_lo = sem("h_tmp"), sem("h_hi"), sem("h_lo")
        qkv_ev, kv_in, kv_out = sem("qkv_ev"), sem("kv_in"), sem("kv_out")
        st_rdy, s_rdy, s_used, mx_rdy, ex_rdy, pn_rdy = (sem(n) for n in ("st_rdy", "s_rdy", "s_used", "mx_rdy", "ex_rdy", "pn_rdy"))
        tr_rdy, pt_rdy, pv_rdy, o_used = (sem(n) for n in ("tr_rdy", "pt_rdy", "pv_rdy", "o_used"))
        sp_cp = sem("sp_cp")
        sp_out = [sem("sp_out0"), sem("sp_out1")]
        ml_in, g_in, row_d, row_a, row_p, row_v = (sem(n) for n in ("ml_in", "g_in", "row_d", "row_a", "row_p", "row_v"))
        zc_in = [sem("zc_in0"), sem("zc_in1")]
        sr_rdy, kvt_rdy, d_rdy, wg_rdy, kv_rdy, p_rdy, nu_rdy, e_done, var_rdy, sd_rdy, hn_rdy, ht_rdy, ht_cp = (
            sem(n) for n in ("sr_rdy", "kvt_rdy", "d_rdy", "wg_rdy", "kv_rdy", "p_rdy", "nu_rdy", "e_done", "var_rdy", "sd_rdy",
                             "hn_rdy", "ht_rdy", "ht_cp"))
        hs_out, st_out = sem("hs_out"), sem("st_out")
        ya_hi, ya_lo = sem("ya_hi"), sem("ya_lo")
        og_in, hn_in = [sem("og_in0"), sem("og_in1")], [sem("hn_in0"), sem("hn_in1")]
        sg_rdy, yb_rdy, yb_hi, yb_lo = (sem(n) for n in ("sg_rdy", "yb_rdy", "yb_hi", "yb_lo"))
        gt_in = [sem("gt_in0"), sem("gt_in1")]
        gt_rdy, gt_used, mg_rdy, mg_hi, mg_lo = (sem(n) for n in ("gt_rdy", "gt_used", "mg_rdy", "mg_hi", "mg_lo"))
        xr_in = [sem("xr_in0"), sem("xr_in1")]
        ln_s1, s1_add, sq_used, r_rdy, ln_sq, ln_squ, ln_v, ln_s, ln_dg, ln_r, ln_t, ln_bc, ln_bn, ln_p, ln_m, h2_d = (
            sem(n) for n in ("ln_s1", "s1_add", "sq_used", "r_rdy", "ln_sq", "ln_squ", "ln_v", "ln_s", "ln_dg", "ln_r", "ln_t", "ln_bc", "ln_bn", "ln_p", "ln_m", "h2_d"))
        h2_hi, h2_lo, fc_in = (sem(n) for n in ("h2_hi", "h2_lo", "fc_in"))
        u_rdy, cv_a, cv_d, gl_rdy, pr_rdy, fa_hi, fa_lo = (sem(n) for n in ("u_rdy", "cv_a", "cv_d", "gl_rdy", "pr_rdy", "fa_hi", "fa_lo"))
        y_rdy, y_out, cs_out = sem("y_rdy"), sem("y_out"), sem("cs_out")
        block = ctx.enter_context(nc.Block())

        def hslot(q):
            return ST[:, (2 + q % 12 // 3) % 4, (q % 3) * NW:(q % 3 + 1) * NW]

        adaT_tmp = at("adaT_tmp", [P, 2, D], o_S + 8192)[:, :, :]

        def yb_stage(m):
            return (ST[:, 0, 0:T], ST[:, 1, 0:T]) if m % 2 == 0 else (XC[:, KT - 2, :], XC[:, KT - 1, :])

        def pieces(n):
            a, b = n * NW, (n + 1) * NW
            return [(a, b, 0)] if b <= TP else [(a, TP, 0), (TP, b, 1)]

        @block.sync
        def _(sp):
            def panel_pair(i):
                for s in range(2):
                    wait(sp, raw_used, 2 * i + s - 1)
                    sp.dma_start(raw[:, s, :], io["w_panels"][bass.ds(i * 2 + s, 1), :, :].rearrange("o p n -> p (o n)"))\
                      .then_inc(raw_in[s], 16)

            for m in range(KT):
                for i in range(2):
                    q = 2 * m + i
                    wait(sp, ada_used, q - KT + 1)
                    sp.dma_start(ada[:, q % KT, :], io["w_ada"][i * KT + m]).then_inc(ada_in[q % KT], 16)
                sp.dma_start(XC[:, m, :], io["x"][:, m, :]).then_inc(x_in[m], 16)
                if m == 1:
                    panel_pair(0)
            with sp.Fori(1, N_PANEL // 2) as i:
                panel_pair(i)
            for n in range(NT):
                for i, (a, b) in enumerate(zip(LN2_CUTS[0:3], LN2_CUTS[1:4])):
                    sp.wait_ge(y_rdy, 3 * n + i + 1)
                    sp.dma_start(io["y"][:, a:b, n * NW:(n + 1) * NW], XC[:, a:b, n * NW:(n + 1) * NW]).then_inc(y_out, 16)
            sp.wait_ge(y_out, 16 * 3 * NT)

        @block.gpsimd
        def _(pool):
            def split_pair(i, both=False):
                for s in range(2):
                    pool.wait_ge(raw_in[s], (i + 1) * 16)
                    if both and s:
                        pool.wait_ge(acc_ready[NT - 1], M_LN1)
                    elif both:
                        pool.wait_ge(w_start, P_FFN)
                    elif not isinstance(i, int):
                        pool.wait_ge(w_start, i * 2 + s)
                    pool.sem_inc(split_begun, 1)
                    nc.gpsimd.tensor_copy(whl[:, s, 0, :], raw[:, s, :]).then_inc(w_hi, 1)
                    pool.wait_ge(w_hi, i * 2 + s + 1)
                    nc.gpsimd.tensor_tensor(whl[:, s, 1, :], raw[:, s, :], whl[:, s, 0, :].bitcast(F32), ALU.subtract)\
                      .then_inc(w_ready, 1)
                    pool.wait_ge(w_ready, i * 2 + s + 1)
                    pool.sem_inc(raw_used, 1)

            split_pair(0)
            with pool.Fori(1, P_FFN // 2) as i:
                split_pair(i)
            split_pair(P_FFN // 2, both=True)
            for q in range(NT * KT):
                n, k = divmod(q, KT)
                cols = slice(n * NW, (n + 1) * NW)
                pool.wait_ge(h2_hi, q + 1)
                if k % 4 == 3:
                    pool.wait_ge(h2_d, q // 4 + 1)
                nc.gpsimd.tensor_tensor(XA[:, 1, k, cols], hslot(q), XA[:, 0, k, cols].bitcast(F32), ALU.subtract).then_inc(h2_lo, 1)
            with pool.Fori(P_FFN // 2 + 1, N_PANEL // 2) as i:
                split_pair(i)
            for k in range(1, KT - 1):
                pool.wait_ge(r_rdy, KT + k + 1)
                wait(pool, s1_add, k - 1)
                nc.gpsimd.tensor_tensor(lsum[:, 0, :], XC[:, 0, :] if k == 1 else lsum[:, 0, :], XC[:, k, :], ALU.add)\
                  .then_inc(s1_add, 1)
            k0 = LN2_CUTS[2]
            for n in range(NT):
                cols = slice(n * NW, (n + 1) * NW)
                pool.wait_ge(ln_bc, n + 1)
                nc.gpsimd.tensor_tensor(XC[:, k0:KT, cols], XC[:, k0:KT, cols], lsum[:, 0:1, cols].to_broadcast([P, KT - k0, NW]),
                                        ALU.mult).then_inc(ln_m, 1)
                pool.wait_ge(ln_m, n + 1)
                pool.wait_ge(ln_bn, n + 1)
                nc.gpsimd.tensor_tensor(XC[:, k0:KT, cols], XC[:, k0:KT, cols], lsum[:, 1:2, cols].to_broadcast([P, KT - k0, NW]),
                                        ALU.add).then_inc(ln_p, 1)

        @block.tensor
        def _(pe):
            mm = nc.tensor.matmul

            def gemm_half(p, slot, n, half, rhs):
                if n == 0 and half == 0:
                    pe.wait_ge(w_ready, p + 1)
                if half == 0:
                    wait(pe, acc_free[n], p)
                for k in range(half * KT // 2, (half + 1) * KT // 2):
                    for j, (wi, xi) in enumerate(((0, 0), (0, 1), (1, 0))):
                        last = mm(acc[:, n, 0:NW], whl[:, slot, wi, k * P:(k + 1) * P], rhs[:, xi, k, n * NW:(n + 1) * NW],
                                  start=(k == 0 and j == 0), stop=(k == KT - 1 and j == 2))
                        if n == 0 and k == 0 and j == 0:
                            last.then_inc(w_start, 1)
                if half == 1:
                    last.then_inc(acc_ready[n], 1)

            def gemm(p, slot, n, rhs):
                for half in range(2):
                    gemm_half(p, slot, n, half, rhs)

            pe.wait_ge(sl_d, 1)
            for m in range(KT + 4):
                if 1 <= m <= KT:
                    pe.wait_ge(ada_row, m)
                    wait(pe, ada_mod, m - 1)
                    for i in range(2):
                        last = nc.tensor.transpose(px[:, 4, 2 * i:2 * i + 2], mrow[:, (m - 1) % 2, i * P:(i + 1) * P],
                                                   ident[0:2, 0:2])
                    last.then_inc(ada_col, 1)
                if m < KT:
                    for i in range(2):
                        q = 2 * m + i
                        pe.wait_ge(ada_in[q % KT], (q // KT + 1) * 16)
                        for k in range(KT):
                            last = mm(px[0:2, 3, i * P:(i + 1) * P], silu[:, 1, k, :], ada[:, q % KT, k * P:(k + 1) * P],
                                      start=(k == 0), stop=(k == KT - 1))
                        last.then_inc(ada_used, 1)
                for p in range(2):
                    k = m - 2 - 2 * p
                    if not 0 <= k < KT:
                        continue
                    if p == 0:
                        pe.wait_ge(h_lo, k + 1)
                    if k == 0:
                        pe.wait_ge(w_ready, p + 1)
                    for j, (wi, xi) in enumerate(((0, 0), (0, 1), (1, 0))):
                        for n in range(NT):
                            last = mm((acc, px)[p][:, n, 0:NW], whl[:, p, wi, k * P:(k + 1) * P],
                                      XA[:, xi, k, n * NW:(n + 1) * NW], start=(k == 0 and j == 0),
                                      stop=(k == KT - 1 and j == 2))
                            if n == 0 and j == 0 and (p, k) in ((0, 0), (1, KT - 2)):
                                last.then_inc(w_start, 1)
                            if k == KT - 1 and j == 2:
                                last.then_inc(acc_ready[n], 1)

            with pe.Fori(1, KT // 2) as i:
                for s in range(2):
                    for n in range(NT):
                        gemm(i * 2 + s, s, n, XA)
            for p in range(KT, P_ATT):
                for n in range(NT):
                    gemm(p, p % 2, n, XA)

            def att_scores(c, a, par, g, w, kb):
                if g == 0:
                    pe.wait_ge(st_rdy, c + 1)
                wait(pe, s_used, a)
                if g == 0:
                    if w > kb:
                        nc.tensor.transpose(px[0:w - kb, 0, 384:512], vs[:, par, 0:w - kb], ident[:, :])
                    nc.tensor.transpose(px[0:kb, 1, 384:512], vs[:, par, w - kb:w], ident[:, :])
                for j in range(4):
                    last = mm(px[:, j // 2, (j % 2) * BAND:(j % 2) * BAND + w], qs[:, par, 4 * g + j, :], ks[:, par, g, 0:w],
                              start=True, stop=True, skip_group_check=True)
                last.then_inc(s_rdy, 1)

            def att_transpose(a, g, w, kb):
                pe.wait_ge(pn_rdy, a + 1)
                wait(pe, pt_rdy, a)
                for j in range(4):
                    if w > kb:
                        nc.tensor.transpose(px[0:w - kb, 2, j * P:(j + 1) * P], pb[:, g, j, 0:w - kb], ident[:, :])
                    last = nc.tensor.transpose(px[0:kb, 3, j * P:(j + 1) * P], pb[:, g, j, w - kb:w], ident[:, :])
                last.then_inc(tr_rdy, 1)

            def att_values(a, par, g, w, kb):
                pe.wait_ge(pt_rdy, a + 1)
                wait(pe, o_used, a)
                for e in range(2):
                    out = px[64 * e:64 * e + 64, 4, 0:4 * CH]
                    if w > kb:
                        mm(out, vt[0:w - kb, par, 0, g * 64:g * 64 + 64], pta[0:w - kb, :, 64 * e:64 * e + 64],
                           start=True, stop=False)
                    last = mm(out, vt[0:kb, par, 1, g * 64:g * 64 + 64], ptb[0:kb, :, 64 * e:64 * e + 64],
                              start=(w == kb), stop=True)
                last.then_inc(pv_rdy, 1)

            def att_chunk(c, par, w, kb, wp, kbp):
                slot = (P_ATT + par) % 2
                first = isinstance(c, int) and c == 0
                for g in range(2):
                    if first and g == 0:
                        for half in range(2):
                            gemm_half(P_ATT, slot, 0, half, XA)
                        att_scores(0, 0, 0, 0, w, kb)
                        gemm_half(P_ATT, slot, 1, 0, XA)
                        continue
                    before = (c * 2 - 1, 1 - par, 1, wp, kbp) if g == 0 else (c * 2, par, 0, w, kb)
                    att_scores(c, c * 2 + g, par, g, w, kb)
                    gemm_half(c + P_ATT, slot, *divmod(3 * g, 2), XA)
                    att_transpose(before[0], before[2], before[3], before[4])
                    gemm_half(c + P_ATT, slot, *divmod(3 * g + 1, 2), XA)
                    att_values(*before)
                    gemm_half(c + P_ATT, slot, *divmod(3 * g + 2, 2), XA)

            att_chunk(0, 0, CH, CH, 0, 0)
            att_chunk(1, 1, 2 * CH, CH, CH, CH)
            att_chunk(2, 0, BAND, CH, 2 * CH, CH)
            att_chunk(3, 1, BAND, CH, BAND, CH)
            with pe.Fori(2, NCH // 2) as i:
                att_chunk(i * 2, 0, BAND, CH, BAND, CH)
                att_chunk(i * 2 + 1, 1, BAND, CH, BAND, CH)
            att_chunk(NCH, 0, WIN + TS, TS, BAND, CH)
            att_transpose(2 * NCH + 1, 1, WIN + TS, TS)
            att_values(2 * NCH + 1, 0, 1, WIN + TS, TS)

            for n in range(NT - 1):
                gemm(P_ML, P_ML % 2, n, XA)
            pe.wait_ge(row_d, 2)
            pe.wait_ge(ml_in, 16 * 3)
            for c in range(NLC + 1):
                L = LC if c < NLC else TS
                nc.tensor.transpose(px[0:L, 0, 4 * c:4 * c + 4], rowC[:, c * LC:c * LC + L], ident[0:HB, 0:HB])
                nc.tensor.transpose(px[0:L, 0, 64 + 4 * c:68 + 4 * c], rowM[:, c * LC:c * LC + L], ident[0:HB, 0:HB])
            for h in range(HB):
                last = mm(px[:, 0, 128 + 9 * h:137 + 9 * h], sel[:, h, :], mprow[:, :], start=True, stop=True)
            last.then_inc(row_p, 1)
            gemm(P_ML, P_ML % 2, NT - 1, XA)

            def ml_unit(c, r, par, h, L):
                u = c * 4 + h
                z = zc[:, par, :, :]
                smp = isinstance(c, int) and c == NLC
                q0, cuts = ml_part(c)
                part = list(range(cuts[h], cuts[h + 1]))

                def share(n):
                    for i in part[:n]:
                        b = i // 6
                        slot = (P_ML + b + (q0 if isinstance(c, int) else par)) % 2
                        gemm_half(q0 + (P_ML + b), slot, *divmod(i % 6, 2), XA)
                    del part[:n]

                if h == 0:
                    pe.wait_ge(zc_in[par], (r + 1) * 16)
                if isinstance(c, int) and c == 0 and h == 0:
                    pe.wait_ge(row_v, 2)
                wait(pe, p_rdy, u)
                mm(px[0:L, 0, 0:L], z[:, h, 0:L], z[:, 4 + h, 0:L], start=True, stop=True)
                tok = slice(c * LC, c * LC + L) if isinstance(c, int) else bass.ds(c * LC, L)
                mm(px[:, 0, P:P + L], sel[:, h, :], rowR[:, tok], start=True, stop=True).then_inc(sr_rdy, 1)
                wait(pe, kv_rdy, u)
                nc.tensor.transpose(px[0:L, 1, 0:P], z[:, h, 0:L], ident[:, :])
                nc.tensor.transpose(px[0:L, 1, P:2 * P], z[:, 8 + 2 * h, 0:L], ident[:, :])
                nc.tensor.transpose(px[0:L, 1, 2 * P:3 * P], z[:, 9 + 2 * h, 0:L], ident[:, :]).then_inc(kvt_rdy, 1)
                share(2)
                pe.wait_ge(kv_rdy, u + 1)
                pe.wait_ge(p_rdy, u + 1)
                wait(pe, e_done, u)
                st = cst[:, 1 if smp else 0, h, :]
                mm(px[0:L, 2, 0:DV + 1], pt[0:L, 0:L], va[0:L, :], start=True, stop=False)
                mm(px[0:L, 2, 0:DV + 1], qg[:, 0:L], st, start=False, stop=True)
                mm(px[:, 3, 0:DV + 1], kw[0:L, :], va[0:L, :], start=True, stop=True).then_inc(nu_rdy, 1)
                share(1)
                if not (isinstance(c, int) and c == 0) and h in (1, 2):
                    ml_turn(c - 1, h - 1, LC)
                share(2)

            def ml_turn(c, b, L):
                if b == 0:
                    pe.wait_ge(hn_rdy, c + 1)
                wait(pe, ht_cp, c * 2 + b)
                for j in range(4):
                    last = nc.tensor.transpose(px[:, 4, j * P:j * P + L], hn[0:L, 2 * b + j // 2, (j % 2) * P:(j % 2) * P + P],
                                               ident[0:L, 0:L])
                last.then_inc(ht_rdy, 1)

            for c in range(2):
                for h in range(HB):
                    ml_unit(c, 0, c, h, LC)
            with pe.Fori(1, NLC // 2 - 1) as i:
                for par in range(2):
                    for h in range(HB):
                        ml_unit(i * 2 + par, i, par, h, LC)
            for c in range(NLC - 2, NLC):
                for h in range(HB):
                    ml_unit(c, NLC // 2 - 1, c % 2, h, LC)
            for h in range(HB):
                ml_unit(NLC, NLC // 2, 0, h, TS)

            def panels8(p0, rhs, first=0):
                with pe.Fori(first, KT // 2) as i:
                    for s in range(2):
                        for n in range(NT):
                            gemm(i * 2 + (p0 + s), (p0 + s) % 2, n, rhs)

            def gemm_first(p, rhs, ready):
                pe.wait_ge(w_ready, p + 1)
                for k in range(KT):
                    pe.wait_ge(ready, k + 1)
                    for j, (wi, xi) in enumerate(((0, 0), (0, 1), (1, 0))):
                        for n in range(NT):
                            if k == 0 and j == 0:
                                pe.wait_ge(acc_free[n], p)
                            last = mm(acc[:, n, 0:NW], whl[:, p % 2, wi, k * P:(k + 1) * P], rhs[:, xi, k, n * NW:(n + 1) * NW],
                                      start=(k == 0 and j == 0), stop=(k == KT - 1 and j == 2))
                            if k == 0 and j == 0 and n == 0:
                                last.then_inc(w_start, 1)
                            if k == KT - 1 and j == 2:
                                last.then_inc(acc_ready[n], 1)

            for n in range(NT):
                pe.wait_ge(ya_lo, KT * (n + 1))
                gemm(P_PA, P_PA % 2, n, XA)
            for b in range(2):
                ml_turn(NLC, b, TS)
            for n in range(NT):
                gemm(P_PA + 1, (P_PA + 1) % 2, n, XA)
            panels8(P_PA, XA, 1)
            gemm_first(P_PB, XB, yb_lo)
            for n in range(NT):
                gemm(P_PB + 1, (P_PB + 1) % 2, n, XB)
            panels8(P_PB, XB, 1)

            def ln_sum(ln):
                for q, ready, count in ((0, ln_s1, ln + 1), (1, sq_used, (KT - 1) * (ln + 1))):
                    pe.wait_ge(ready, count)
                    for c in range(NLC + 1):
                        L = LC if c < NLC else TS
                        last = mm(px[0:L, 3 + q, c:c + 1], lsum[:, q, c * LC:c * LC + L], ones[:, 0:1],
                                  start=True, stop=True, skip_group_check=True)
                last.then_inc(ln_squ, 1)

            def ln_spread(M, ln):
                pe.wait_ge(ln_dg, 2 * ln + 1)
                for n in range(NT):
                    mm(px[:, n, 0:NW], ones[:, :], ST[:, 0, n * NW:(n + 1) * NW], start=True, stop=True).then_inc(ln_r, 1)
                    if n == 0:
                        pe.wait_ge(ln_dg, 2 * ln + 2)
                    pe.wait_ge(acc_free[n], M)
                    mm(acc[:, n, 0:NW], ones[:, :], ST[:, 1, n * NW:(n + 1) * NW], start=True, stop=True).then_inc(acc_ready[n], 1)

            gemm_first(P_OUT, XA, mg_lo)
            for m in range(1, KT):
                for n in range(NT):
                    gemm(P_OUT + m, (P_OUT + m) % 2, n, XA)
            ln_sum(0)
            ln_spread(M_LN1, 0)

            def up(pi, M, i):
                pe.wait_ge(w_ready, pi + 1)
                for n in range(NT):
                    pe.wait_ge(acc_free[n], M)
                    for k in range(KT):
                        for j, (wi, xi) in enumerate(((0, 0), (0, 1), (1, 0))):
                            last = mm(acc[:, n, 0:NW], whl[:, i % 2, wi, k * P:(k + 1) * P], XA[:, xi, k, n * NW:(n + 1) * NW],
                                      start=(k == 0 and j == 0), stop=(k == KT - 1 and j == 2))
                            if n == 0 and k == 0 and j == 0:
                                last.then_inc(w_start, 1)
                    last.then_inc(acc_ready[n], 1)

            def down(pi, M, par, j):
                pe.wait_ge(fa_lo, j * 2 + 2)
                for m in range(KT):
                    s = m // 4
                    if m % 4 == 0:
                        pe.wait_ge(w_ready, pi + s + 1)
                    for n in range(NT):
                        pe.wait_ge(acc_free[n], M + m)
                        for k in range(2):
                            col = ((m % 4) * 2 + k) * P
                            for q, (wi, xi) in enumerate(((0, 0), (0, 1), (1, 0))):
                                last = mm(acc[:, n, 0:NW], whl[:, s, wi, col:col + P], fa[:, par, xi, k, n * NW:(n + 1) * NW],
                                          start=(k == 0 and q == 0), stop=(k == 1 and q == 2))
                                if m % 4 == 0 and n == 0 and k == 0 and q == 0:
                                    last.then_inc(w_start, 1)
                        last.then_inc(acc_ready[n], 1)

            for n in range(NT):
                pe.wait_ge(h2_lo, KT * (n + 1))
                for i in range(2):
                    if n == 0:
                        pe.wait_ge(w_ready, P_FFN + i + 1)
                    if i == 0:
                        pe.wait_ge(acc_free[n], M_FFN)
                    for k in range(KT):
                        for j, (wi, xi) in enumerate(((0, 0), (0, 1), (1, 0))):
                            last = mm((acc, px)[i][:, n, 0:NW], whl[:, i, wi, k * P:(k + 1) * P], XA[:, xi, k, n * NW:(n + 1) * NW],
                                      start=(k == 0 and j == 0), stop=(k == KT - 1 and j == 2))
                            if k == 0 and j == 0 and (i, n) in ((0, 0), (1, NT - 1)):
                                last.then_inc(w_start, 1)
                    last.then_inc(acc_ready[n], 1)
            for i in range(2, 4):
                up(P_FFN + i, M_FFN + i, i)

            def ffn_iter(j, par):
                for i in range(4):
                    up(j * 6 + (P_FFN - 2 + i), j * 12 + (M_FFN - 8 + i), i)
                down(j * 6 + (P_FFN + 2), j * 12 + (M_FFN - 4), 1 - par, j - 1)

            with pe.Fori(0, (FG - 1) // 2) as i:
                ffn_iter(i * 2 + 1, 1)
                ffn_iter(i * 2 + 2, 0)
            down(P_FFN + 6 * FG - 2, M_FFN + 12 * FG - 8, 0, FG - 1)
            ln_sum(1)
            ln_spread(M_LN2, 1)

        @block.scalar
        def _(act):
            A = nc.scalar.activation
            act.dma_start(small[:, :], io["small"]).then_inc(c_in, 16)
            act.dma_start(ident[:, :], io["ident"]).then_inc(c_in, 16)
            act.dma_start(ones[:, :], io["ones"]).then_inc(c_in, 16)
            act.wait_ge(c_in, 48)
            A(silu[:, 0, :, :], small[:, C_C:C_C + 16].rearrange("p (k s) -> p k s", s=2), ACT.Sigmoid).then_inc(sl_e, 1)
            for m in range(KT + 1):
                if m < KT:
                    act.wait_ge(ada_used, 2 * m + 2)
                    wait(act, ada_col, m - 1)
                    A(mrow[:, m % 2, :], px[0:2, 3, 0:2 * P], ACT.Copy).then_inc(ada_row, 1)
                if m >= 1:
                    act.wait_ge(h_tmp, m)
                    A(XA[:, 0, m - 1, :], ST[:, (m - 1) % 4, 0:T], ACT.Copy).then_inc(h_hi, 1)
            act.dma_start(sbc[:, :, :], io["c_bc"]).then_inc(cb_in, 16)
            for i in range(4):
                act.dma_start(adaT[:, i, :], io["w_adaT"][i]).then_inc(adaT_in[i], 16)
            act.wait_ge(ada_col, KT)
            act.dma_start(alibi[:, :, :], io["alibi"]).then_inc(kv_in, 16)
            act.dma_start(kk[:, :, TP:TP + WIN], io["k_cache"]).then_inc(kv_in, 16)
            act.dma_start(vv[:, TP:TP + WIN], io["v_cache"]).then_inc(kv_in, 16)

            def take(M, n, dsts, src=acc):
                act.wait_ge(acc_ready[n], M + 1)
                for dst, a, b in dsts:
                    last = A(dst, src[:, n, a:b], ACT.Copy)
                last.then_inc(acc_free[n], 1)
                return last

            def q_evac(m):
                for n in range(NT):
                    dst = XC[:, m, n * NW:(n + 1) * NW] if isinstance(m, int) else \
                        XC[:, bass.ds(m, 1), n * NW:(n + 1) * NW].rearrange("p o w -> p (o w)")
                    take(m, n, [(dst, 0, NW)], px if isinstance(m, int) and m == 1 else acc)

            def adaT_load(m, i):
                wait(act, adaT_used, m * 4 + i - 3)
                act.dma_start(adaT[:, i, :], io["w_adaT"][bass.ds(m * 4 + i, 1), :, :].rearrange("o p n -> p (o n)"))\
                   .then_inc(adaT_in[i], 16)

            act.wait_ge(cb_in, 16)
            act.wait_ge(h_lo, KT)
            A(adaT_tmp, sbc[:, :, :], ACT.Sigmoid).then_inc(sl_e, 1)
            q_evac(0)
            q_evac(1)
            for i in range(4):
                adaT_load(1, i)
            with act.Fori(2, KT) as m:
                q_evac(m)
                for i in range(4):
                    adaT_load(m, i)
            for p in range(KT, P_ATT):
                row = vv[:, :] if p == P_ATT - 1 else kk[:, p - KT, :]
                for n in range(NT):
                    dst = []
                    for a, b, s in pieces(n):
                        o = WIN * s
                        dst.append((row[:, a + o:b + o], a - n * NW, b - n * NW))
                    take(p, n, dst)
            act.drain().then_inc(qkv_ev, 1)

            def att_stage(c, par, w):
                smp = isinstance(c, int) and c == NCH
                qn = TS if smp else CH
                lo = TP if smp else None
                if isinstance(c, int):
                    qsl = slice(c * CH, c * CH + qn)
                    lo = TP if smp else (c + 1) * CH - w
                    bsl = slice(lo, lo + w)
                else:
                    qsl = bass.ds(c * CH, qn)
                    bsl = bass.ds(c * CH + (CH - w), w)
                wait(act, s_rdy, c * 2 - 2)
                for e in range(2):
                    A(qs[64 * e:64 * e + 64, par, :, 64 * e:64 * e + qn], XC[64 * e:64 * e + 64, :, qsl], ACT.Copy, scale=0.125)
                A(ks[:, par, :, 0:w], kk[:, :, bsl], ACT.Copy)
                A(vs[:, par, 0:w], vv[:, bsl], ACT.Copy).then_inc(st_rdy, 1)

            def att_exp(a, g, w):
                act.wait_ge(mx_rdy, a + 1)
                for j in range(4):
                    A(pb[:, g, j, 0:w], pb[:, g, j, 0:w], ACT.Exp, bias=nmx[:, g, j:j + 1], accum_out=rsum[:, g, j:j + 1])
                A(esk[:, g, :], esk[:, g, :], ACT.Exp).then_inc(ex_rdy, 1)

            def att_ptake(a, w, kb):
                act.wait_ge(tr_rdy, a + 1)
                wait(act, pv_rdy, a)
                if w > kb:
                    A(pta[0:w - kb, :, :], px[0:w - kb, 2, :].rearrange("p (j q) -> p j q", j=4), ACT.Copy)
                A(ptb[0:kb, :, :], px[0:kb, 3, :].rearrange("p (j q) -> p j q", j=4), ACT.Copy).then_inc(pt_rdy, 1)

            def spill_take(M, n, slot):
                act.wait_ge(acc_ready[n], M + 1)
                A(ST[:, slot, n * NW:(n + 1) * NW], acc[:, n, 0:NW], ACT.Copy).then_inc(acc_free[n], 1)

            def spill_free(slot, rounds):
                wait(act, sp_out[slot], rounds * 16)

            def spill_store(q, slot):
                act.drain().then_inc(sp_cp, 1)
                act.wait_ge(sp_cp, q + 1)
                act.dma_start(io["zs"][bass.ds(q, 1), :, :].rearrange("o p n -> p (o n)"), ST[:, slot, 0:T]).then_inc(sp_out[slot], 16)

            def att_chunk(c, r, par, w, wp, kbp, wn):
                kb = TS if isinstance(c, int) and c == NCH else CH
                if wp:
                    att_ptake(c * 2 - 1, wp, kbp)
                att_exp(c * 2, 0, w)
                spill_free(par, r)
                spill_take(c + P_ATT, 0, par)
                if wn:
                    att_stage(c + 1, 1 - par, wn)
                att_ptake(c * 2, w, kb)
                att_exp(c * 2 + 1, 1, w)
                spill_take(c + P_ATT, 1, par)
                spill_take(c + P_ATT, 2, par)
                spill_store(c, par)

            act.wait_ge(ada_ev, 1)
            att_stage(0, 0, CH)
            act.wait_ge(qkv_ev, 1)
            act.wait_ge(kv_in, 48)
            for j in range(2):
                for s, a in ((0, TP - WIN), (1, TP + TS)):
                    act.dma_start(io["k_out"][j, s], kk[0:64, j, a:a + WIN]).then_inc(kv_out, 16)
                    act.dma_start(io["v_out"][j, s], vv[64 * j:64 * j + 64, a:a + WIN]).then_inc(kv_out, 16)
            att_chunk(0, 0, 0, CH, 0, 0, 2 * CH)
            att_chunk(1, 0, 1, 2 * CH, CH, CH, BAND)
            act.wait_ge(sp_out[0], 16)
            act.dma_start(rowI, io["zs"][0, 0:HB, :]).then_inc(g_in, 16)
            act.dma_start(rowF, io["zs"][0, HB:2 * HB, :]).then_inc(g_in, 16)
            act.dma_start(rowE[:, :], io["rmask"]).then_inc(g_in, 16)
            att_chunk(2, 1, 0, BAND, 2 * CH, CH, BAND)
            act.wait_ge(g_in, 48)
            A(rowC[:, :], rowF, ACT.Abs, bias=small[0:HB, C_BF:C_BF + 1])
            act.drain()
            A(rowC[:, :], rowC[:, :], ACT.Exp, scale=-1.0).then_inc(row_a, 1)
            att_chunk(3, 1, 1, BAND, BAND, CH, BAND)
            with act.Fori(2, NCH // 2 - 1) as i:
                att_chunk(i * 2, i, 0, BAND, BAND, CH, BAND)
                att_chunk(i * 2 + 1, i, 1, BAND, BAND, CH, BAND)
            act.wait_ge(row_d, 1)
            A(rowD[:, :], rowD[:, :], ACT.Ln).then_inc(row_a, 1)
            att_chunk(NCH - 2, NCH // 2 - 1, 0, BAND, BAND, CH, BAND)
            att_chunk(NCH - 1, NCH // 2 - 1, 1, BAND, BAND, CH, WIN + TS)
            att_chunk(NCH, NCH // 2, 0, WIN + TS, BAND, CH, 0)
            att_ptake(2 * NCH + 1, WIN + TS, TS)

            act.wait_ge(o_used, 2 * NCH + 2)
            act.wait_ge(sp_out[0], 16 * 9)
            act.wait_ge(sp_out[1], 16 * 8)
            act.wait_ge(kv_out, 16 * 8)
            act.dma_start(sel[:, :, :], io["sel"]).then_inc(ml_in, 16)
            act.dma_start(cmask[:, :], io["cmask"]).then_inc(ml_in, 16)
            act.dma_start(cst[:, 1, :, :], io["c_state"]).then_inc(ml_in, 16)

            def load_chunk(c, par, L):
                tok = slice(c * LC, c * LC + L) if isinstance(c, int) else bass.ds(c * LC, L)
                act.dma_start(zc[:, par, :, 0:L], io["zs"][1:17, :, tok].rearrange("q p t -> p q t")).then_inc(zc_in[par], 16)

            def ml_spill(c, r, par, b, n):
                q0 = ml_part(c)[0]
                if isinstance(c, int):
                    slot = (Q_O + q0 + b) % 2
                    earlier = (Q_O + q0 + b) // 2
                else:
                    slot = (Q_O + par + b) % 2
                    earlier = r * PPC + (Q_O + PPC * par + b) // 2
                if n == 0:
                    spill_free(slot, earlier)
                spill_take(q0 + (P_ML + b), n, slot)
                if n == NT - 1:
                    spill_store(q0 + (Q_O + b), slot)

            load_chunk(0, 0, LC)
            for n in range(NT - 1):
                ml_spill(0, 0, 0, 0, n)
            act.wait_ge(row_v, 1)
            for c in range(NLC + 1):
                L = LC if c < NLC else TS
                A(em_c[0:L, c, :], em_c[0:L, c, :], ACT.Exp, scale=-1.0)
            act.drain().then_inc(row_v, 1)
            ml_spill(0, 0, 0, 0, NT - 1)

            def ya_round(n):
                act.wait_ge(acc_ready[n], P_PA)
                for k in range(KT):
                    A(XA[:, 0, k, n * NW:(n + 1) * NW], XC[:, k, n * NW:(n + 1) * NW], ACT.Copy).then_inc(ya_hi, 1)

            def ml_unit(c, r, par, h, L):
                u = c * 4 + h
                smp = isinstance(c, int) and c == NLC
                first = isinstance(c, int) and c == 0
                act.wait_ge(d_rdy, u + 1)
                A(wd[0:L, 0:L], wd[0:L, 0:L], ACT.Exp)
                bias = mp_c[:, h, c:c + 1] if isinstance(c, int) else mp_c[:, h, bass.ds(c, 1)]
                A(gb[:, 0:L], rs[:, 0:L], ACT.Exp, bias=bias).then_inc(wg_rdy, 1)
                act.wait_ge(wg_rdy, u + 1)
                A(wks[0:L, :], wd[0:L, L - 1:L], ACT.Copy, scale=KB_SCALE)
                act.wait_ge(kvt_rdy, u + 1)
                wait(act, nu_rdy, u)
                A(va[0:L, 0:DV], px[0:L, 1, P:3 * P], ACT.Copy)
                act.drain()
                A(kw[0:L, :], px[0:L, 1, 0:P], ACT.Copy, scale=wks[0:L, :]).then_inc(kv_rdy, 1)
                if h in (1, 2) and not first:
                    ml_turn(c - 1, h - 1, LC)
                if h == 1 and not smp:
                    wait(act, nu_rdy, c * 4)
                    load_chunk(c + 1, 1 - par, TS if isinstance(c, int) and c == NLC - 1 else LC)
                if smp and h == HB - 1:
                    ya_round(0)
                if h == 3:
                    act.wait_ge(var_rdy, c + 1)
                    A(rstd[0:L, :], rstd[0:L, :], ACT.Sqrt).then_inc(sd_rdy, 1)
                q0, cuts = ml_part(c)
                for i in range(cuts[h], cuts[h + 1]):
                    if i % 2:
                        ml_spill(c, r, par, i // 6, (i % 6) // 2)

            def ml_turn(c, b, L):
                act.wait_ge(ht_rdy, c * 2 + b + 1)
                if b == 0:
                    wait(act, hs_out, c * 16)
                A(hT[:, 4 * b:4 * b + 4, 0:L], px[:, 4, :].rearrange("p (j q) -> p j q", j=4)[:, :, 0:L], ACT.Copy).then_inc(ht_cp, 1)
                if b == 1:
                    act.wait_ge(ht_cp, c * 2 + 2)
                    tok = slice(c * LC, c * LC + L) if isinstance(c, int) else bass.ds(c * LC, L)
                    act.dma_start(io["hs"][:, :, tok].rearrange("j p t -> p j t"), hT[:, :, 0:L]).then_inc(hs_out, 16)

            act.wait_ge(row_v, 3)
            for c in range(2):
                for h in range(HB):
                    ml_unit(c, 0, c, h, LC)
            with act.Fori(1, NLC // 2 - 1) as i:
                for par in range(2):
                    for h in range(HB):
                        ml_unit(i * 2 + par, i, par, h, LC)
            for c in range(NLC - 2, NLC):
                for h in range(HB):
                    ml_unit(c, NLC // 2 - 1, c % 2, h, LC)
            for h in range(HB):
                ml_unit(NLC, NLC // 2, 0, h, TS)
            def load_gate(q0, m, s, used):
                wait(act, gt_used, used)
                act.dma_start(ST[:, 2 + s, 0:T], io["zs"][q0 + m]).then_inc(gt_in[s], 16)

            ya_round(1)
            act.wait_ge(sp_out[0], 16 * (Q_GA // 2 + 1))
            act.wait_ge(sp_out[1], 16 * (Q_GA // 2 + 1))
            for m in range(2):
                load_gate(Q_GA, m, m, 0)
            ya_round(2)
            for m in range(2):
                act.wait_ge(gt_in[m], 16)
                A(ST[:, 2 + m, 0:T], ST[:, 2 + m, 0:T], ACT.Sigmoid).then_inc(gt_rdy, 1)
            for b in range(2):
                ml_turn(NLC, b, TS)
            act.wait_ge(e_done, 4 * NLC + 4)
            act.dma_start(io["c_out"].rearrange("s p h v -> p s h v"), cst[:, :, :, :]).then_inc(st_out, 16)
            act.dma_start(io["m_out"][0], rowM[:, TP - 1:TP]).then_inc(st_out, 16)
            act.dma_start(io["m_out"][1], rowM[:, T - 1:T]).then_inc(st_out, 16)

            act.wait_ge(sp_out[0], 16 * ((N_SPILL + 1) // 2))
            act.wait_ge(sp_out[1], 16 * (N_SPILL // 2))
            act.wait_ge(hs_out, 16 * (NLC + 1))
            act.wait_ge(ya_lo, NT * KT)

            def load_yb(m):
                wait(act, yb_lo, m - 1)
                act.dma_start(yb_stage(m)[0], io["zs"][Q_O + m]).then_inc(og_in[m % 2], 16)
                act.dma_start(yb_stage(m)[1], io["hs"][m]).then_inc(hn_in[m % 2], 16)

            load_yb(0)
            load_yb(1)
            act.wait_ge(st_out, 48)
            for kind, m in BRANCH_ORDER:
                if kind == "a":
                    if m >= 2:
                        act.wait_ge(gt_in[m % 2], 16 * (m // 2 + 1))
                        A(ST[:, 2 + m % 2, 0:T], ST[:, 2 + m % 2, 0:T], ACT.Sigmoid).then_inc(gt_rdy, 1)
                elif kind == "g":
                    load_gate(Q_GA, m, m % 2, m - 1)
                else:
                    act.wait_ge(og_in[m % 2], 16 * (m // 2 + 1))
                    A(yb_stage(m)[0], yb_stage(m)[0], ACT.Sigmoid).then_inc(sg_rdy, 1)
                    act.wait_ge(yb_rdy, m + 1)
                    A(XB[:, 0, m, :], yb_stage(m)[0], ACT.Copy).then_inc(yb_hi, 1)
                    if m + 2 < KT:
                        load_yb(m + 2)
            for m in range(2):
                load_gate(Q_GB, m, m, KT - 1 + m)
            for m in range(KT):
                act.wait_ge(gt_in[m % 2], 16 * (4 + m // 2 + 1))
                A(ST[:, 2 + m % 2, 0:T], ST[:, 2 + m % 2, 0:T], ACT.Sigmoid).then_inc(gt_rdy, 1)
                act.wait_ge(mg_rdy, m + 1)
                A(XA[:, 0, m, :], ST[:, 0, 0:T], ACT.Copy).then_inc(mg_hi, 1)
                if m + 2 < KT:
                    load_gate(Q_GB, m + 2, m % 2, KT + m + 1)
            def squares(ln, k):
                act.wait_ge(r_rdy, KT * ln + k + 1)
                if k >= 2:
                    act.wait_ge(sq_used, (KT - 1) * ln + max(1, k - 2))
                A(ST[:, k % 2, 0:T], XC[:, k, :], ACT.Square).then_inc(ln_sq, 1)

            act.wait_ge(mg_lo, KT)
            for m in range(KT):
                wait(act, gt_used, 2 * KT if m < 2 else 0)
                if m >= 2:
                    squares(0, m - 2)
                act.dma_start(ST[:, 2 + m % 2, 0:T], io["x"][:, m, :]).then_inc(xr_in[m % 2], 16)
            squares(0, KT - 2)
            squares(0, KT - 1)

            def ln_sqrt(ln):
                act.wait_ge(ln_v, ln + 1)
                A(lst[:, 2, :], lst[:, 2, :], ACT.Sqrt).then_inc(ln_s, 1)

            ln_sqrt(0)
            act.dma_start(fc[:, :, :, :], io["ffn_consts"]).then_inc(fc_in, 16)
            for n in range(NT):
                for k in range(KT):
                    q = n * KT + k
                    act.wait_ge(ln_t, q // 2 + 1)
                    if q == 6:
                        act.wait_ge(acc_ready[NT - 1], M_LN1 + 1)
                    if k % 4 != 3:
                        if q >= 12:
                            act.wait_ge(h2_lo, q - 11)
                        for a, b, s in pieces(n):
                            A(hslot(q)[:, a - n * NW:b - n * NW], XC[:, k, a:b], ACT.Identity, scale=der[:, s, k:k + 1],
                              bias=der[:, 2 + s, k:k + 1])
                    for a, b, s in pieces(n):
                        last = A(XA[:, 0, k, a:b], XC[:, k, a:b], ACT.Identity, scale=der[:, s, k:k + 1],
                                 bias=der[:, 2 + s, k:k + 1])
                    last.then_inc(h2_hi, 1)

            def fgroup(j):
                return fc[:, j, :, :] if isinstance(j, int) else fc[:, bass.ds(j, 1), :, :].rearrange("p o a b -> p (o a) b")

            def ffn_up(j, M, par, i):
                src = px if isinstance(j, int) and j == 0 and i == 1 else acc
                wait(act, cv_d, j * 4 + i - 3)
                A(ub[:, i, TP + 2:TP + 4], fca[:, i, 5:7], ACT.Copy)
                for n in range(NT):
                    act.wait_ge(acc_ready[n], M + 1)
                    for a, b, s in pieces(n):
                        last = A(ub[:, i, 2 + a + 2 * s:2 + b + 2 * s], src[:, n, a - n * NW:b - n * NW], ACT.Identity,
                                 bias=fca[:, i, 0:1])
                    last.then_inc(acc_free[n], 1)
                act.drain().then_inc(u_rdy, 1)
                wait(act, fa_lo, j * 2)
                A(ST[:, i, 0:CW], ub[:, i, 2:UW], ACT.Identity, scale=fca[:, i, 3:4], bias=fca[:, i, 4:5]).then_inc(cv_a, 1)

            def ffn_gelu(j, i):
                act.wait_ge(cv_d, j * 4 + i + 1)
                A(ST[:, i, 0:CW], ST[:, i, 0:CW], ACT.Gelu_apprx_tanh).then_inc(gl_rdy, 1)

            def ffn_round(j, par):
                for t in range(2):
                    act.wait_ge(pr_rdy, j * 2 + t + 1)
                    A(fa[:, par, 0, t, 0:TP], ST[:, t, 0:TP], ACT.Copy)
                    A(fa[:, par, 0, t, TP:T], ST[:, t, TP + 2:CW], ACT.Copy).then_inc(fa_hi, 1)

            def ffn_group(j, M, par):
                A(fca[:, :, :], fgroup(j), ACT.Copy)
                act.drain()
                for i in range(4):
                    ffn_up(j, M + i, par, i)
                    if i == 3:
                        ffn_gelu(j, 2)
                ffn_gelu(j, 3)
                ffn_round(j, par)

            act.wait_ge(fc_in, 16)
            act.wait_ge(h2_lo, NT * KT)
            ffn_group(0, M_FFN, 0)
            with act.Fori(0, (FG - 1) // 2) as i:
                ffn_group(i * 2 + 1, i * 24 + (M_FFN + 4), 1)
                ffn_group(i * 2 + 2, i * 24 + (M_FFN + 16), 0)
            act.wait_ge(cs_out, 1)
            act.dma_start(io["cs_out"], cs[:, :, :, :]).then_inc(cs_out, 16)
            for k in range(KT):
                squares(1, k)
            ln_sqrt(1)
            for n in range(NT):
                act.wait_ge(acc_ready[n], M_LN2 + 1)
                A(lsum[:, 1, n * NW:(n + 1) * NW], acc[:, n, 0:NW], ACT.Copy).then_inc(ln_bn, 1)
            for n in range(NT):
                for i, (a, b) in enumerate(zip(LN2_CUTS[0:3], LN2_CUTS[1:4])):
                    if i < 2:
                        act.wait_ge(ln_t, LN1_STEPS + 2 * n + i + 1)
                    else:
                        act.wait_ge(ln_p, n + 1)
                    for k in range(a, b):
                        part = XC[:, k, n * NW:(n + 1) * NW]
                        last = A(part, part, ACT.Identity, scale=small[:, C_L2W + k:C_L2W + k + 1],
                                 bias=small[:, C_L2B + k:C_L2B + k + 1])
                    last.then_inc(y_rdy, 1)
            act.wait_ge(cs_out, 17)

        @block.vector
        def _(dve):
            V = nc.vector
            V.memset(lst[:, :, :], 1.0)
            dve.wait_ge(c_in, 48)
            dve.wait_ge(sl_e, 1)
            V.tensor_tensor(silu[:, 1, :, :], silu[:, 0, :, :], small[:, C_C:C_C + 16].rearrange("p (k s) -> p k s", s=2),
                            ALU.mult).then_inc(sl_d, 1)
            bada = small[:, C_BADA:C_BADA + 48].rearrange("p (i m) -> p i m", i=6)
            V.tensor_copy(der[:, 0, :], bada[:, 0, :])
            V.tensor_scalar(der[:, 1, :], bada[:, 1, :], 1.0, None, ALU.add)
            dve.drain()

            def h_low(k):
                dve.wait_ge(h_hi, k + 1)
                V.tensor_tensor(XA[:, 1, k, :], ST[:, k % 4, 0:T], XA[:, 0, k, :].bitcast(F32), ALU.subtract).then_inc(h_lo, 1)

            for m in range(KT):
                dve.wait_ge(ada_col, m + 1)
                V.tensor_tensor(mod[:, 0:2, m, :], px[:, 4, 0:4].rearrange("p (i s) -> p i s", i=2),
                                der[:, 0:2, m:m + 1].to_broadcast([P, 2, 2]), ALU.add).then_inc(ada_mod, 1)
                dve.drain()
                dve.wait_ge(x_in[m], 16)
                for a, b, s in ((0, TP, 0), (TP, T, 1)):
                    last = V.tensor_scalar(ST[:, m % 4, a:b], XC[:, m, a:b], mod[:, 1, m, s:s + 1], mod[:, 0, m, s:s + 1],
                                           ALU.mult, ALU.add)
                last.then_inc(h_tmp, 1)
                h_low(m)
            dve.wait_ge(sl_e, 2)
            V.tensor_tensor(sbc[:, :, :], sbc[:, :, :], adaT_tmp, ALU.mult)
            dve.drain()
            modf = mod[:, :, :, :].rearrange("p i m s -> p (i m) s")

            def ada_four(m):
                for i in range(4):
                    dve.wait_ge(adaT_in[i], (m + 1) * 16)
                    for s in range(2):
                        V.tensor_tensor_reduce(adaT_tmp[:, s, :], adaT[:, i, :], sbc[:, s, :], 1.0, 0.0, ALU.mult, ALU.add,
                                                      ast[:, i, s:s + 1])
                    dve.drain().then_inc(adaT_used, 1)
                at4 = slice(16 + 4 * m, 20 + 4 * m) if isinstance(m, int) else bass.ds(m * 4 + 16, 4)
                bt4 = slice(C_BADA + 16 + 4 * m, C_BADA + 20 + 4 * m) if isinstance(m, int) else bass.ds(m * 4 + (C_BADA + 16), 4)
                V.tensor_tensor(modf[:, at4, :], ast[:, :, :], small[:, bt4].unsqueeze(2).to_broadcast([P, 4, 2]), ALU.add)
                dve.drain()

            ada_four(0)
            with dve.Fori(1, KT) as m:
                ada_four(m)
            V.tensor_scalar(mod[:, 4, :, :], mod[:, 4, :, :], 1.0, None, ALU.add)
            V.memset(qs[:, :, :, :], 0.0)
            dve.drain().then_inc(ada_ev, 1)
            for k in range(KT):
                w, b = small[:, C_L1W + k:C_L1W + k + 1], small[:, C_L1B + k:C_L1B + k + 1]
                for s in range(2):
                    V.tensor_scalar(der[:, s, k:k + 1], w, mod[:, 4, k, s:s + 1], None, ALU.mult)
                    V.tensor_scalar(der[:, 2 + s, k:k + 1], b, mod[:, 4, k, s:s + 1], mod[:, 3, k, s:s + 1], ALU.mult, ALU.add)
            V.tensor_scalar(der[:, 4, :], small[:, C_L1W:C_L1W + KT], ALPHA, None, ALU.mult)
            V.tensor_scalar(der[:, 5, :], small[:, C_L1B:C_L1B + KT], ALPHA, None, ALU.mult)
            dve.drain()

            def att_max(c, a, par, g, w, kb):
                dve.wait_ge(s_rdy, a + 1)
                wait(dve, tr_rdy, a - 1)
                for b in range(2):
                    V.tensor_tensor(pb[:, g, 2 * b:2 * b + 2, 0:w],
                                    px[:, b, 0:2 * BAND].rearrange("p (j w) -> p j w", j=2)[:, :, 0:w],
                                    alibi[:, 4 * g + 2 * b:4 * g + 2 * b + 2, alo(c, w):alo(c, w) + w], ALU.add)
                if g == 0:
                    wait(dve, pv_rdy, a - 2)
                    if w > kb:
                        V.tensor_copy(vt[0:w - kb, par, 0, :], px[0:w - kb, 0, 384:512])
                    V.tensor_copy(vt[0:kb, par, 1, :], px[0:kb, 1, 384:512])
                dve.drain().then_inc(s_used, 1)
                V.tensor_reduce(nmx[:, g, :], pb[:, g, :, 0:w], AX.X, ALU.max)
                dve.drain()
                V.tensor_tensor(nmx[:, g, :], nmx[:, g, :], small[:, C_SINK + 4 * g:C_SINK + 4 * g + 4], ALU.max)
                dve.drain()
                V.tensor_scalar(nmx[:, g, :], nmx[:, g, :], -1.0, None, ALU.mult)
                dve.drain()
                V.tensor_tensor(esk[:, g, :], nmx[:, g, :], small[:, C_SINK + 4 * g:C_SINK + 4 * g + 4], ALU.add).then_inc(mx_rdy, 1)

            def alo(c, w):
                return 0 if isinstance(c, int) and c == NCH else BAND - w

            def att_norm(a, g, w):
                dve.wait_ge(ex_rdy, a + 1)
                V.tensor_tensor(rden[:, :], rsum[:, g, :], esk[:, g, :], ALU.add)
                dve.drain()
                V.reciprocal(rden[:, :], rden[:, :])
                dve.drain()
                V.tensor_tensor(pb[:, g, :, 0:w], pb[:, g, :, 0:w], rden[:, :].unsqueeze(2).to_broadcast([P, 4, w]), ALU.mult)\
                 .then_inc(pn_rdy, 1)

            def att_take(c, a, g):
                dve.wait_ge(pv_rdy, a + 1)
                n = TS if isinstance(c, int) and c == NCH else CH
                tok = slice(c * CH, c * CH + n) if isinstance(c, int) else bass.ds(c * CH, n)
                V.tensor_copy(XC[:, 4 * g:4 * g + 4, tok], px[:, 4, 0:4 * CH].rearrange("p (j q) -> p j q", j=4)[:, :, 0:n])\
                 .then_inc(o_used, 1)

            def att_chunk(c, par, w, wp):
                kb = TS if isinstance(c, int) and c == NCH else CH
                att_max(c, c * 2, par, 0, w, kb)
                if wp:
                    att_take(c - 1, c * 2 - 1, 1)
                att_norm(c * 2, 0, w)
                att_max(c, c * 2 + 1, par, 1, w, kb)
                att_take(c, c * 2, 0)
                att_norm(c * 2 + 1, 1, w)

            dve.wait_ge(kv_in, 48)
            att_chunk(0, 0, CH, 0)
            att_chunk(1, 1, 2 * CH, CH)
            att_chunk(2, 0, BAND, 2 * CH)
            att_chunk(3, 1, BAND, BAND)
            dve.wait_ge(row_a, 1)
            V.tensor_scalar(rowD[:, :], rowC[:, :], 1.0, None, ALU.add)
            V.tensor_scalar(rowF, rowF, small[0:HB, C_BF:C_BF + 1], 0.0, ALU.add, ALU.min)
            V.tensor_scalar(rowI, rowI, small[0:HB, C_BI:C_BI + 1], None, ALU.add)
            dve.drain()
            V.tensor_scalar(rowR[:, :], rowD[:, :], -1.0, None, ALU.add).then_inc(row_d, 1)
            dve.drain()
            V.tensor_tensor(rowC[:, :], rowC[:, :], rowR[:, :], ALU.subtract)
            with dve.Fori(2, NCH // 2) as i:
                att_chunk(i * 2, 0, BAND, BAND)
                att_chunk(i * 2 + 1, 1, BAND, BAND)
            dve.wait_ge(row_a, 2)
            dve.drain()
            V.tensor_tensor(rowC[:, :], rowC[:, :], rowD[:, :], ALU.add)
            dve.drain()
            V.tensor_tensor(rowF, rowF, rowC[:, :], ALU.subtract)
            dve.drain()
            V.tensor_tensor_scan(rowD[:, :], rowE[:, :], rowF, 0.0, ALU.mult, ALU.add)
            V.tensor_tensor_scan(rowM[:, 0:TP], rowF[:, 0:TP], rowI[:, 0:TP], 0.0, ALU.add, ALU.max)
            V.tensor_tensor_scan(rowM[:, TP:T], rowF[:, TP:T], rowI[:, TP:T], small[0:HB, C_M0:C_M0 + 1], ALU.add, ALU.max)
            att_chunk(NCH, 0, WIN + TS, BAND)
            V.tensor_tensor(rowC[:, :], rowI, rowD[:, :], ALU.subtract)
            V.tensor_tensor(rowR[:, :], rowD[:, :], rowM[:, :], ALU.subtract)
            att_take(NCH, 2 * NCH + 1, 1)
            V.memset(mprow[:, 0:1], 0.0)
            V.tensor_copy(mprow[:, NLC:NLC + 1], small[0:HB, C_M0:C_M0 + 1])
            V.memset(va[:, DV:DV + 1], 1.0)
            V.memset(cst[:, 0, :, :], 0.0)
            dve.drain()
            V.tensor_copy(mprow[:, 1:NLC], rowM[:, 0:TP].rearrange("p (c l) -> p c l", l=LC)[:, 0:NLC - 1, LC - 1])
            dve.drain().then_inc(row_d, 1)
            dve.wait_ge(row_p, 1)
            dve.wait_ge(ml_in, 48)
            for c0, c1, L in ((0, NLC, LC), (NLC, NLC + 1, TS)):
                V.tensor_copy(at_c[0:L, c0:c1, :], px[0:L, 0, 4 * c0:4 * c1].rearrange("p (c h) -> p c h", h=HB))
                V.tensor_copy(em_c[0:L, c0:c1, :], px[0:L, 0, 64 + 4 * c0:64 + 4 * c1].rearrange("p (c h) -> p c h", h=HB))
            V.tensor_copy(mp_c[:, :, :], px[:, 0, 128:164].rearrange("p (h c) -> p h c", h=HB))
            dve.drain().then_inc(row_v, 1)
            dve.wait_ge(row_v, 2)
            dve.drain().then_inc(row_v, 1)

            def ya_low(n):
                cols = slice(n * NW, (n + 1) * NW)
                for k in range(KT):
                    dve.wait_ge(ya_hi, n * KT + k + 1)
                    V.tensor_tensor(XA[:, 1, k, cols], XC[:, k, cols], XA[:, 0, k, cols].bitcast(F32), ALU.subtract)\
                     .then_inc(ya_lo, 1)

            def ml_unit(c, par, h, L):
                u = c * 4 + h
                ci = c if isinstance(c, int) else None

                def col(t, n=L):
                    return t[0:n, c, h:h + 1] if ci is not None else \
                        t[0:n, bass.ds(c, 1), h:h + 1].rearrange("p a b -> p (a b)")

                dve.wait_ge(sr_rdy, u + 1)
                V.tensor_copy(rs[:, 0:L], px[:, 0, P:P + L])
                dve.drain()
                V.scalar_tensor_tensor(wd[0:L, 0:L], rs[0:L, 0:L], col(at_c), cmask[0:L, 0:L], ALU.add, ALU.add).then_inc(d_rdy, 1)
                dve.wait_ge(wg_rdy, u + 1)
                V.scalar_tensor_tensor(pt[0:L, 0:L], px[0:L, 0, 0:L], KB_SCALE, wd[0:L, 0:L], ALU.mult, ALU.mult)
                V.tensor_tensor(qg[:, 0:L], zc[:, par, 4 + h, 0:L], gb[:, 0:L], ALU.mult)
                dve.drain().then_inc(p_rdy, 1)
                if h == 0 and ci != 0:
                    ml_norm(c - 1, LC)
                if ci == NLC and h == HB - 1:
                    ya_low(0)
                dve.wait_ge(nu_rdy, u + 1)
                s = 1 if ci == NLC else 0
                V.scalar_tensor_tensor(cst[:, s, h, :], cst[:, s, h, :], gb[:, L - 1:L], px[:, 3, 0:DV + 1], ALU.mult, ALU.add)
                V.tensor_scalar(dn[0:L, 0:1], px[0:L, 2, DV:DV + 1], -1.0, col(em_c), ALU.mult, ALU.max)
                dve.drain()
                V.tensor_tensor(dn[0:L, 0:1], dn[0:L, 0:1], px[0:L, 2, DV:DV + 1], ALU.max)
                dve.drain()
                V.reciprocal(dn[0:L, 1:2], dn[0:L, 0:1])
                dve.drain()
                V.tensor_scalar(hh[0:L, h, :], px[0:L, 2, 0:DV], dn[0:L, 1:2], None, ALU.mult)
                dve.drain().then_inc(e_done, 1)
                V.bn_stats(bst[0:L, h, :], hh[0:L, h, :])
                dve.drain()
                V.bn_aggr(mv[0:L, h, :], bst[0:L, h, :])
                if h == HB - 1:
                    dve.drain()
                    V.tensor_scalar(rstd[0:L, :], mv[0:L, :, 1], EPS, None, ALU.add).then_inc(var_rdy, 1)

            def ml_norm(c, L):
                dve.wait_ge(sd_rdy, c + 1)
                wait(dve, ht_rdy, c * 2)
                V.reciprocal(rstd[0:L, :], rstd[0:L, :])
                dve.drain()
                for h in range(HB):
                    last = V.tensor_scalar(hn[0:L, h, :], hh[0:L, h, :], mv[0:L, h, 0:1], rstd[0:L, h:h + 1],
                                           ALU.subtract, ALU.mult)
                dve.drain().then_inc(hn_rdy, 1)

            for c in range(2):
                for h in range(HB):
                    ml_unit(c, c, h, LC)
            with dve.Fori(1, NLC // 2) as i:
                for par in range(2):
                    for h in range(HB):
                        ml_unit(i * 2 + par, par, h, LC)
            for h in range(HB):
                ml_unit(NLC, 0, h, TS)
            for n in range(1, NT):
                ya_low(n)
            ml_norm(NLC, TS)

            dve.drain()
            for kind, m in BRANCH_ORDER:
                if kind == "a":
                    dve.wait_ge(gt_rdy, m + 1)
                    if m == KT - 2:
                        dve.wait_ge(yb_lo, KT)
                    for n in range(NT):
                        dve.wait_ge(acc_ready[n], P_PA + m + 1)
                        V.tensor_tensor(XC[:, m, n * NW:(n + 1) * NW], acc[:, n, 0:NW], ST[:, 2 + m % 2, n * NW:(n + 1) * NW],
                                        ALU.mult).then_inc(acc_free[n], 1)
                    dve.drain().then_inc(gt_used, 1)
                elif kind == "y":
                    og, hn_m = yb_stage(m)
                    dve.wait_ge(hn_in[m % 2], 16 * (m // 2 + 1))
                    dve.wait_ge(sg_rdy, m + 1)
                    V.scalar_tensor_tensor(og, og, small[:, C_NW + m:C_NW + m + 1], hn_m, ALU.mult, ALU.mult).then_inc(yb_rdy, 1)
                    dve.wait_ge(yb_hi, m + 1)
                    V.tensor_tensor(XB[:, 1, m, :], og, XB[:, 0, m, :].bitcast(F32), ALU.subtract).then_inc(yb_lo, 1)
            for m in range(KT):
                dve.wait_ge(gt_rdy, KT + m + 1)
                for n in range(NT):
                    dve.wait_ge(acc_ready[n], P_PB + m + 1)
                    V.tensor_tensor(ST[:, 0, n * NW:(n + 1) * NW], acc[:, n, 0:NW], ST[:, 2 + m % 2, n * NW:(n + 1) * NW], ALU.mult)\
                     .then_inc(acc_free[n], 1)
                dve.drain().then_inc(gt_used, 1)
                V.tensor_tensor(ST[:, 0, 0:T], ST[:, 0, 0:T], XC[:, m, :], ALU.add).then_inc(mg_rdy, 1)
                dve.wait_ge(mg_hi, m + 1)
                V.tensor_tensor(XA[:, 1, m, :], ST[:, 0, 0:T], XA[:, 0, m, :].bitcast(F32), ALU.subtract).then_inc(mg_lo, 1)
                dve.drain()
            def ln_add(k):
                last = V.tensor_tensor(lsum[:, 0, :], XC[:, 0, :] if k == 1 else lsum[:, 0, :], XC[:, k, :], ALU.add)
                if k == KT - 1:
                    last.then_inc(ln_s1, 1)

            def ln_add_square(ln, k):
                dve.wait_ge(ln_sq, KT * ln + k + 1)
                V.tensor_tensor(lsum[:, 1, :], ST[:, 0, 0:T] if k == 1 else lsum[:, 1, :], ST[:, k % 2, 0:T], ALU.add)\
                 .then_inc(sq_used, 1)

            for m in range(KT):
                if m >= 2:
                    ln_add(m - 1)
                    ln_add_square(0, m - 1)
                dve.wait_ge(xr_in[m % 2], 16 * (m // 2 + 1))
                V.tensor_scalar(ST[:, 2 + m % 2, 0:T], ST[:, 2 + m % 2, 0:T], ALPHA, None, ALU.mult)
                dve.drain()
                for n in range(NT):
                    dve.wait_ge(acc_ready[n], P_OUT + m + 1)
                    for a, b, s in pieces(n):
                        last = V.scalar_tensor_tensor(XC[:, m, a:b], acc[:, n, a - n * NW:b - n * NW], mod[:, 2, m, s:s + 1],
                                                      ST[:, 2 + m % 2, a:b], ALU.mult, ALU.add)
                    last.then_inc(acc_free[n], 1)
                dve.drain().then_inc(r_rdy, 1)
            ln_add(KT - 1)
            ln_add_square(0, KT - 1)

            def ln_scales(ln):
                dve.wait_ge(ln_squ, ln + 1)
                for q in range(2):
                    V.tensor_copy(lst[:, q, 0:NLC], px[:, 3 + q, 0:NLC])
                    V.tensor_copy(lst[0:TS, q, NLC:NLC + 1], px[0:TS, 3 + q, NLC:NLC + 1])
                dve.drain()
                V.tensor_tensor(lst[:, 2, :], lst[:, 0, :], lst[:, 0, :], ALU.mult)
                dve.drain()
                V.tensor_tensor(lst[:, 2, :], lst[:, 1, :], lst[:, 2, :], ALU.subtract)
                dve.drain()
                V.tensor_scalar(lst[:, 2, :], lst[:, 2, :], 0.0, EPS, ALU.max, ALU.add)
                dve.drain()
                V.reciprocal(lst[:, 2, :], lst[:, 2, :]).then_inc(ln_v, 1)
                dve.wait_ge(ln_s, ln + 1)
                V.tensor_scalar(lst[:, 3, :], lst[:, 2, :], float(D), None, ALU.mult)
                dve.drain()
                V.scalar_tensor_tensor(lst[:, 4, :], lst[:, 0, :], -1.0, lst[:, 3, :], ALU.mult, ALU.mult)
                dve.drain()
                for q in range(2):
                    V.tensor_tensor(ST[:, q, 0:TP].rearrange("p (c l) -> p c l", c=NLC),
                                    ident[:, :].unsqueeze(1).to_broadcast([P, NLC, LC]),
                                    lst[:, 3 + q, 0:NLC].unsqueeze(2).to_broadcast([P, NLC, LC]), ALU.mult)
                    V.tensor_scalar(ST[:, q, TP:T], ident[:, 0:TS], lst[:, 3 + q, NLC:NLC + 1], None, ALU.mult)\
                     .then_inc(ln_dg, 1)

            ln_scales(0)

            for q in range(0, NT * KT, 2):
                n, k = divmod(q, KT)
                cols = slice(n * NW, (n + 1) * NW)
                if k == 0:
                    dve.wait_ge(ln_r, n + 1)
                    dve.wait_ge(acc_ready[n], M_LN1 + 1)
                pair = XC[:, k:k + 2, cols]
                V.tensor_tensor(pair, pair, px[:, n:n + 1, 0:NW].to_broadcast([P, 2, NW]), ALU.mult)
                dve.drain()
                V.tensor_tensor(pair, pair, acc[:, n:n + 1, 0:NW].to_broadcast([P, 2, NW]), ALU.add).then_inc(ln_t, 1)
                if k == KT - 2:
                    dve.drain().then_inc(acc_free[n], 1)
                if k % 4 == 2:
                    dve.drain()
                    if q == 6:
                        dve.wait_ge(acc_ready[NT - 1], M_LN1 + 1)
                    if q + 1 >= 12:
                        dve.wait_ge(h2_lo, q - 10)
                    for a, b, s in pieces(n):
                        last = V.tensor_scalar(hslot(q + 1)[:, a - n * NW:b - n * NW], XC[:, k + 1, a:b], der[:, s, k + 1:k + 2],
                                               der[:, 2 + s, k + 1:k + 2], ALU.mult, ALU.add)
                    last.then_inc(h2_d, 1)
            dve.wait_ge(h2_hi, NT * KT)
            dve.wait_ge(h2_d, NT * KT // 4)
            for k in range(KT):
                V.tensor_scalar(XC[:, k, :], XC[:, k, :], der[:, 4, k:k + 1], der[:, 5, k:k + 1], ALU.mult, ALU.add)

            def fgroup(j):
                return fc[:, j, :, :] if isinstance(j, int) else fc[:, bass.ds(j, 1), :, :].rearrange("p o a b -> p (o a) b")

            def cout(j, i, a):
                return cs[:, j, i, a:a + 2] if isinstance(j, int) else \
                    cs[:, bass.ds(j, 1), i, a:a + 2].rearrange("p a b -> p (a b)")

            def ffn_conv(j, i, split=False):
                dve.wait_ge(u_rdy, j * 4 + i + 1)
                V.tensor_copy(cout(j, i, 0), ub[:, i, TP:TP + 2])
                V.tensor_copy(cout(j, i, 2), ub[:, i, UW - 2:UW])
                dve.wait_ge(cv_a, j * 4 + i + 1)
                V.scalar_tensor_tensor(ST[:, i, 0:CW], ub[:, i, 0:CW], fcd[:, i, 1:2], ST[:, i, 0:CW], ALU.mult, ALU.add)
                dve.drain()
                if not split:
                    ffn_conv_end(i)

            def ffn_conv_end(i):
                V.scalar_tensor_tensor(ST[:, i, 0:CW], ub[:, i, 1:CW + 1], fcd[:, i, 2:3], ST[:, i, 0:CW], ALU.mult, ALU.add)\
                 .then_inc(cv_d, 1)

            def ffn_prod(j, t):
                dve.wait_ge(gl_rdy, j * 2 + t + 1)
                V.tensor_tensor(ST[:, t, 0:CW], ST[:, t, 0:CW], ST[:, 2 + t, 0:CW], ALU.mult).then_inc(pr_rdy, 1)

            def ffn_low(j, par, t):
                dve.wait_ge(fa_hi, j * 2 + t + 1)
                V.tensor_tensor(fa[:, par, 1, t, 0:TP], ST[:, t, 0:TP], fa[:, par, 0, t, 0:TP].bitcast(F32), ALU.subtract)
                V.tensor_tensor(fa[:, par, 1, t, TP:T], ST[:, t, TP + 2:CW], fa[:, par, 0, t, TP:T].bitcast(F32), ALU.subtract)
                dve.drain().then_inc(fa_lo, 1)

            def ffn_take(M, m):
                for n in range(NT):
                    dve.wait_ge(acc_ready[n], M + m + 1)
                    for a, b, s in pieces(n):
                        last = V.scalar_tensor_tensor(XC[:, m, a:b], acc[:, n, a - n * NW:b - n * NW], mod[:, 5, m, s:s + 1],
                                                      XC[:, m, a:b], ALU.mult, ALU.add)
                    last.then_inc(acc_free[n], 1)

            def ffn_iter(j, par, M):
                V.tensor_copy(fcd[:, :, :], fgroup(j))
                dve.drain()
                for i in range(3):
                    ffn_conv(j, i)
                ffn_take(M, 0)
                ffn_conv(j, 3, split=True)
                ffn_take(M, 1)
                ffn_conv_end(3)
                ffn_take(M, 2)
                ffn_take(M, 3)
                ffn_prod(j, 0)
                ffn_take(M, 4)
                ffn_prod(j, 1)
                ffn_take(M, 5)
                ffn_low(j, par, 0)
                ffn_take(M, 6)
                ffn_take(M, 7)
                ffn_low(j, par, 1)

            dve.wait_ge(fc_in, 16)
            V.memset(ub[:, :, 0:2], 0.0)
            V.tensor_copy(fcd[:, :, :], fgroup(0))
            dve.drain()
            for i in range(4):
                ffn_conv(0, i)
            for t in range(2):
                ffn_prod(0, t)
            for t in range(2):
                ffn_low(0, 0, t)
            with dve.Fori(0, (FG - 1) // 2) as i:
                ffn_iter(i * 2 + 1, 1, i * 24 + (M_FFN + 8))
                ffn_iter(i * 2 + 2, 0, i * 24 + (M_FFN + 20))
            dve.drain().then_inc(cs_out, 1)
            for m in range(KT):
                ffn_take(M_FFN + 12 * FG - 8, m)
                dve.drain().then_inc(r_rdy, 1)
                if m >= 2:
                    ln_add_square(1, m - 1)
            dve.wait_ge(s1_add, KT - 2)
            ln_add(KT - 1)
            dve.drain()
            ln_add_square(1, KT - 1)
            ln_scales(1)
            for n in range(NT):
                cols = slice(n * NW, (n + 1) * NW)
                dve.wait_ge(ln_r, NT + n + 1)
                V.tensor_copy(lsum[:, 0, cols], px[:, n, 0:NW]).then_inc(ln_bc, 1)
                dve.drain()
                k1 = LN2_CUTS[2]
                V.tensor_tensor(XC[:, 0:k1, cols], XC[:, 0:k1, cols], lsum[:, 0:1, cols].to_broadcast([P, k1, NW]), ALU.mult)
                dve.drain()
                dve.wait_ge(ln_bn, n + 1)
                for a, b in zip(LN2_CUTS[0:2], LN2_CUTS[1:3]):
                    V.tensor_tensor(XC[:, a:b, cols], XC[:, a:b, cols], lsum[:, 1:2, cols].to_broadcast([P, b - a, NW]), ALU.add)\
                     .then_inc(ln_t, 1)


IN_SHAPES = {
    "w_panels": (N_PANEL, P, D), "w_ada": (16, P, D), "w_adaT": (32, P, D), "c_bc": (P, 2, D),
    "x": (P, KT, T), "small": (P, N_SMALL), "ident": (P, P), "ones": (P, P),
    "alibi": (P, 8, BAND), "k_cache": (P, 2, WIN), "v_cache": (P, WIN), "rmask": (HB, T), "sel": (HB, HB, P), "cmask": (P, P),
    "c_state": (P, HB, DV + 1), "ffn_consts": (P, FG, 4, 8),
}
OUT_SHAPES = {
    "y": (P, KT, T), "k_out": (2, 2, 64, WIN), "v_out": (2, 2, 64, WIN), "c_out": (2, P, HB, DV + 1), "m_out": (2, HB, 1),
    "cs_out": (P, FG, 4, 4),
}


def tiles(w):
    n = w.shape[1] // P
    return w.reshape(KT, P, n, P).transpose(2, 1, 0, 3).reshape(n, P, D)


def kernel(**inputs):
    import concourse.bacc as bacc
    from concourse.bass_utils import run_bass_kernel_spmd

    a = {k: np.asarray(v) for k, v in inputs.items()}
    f = np.float32
    w_in = a["w_in"][0]
    cut = np.cumsum([1024, 128, 128, 512, 512, 1024, 4, 4, 1024, 1024])
    qa, ka, va, qb, kb, vb, ig, fg, og, ga, gb = np.split(w_in, cut, axis=1)
    kdup = np.concatenate([ka[:, 0:64], ka[:, 0:64], ka[:, 64:128], ka[:, 64:128]], axis=1)
    gates = np.concatenate([ig, fg, np.zeros((D, P - 8), f)], axis=1)
    up = tiles(a["w_up"][0])
    dn = a["w_down"][0].reshape(FG, 2, P, 2, 4, P).transpose(0, 3, 2, 4, 1, 5).reshape(FG, 2, P, D)

    def up4(j):
        return [up[2 * j], up[2 * j + 1], up[UT // 2 + 2 * j], up[UT // 2 + 2 * j + 1]]

    panels = [tiles(np.concatenate([qa, kdup, va, gates, kb, qb, vb, og, gb, ga], axis=1)),
              tiles(a["w_proj_a"][0]), tiles(a["w_proj_b"][0]), tiles(a["w_out"][0])]
    ffn = up4(0)
    for j in range(1, FG):
        ffn += up4(j) + [dn[j - 1, 0], dn[j - 1, 1]]
    ffn += [dn[FG - 1, 0], dn[FG - 1, 1]]
    w_panels = np.concatenate(panels + [np.stack(ffn)], axis=0)

    def cols(v):
        return v.reshape(-1, P).T

    x = np.concatenate([a["x_prompt"][0], a["x_sample"][0]], axis=0)
    small = np.zeros((P, N_SMALL), f)
    small[:, C_BADA:C_BADA + 48] = cols(a["b_ada"][0])
    for c, nme in ((C_L1W, "ln1_w"), (C_L1B, "ln1_b"), (C_L2W, "ln2_w"), (C_L2B, "ln2_b"), (C_NW, "mlstm_norm_w")):
        small[:, c:c + 8] = cols(a[nme][0])
    small[:, C_C:C_C + 16:2] = cols(a["c_prompt"][0])
    small[:, C_C + 1:C_C + 16:2] = cols(a["c_sample"][0])
    small[:, C_SINK:C_SINK + 8] = np.repeat(a["attn_sinks"][0].reshape(8, 2).T, 64, axis=0)
    small[0:HB, C_BI] = a["b_igate"][0]
    small[0:HB, C_BF] = a["b_fgate"][0]
    small[0:HB, C_M0] = a["state_mlstm_m"][0, 0]
    kc = a["cache_attn_k"][0, 0].transpose(1, 2, 0)
    vc = a["cache_attn_v"][0, 0].transpose(1, 2, 0)
    k_cache = np.concatenate([kc, kc], axis=1).transpose(1, 0, 2)
    c_state = np.concatenate([a["state_mlstm_C"][0, 0], a["state_mlstm_n"][0, 0][:, None, :]], axis=1).transpose(2, 0, 1)
    fcn = np.zeros((UT, P, 8), f)
    fcn[:, :, 0] = a["b_up"][0].reshape(UT, P)
    for j in range(3):
        fcn[:, :, 1 + j] = a["conv_w"][0, j].reshape(UT, P)
    fcn[:, :, 4] = a["conv_b"][0].reshape(UT, P)
    for j in range(2):
        fcn[:, :, 5 + j] = a["state_ffn_conv"][0, 0, j].reshape(UT, P)
    ffn_consts = fcn.reshape(2, FG, 2, P, 8).transpose(3, 1, 0, 2, 4).reshape(P, FG, 4, 8)

    slopes = (f(2.0) ** (f(-8.0) * np.arange(1, 17, dtype=f) / f(16))).astype(f)
    dist = np.abs(WIN + np.arange(CH)[:, None] - np.arange(BAND)[None, :]).astype(f)
    alibi = (-slopes.reshape(8, 2).transpose(1, 0)[:, None, :, None] * dist[None, :, None, :]).reshape(P, 8, BAND)
    rmask = np.ones((HB, T), f)
    rmask[:, 0:T:LC] = 0.0
    sel = np.zeros((HB, HB, P), f)
    for h in range(HB):
        sel[h, h, :] = 1.0
    cmask = np.where(np.arange(P)[:, None] <= np.arange(P)[None, :], f(0), f(-1e30)).astype(f)

    arrays = {
        "w_panels": w_panels, "w_ada": tiles(a["w_ada"][0][:, 0:2048]), "w_adaT": a["w_ada"][0][:, 2048:].T,
        "c_bc": np.broadcast_to(np.stack([a["c_prompt"][0], a["c_sample"][0]]), (P, 2, D)),
        "x": x.T.reshape(KT, P, T).transpose(1, 0, 2), "small": small,
        "ident": np.eye(P, dtype=f), "ones": np.full((P, P), 1.0 / D, f), "alibi": alibi, "k_cache": k_cache,
        "v_cache": vc.reshape(P, WIN), "rmask": rmask, "sel": sel, "cmask": cmask, "c_state": c_state, "ffn_consts": ffn_consts,
    }
    nc = bacc.Bacc("TRN2", target_bir_lowering=False, num_devices=1)
    io, feed = {}, {}
    for name, shape in IN_SHAPES.items():
        feed[f"in_{name}"] = np.ascontiguousarray(arrays[name].reshape(shape), dtype=f)
        io[name] = nc.dram_tensor(f"in_{name}", shape, F32, kind="ExternalInput").ap()
    for name, shape in OUT_SHAPES.items():
        io[name] = nc.dram_tensor(f"out_{name}", shape, F32, kind="ExternalOutput").ap()
    io["zs"] = nc.dram_tensor("z_spill", (N_SPILL, P, T), F32, kind="Internal").ap()
    io["hs"] = nc.dram_tensor("h_spill", (KT, P, T), F32, kind="Internal").ap()
    build(nc, io)
    r = run_bass_kernel_spmd(nc, [feed], core_ids=[0]).results[0]
    o = {name: np.asarray(r[f"out_{name}"]) for name in OUT_SHAPES}
    y = o["y"].transpose(1, 0, 2).reshape(D, T).T
    ko = o["k_out"].transpose(1, 3, 0, 2)
    vo = o["v_out"].transpose(1, 3, 0, 2)
    co = o["c_out"].transpose(0, 2, 3, 1)
    cso = o["cs_out"].reshape(P, FG, 2, 2, 4).transpose(4, 2, 1, 3, 0).reshape(4, UT * P)
    outs = []
    for s in range(2):
        outs.append((ko[s][None, None], vo[s][None, None], co[s, :, 0:DV][None, None], co[s, :, DV][None, None],
                     o["m_out"][s, :, 0][None, None], cso[2 * s:2 * s + 2][None, None]))
    c = np.ascontiguousarray
    return (c(y[0:TP][None]), c(y[TP:][None])) + tuple(c(t) for t in outs[0]) + tuple(c(t) for t in outs[1])
```
